# Optimizing a Trainium2 kernel written in Bass

```python
import math
import jax, jax.numpy as jnp
from jax import lax
import numpy as np

D_MODEL = 1024
BATCH = 1
SEQ = 512
DEPTH = 1

HEAD_DIM = 64
H_A = 8
H_B = 8
G_B = 2
R_B = H_B // G_B
H_TOT = H_A + H_B
D_A = H_A * HEAD_DIM
D_B = H_B * HEAD_DIM
D_MIX = D_A + D_B
D_KV_B = G_B * HEAD_DIM
DILATED = ((128, 1), (512, 4), (2048, 16))
CMP_LEN = 32
CMP_STRIDE = 16
CMP_HIDDEN = 256
SLC_BLOCK = 64
SLC_TOPK = 16
SLC_LOCAL = 2
WIN = 512
N_BUCKETS = 32
MAX_DIST = 2048
BLOCK_Q = 128
LN_EPS = 1e-5
NEG = -1e30
ALPHA = (2 * DEPTH) ** 0.25
BETA = (8 * DEPTH) ** -0.25
IN_SIZES = (D_A, D_A, D_A, D_A, D_B, 6 * D_KV_B, 3 * H_B, D_B)
IN_OFFSETS = tuple(int(v) for v in np.cumsum(IN_SIZES)[:-1])
D_IN = sum(IN_SIZES)

kernel_name = 'hymba_dilated_nsa_deepnorm_adaln'

def t5_bucket(dist):
    max_exact = N_BUCKETS // 2
    d = jnp.maximum(dist, 0)
    large = max_exact + (jnp.log(jnp.maximum(d, 1).astype(jnp.float32) / max_exact)
                         / math.log(MAX_DIST / max_exact) * (N_BUCKETS - max_exact)).astype(jnp.int32)
    return jnp.where(d < max_exact, d, jnp.minimum(large, N_BUCKETS - 1))

def layer_norm(x, g, b):
    xf = x.astype(jnp.float32)
    mu = xf.mean(-1, keepdims=True)
    var = jnp.square(xf - mu).mean(-1, keepdims=True)
    return ((xf - mu) * lax.rsqrt(var + LN_EPS)).astype(x.dtype) * g + b

def banded_attention(q, k, v, bias_tbl, window, dist_scale):
    B, G, R, L, hd = q.shape
    n_prev = -(-window // BLOCK_Q)
    L_pad = -(-L // BLOCK_Q) * BLOCK_Q
    nb = L_pad // BLOCK_Q
    pad_end = L_pad - L
    q = jnp.pad(q, ((0, 0), (0, 0), (0, 0), (0, pad_end), (0, 0)))
    kp = jnp.pad(k, ((0, 0), (0, 0), (n_prev * BLOCK_Q, pad_end), (0, 0)))
    vp = jnp.pad(v, ((0, 0), (0, 0), (n_prev * BLOCK_Q, pad_end), (0, 0)))

    def band(t):
        parts = [t[:, :, o * BLOCK_Q:o * BLOCK_Q + L_pad].reshape(B, G, nb, BLOCK_Q, hd)
                 for o in range(n_prev + 1)]
        return jnp.concatenate(parts, axis=3)

    kb, vb = band(kp), band(vp)
    qb = q.reshape(B, G, R, nb, BLOCK_Q, hd)
    logits = jnp.einsum('bgrnqd,bgnkd->bgrnqk', qb, kb).astype(jnp.float32)
    kj = jnp.arange((n_prev + 1) * BLOCK_Q)[None, :]
    dist = jnp.arange(BLOCK_Q)[:, None] + n_prev * BLOCK_Q - kj
    key_pos = jnp.arange(nb)[:, None, None] * BLOCK_Q - n_prev * BLOCK_Q + kj[None]
    mask = (dist >= 0) & (dist <= window) & (key_pos >= 0)
    bias = bias_tbl[:, :, t5_bucket(dist * dist_scale)]
    logits = jnp.where(mask, logits + bias[:, :, None], NEG)
    lse = jax.nn.logsumexp(logits, axis=-1)
    p = jnp.exp(logits - lse[..., None]).astype(v.dtype)
    out = jnp.einsum('bgrnqk,bgnkd->bgrnqd', p, vb).reshape(B, G, R, L_pad, hd)[:, :, :, :L]
    return out, lse.reshape(B, G, R, L_pad)[..., :L]

def dilated_attention(q, k, v, bias_tbl):
    B, H, S, hd = q.shape
    outs, lses = [], []
    for window, dil in DILATED:
        def split(t):
            return t.reshape(B, H, S // dil, dil, hd).transpose(0, 1, 3, 2, 4).reshape(B, H * dil, S // dil, hd)
        tbl = jnp.repeat(bias_tbl, dil, axis=0)[:, None]
        o, lse = banded_attention(split(q)[:, :, None], split(k), split(v), tbl, window // dil, dil)
        outs.append(o[:, :, 0].reshape(B, H, dil, S // dil, hd).transpose(0, 1, 3, 2, 4).reshape(B, H, S, hd))
        lses.append(lse[:, :, 0].reshape(B, H, dil, S // dil).transpose(0, 1, 3, 2).reshape(B, H, S))
    w = jax.nn.softmax(jnp.stack(lses), axis=0)
    return jnp.einsum('ibhs,ibhsd->bhsd', w.astype(q.dtype), jnp.stack(outs))

def compress(t, pe, w1, w2):
    B, G, S, hd = t.shape
    n_sub = CMP_LEN // CMP_STRIDE
    chunks = t.reshape(B, G, S // CMP_STRIDE, CMP_STRIDE, hd)
    n_cmp = S // CMP_STRIDE - n_sub + 1
    blocks = jnp.concatenate([chunks[:, :, o:o + n_cmp] for o in range(n_sub)], axis=3)
    blocks = (blocks + pe).reshape(B, G, n_cmp, CMP_LEN * hd)
    return jax.nn.silu(blocks @ w1) @ w2

def nsa_attention(q, kc, vc, k_s, v_s, k_w, v_w, gates, bias_tbl):
    B, G, R, S, hd = q.shape
    n_cmp = kc.shape[2]
    pos = jnp.arange(S)
    blk_end = jnp.arange(n_cmp) * CMP_STRIDE + CMP_LEN - 1
    dist_c = pos[:, None] - blk_end[None]
    mask_c = dist_c >= 0
    logits = jnp.einsum('bgrsd,bgnd->bgrsn', q, kc).astype(jnp.float32) + bias_tbl[:, :, t5_bucket(dist_c)]
    logits = jnp.where(mask_c, logits, NEG)
    p_c = jax.nn.softmax(logits, axis=-1) * mask_c.any(-1)[:, None]
    o_cmp = jnp.einsum('bgrsn,bgnd->bgrsd', p_c.astype(vc.dtype), vc)
    n_slc = S // SLC_BLOCK
    cmp_start = jnp.arange(n_cmp) * CMP_STRIDE
    slc_start = jnp.arange(n_slc) * SLC_BLOCK
    overlap = ((cmp_start[:, None] < slc_start[None] + SLC_BLOCK)
               & (cmp_start[:, None] + CMP_LEN > slc_start[None])).astype(jnp.float32)
    score = jnp.einsum('bgrsn,nm->bgsm', p_c, overlap)
    cur = (pos // SLC_BLOCK)[:, None]
    blk = jnp.arange(n_slc)[None]
    forced = (blk == 0) | ((cur - blk >= 0) & (cur - blk < SLC_LOCAL))
    score = jnp.where(forced, 1e9, jnp.where(blk > cur, -1e9, score))
    k_sel = min(SLC_TOPK, n_slc)
    _, idx = lax.top_k(score, k_sel)
    ks_blocks = k_s.reshape(B, G, n_slc, SLC_BLOCK, hd)
    vs_blocks = v_s.reshape(B, G, n_slc, SLC_BLOCK, hd)
    nq = S // BLOCK_Q
    q_blk = q.reshape(B, G, R, nq, BLOCK_Q, hd).transpose(3, 0, 1, 2, 4, 5)
    idx_blk = idx.reshape(B, G, nq, BLOCK_Q, k_sel).transpose(2, 0, 1, 3, 4)
    gather = jax.vmap(jax.vmap(lambda blocks, ind: blocks[ind]))
    g_idx = jnp.arange(G)[:, None, None, None]
    r_idx = jnp.arange(R)[:, None, None]

    def one_block(args):
        qb, ib, n = args
        kg = gather(ks_blocks, ib).reshape(B, G, BLOCK_Q, k_sel * SLC_BLOCK, hd)
        vg = gather(vs_blocks, ib).reshape(B, G, BLOCK_Q, k_sel * SLC_BLOCK, hd)
        k_pos = (ib[..., None] * SLC_BLOCK + jnp.arange(SLC_BLOCK)).reshape(B, G, BLOCK_Q, k_sel * SLC_BLOCK)
        dist = (n * BLOCK_Q + jnp.arange(BLOCK_Q))[:, None] - k_pos
        bias = bias_tbl[g_idx, r_idx, t5_bucket(dist)[:, :, None]]
        lg = jnp.einsum('bgrqd,bgqkd->bgrqk', qb, kg).astype(jnp.float32)
        lg = jnp.where((dist >= 0)[:, :, None], lg + bias, NEG)
        p = jax.nn.softmax(lg, axis=-1).astype(vg.dtype)
        return jnp.einsum('bgrqk,bgqkd->bgrqd', p, vg)

    o_slc = lax.map(one_block, (q_blk, idx_blk, jnp.arange(nq)))
    o_slc = o_slc.transpose(1, 2, 3, 0, 4, 5).reshape(B, G, R, S, hd)
    o_win, _ = banded_attention(q, k_w, v_w, bias_tbl, WIN - 1, 1)
    gt = gates.reshape(B, S, 3, G, R).transpose(2, 0, 3, 4, 1)[..., None].astype(q.dtype)
    return gt[0] * o_cmp + gt[1] * o_slc + gt[2] * o_win

def hybrid_layer(x, c, w_in, w_out, cmp_pe, cmp_w1, cmp_w2, w_ada, b_ada, ln_g, ln_b, rel_bias):
    B, S, _ = x.shape
    shift, scl, gate = jnp.split(c @ w_ada + b_ada, 3, axis=-1)
    h = x * (1 + scl[:, None]) + shift[:, None]
    qa, ka, va, za, qb, kvb, gb, zb = jnp.split(h @ w_in, IN_OFFSETS, axis=-1)
    heads = lambda t, n: t.reshape(B, S, n, HEAD_DIM).transpose(0, 2, 1, 3)
    qscale = HEAD_DIM ** -0.5
    o_a = dilated_attention(heads(qa, H_A) * qscale, heads(ka, H_A), heads(va, H_A), rel_bias[:, :H_A].T)
    o_a = o_a.transpose(0, 2, 1, 3).reshape(B, S, D_A)
    q_b = (heads(qb, H_B) * qscale).reshape(B, G_B, R_B, S, HEAD_DIM)
    k_c, v_c, k_s, v_s, k_w, v_w = [heads(t, G_B) for t in jnp.split(kvb, 6, axis=-1)]
    kc = compress(k_c, cmp_pe[0], cmp_w1[0], cmp_w2[0])
    vc = compress(v_c, cmp_pe[1], cmp_w1[1], cmp_w2[1])
    tbl_b = rel_bias[:, H_A:].T.reshape(G_B, R_B, N_BUCKETS)
    o_b = nsa_attention(q_b, kc, vc, k_s, v_s, k_w, v_w, jax.nn.sigmoid(gb), tbl_b)
    o_b = o_b.reshape(B, H_B, S, HEAD_DIM).transpose(0, 2, 1, 3).reshape(B, S, D_B)
    y = jnp.concatenate([o_a * jax.nn.silu(za), o_b * jax.nn.silu(zb)], axis=-1) @ w_out
    return layer_norm(ALPHA * x + (1 + gate[:, None]) * y, ln_g, ln_b)

def setup_inputs(seed: int = 0) -> dict:
    key = jax.random.key(seed)
    ks = jax.random.split(key, 12)
    f32 = jnp.float32
    col_scale = jnp.concatenate([
        jnp.ones(2 * D_A, f32), jnp.full((D_A,), BETA, f32), jnp.ones(D_A + D_B, f32),
        jnp.tile(jnp.repeat(jnp.array([1.0, BETA], f32), D_KV_B), 3),
        jnp.ones(3 * H_B + D_B, f32)])
    return {
        'x': jax.random.normal(ks[0], (BATCH, SEQ, D_MODEL), f32),
        'c': jax.random.normal(ks[1], (BATCH, D_MODEL), f32),
        'w_in': jax.random.normal(ks[2], (DEPTH, D_MODEL, D_IN), f32) * D_MODEL ** -0.5 * col_scale,
        'w_out': jax.random.normal(ks[3], (DEPTH, D_MIX, D_MODEL), f32) * D_MIX ** -0.5 * BETA,
        'cmp_pe': 0.02 * jax.random.normal(ks[4], (DEPTH, 2, CMP_LEN, HEAD_DIM), f32),
        'cmp_w1': jax.random.normal(ks[5], (DEPTH, 2, CMP_LEN * HEAD_DIM, CMP_HIDDEN), f32) * (CMP_LEN * HEAD_DIM) ** -0.5,
        'cmp_w2': jax.random.normal(ks[6], (DEPTH, 2, CMP_HIDDEN, HEAD_DIM), f32) * CMP_HIDDEN ** -0.5,
        'w_ada': jax.random.normal(ks[7], (DEPTH, D_MODEL, 3 * D_MODEL), f32) * 0.1 * D_MODEL ** -0.5,
        'b_ada': 0.01 * jax.random.normal(ks[8], (DEPTH, 3 * D_MODEL), f32),
        'ln_g': 1.0 + 0.01 * jax.random.normal(ks[9], (DEPTH, D_MODEL), f32),
        'ln_b': 0.01 * jax.random.normal(ks[10], (DEPTH, D_MODEL), f32),
        'rel_bias': 0.1 * jax.random.normal(ks[11], (N_BUCKETS, H_TOT), f32),
    }

def reference(x, c, w_in, w_out, cmp_pe, cmp_w1, cmp_w2, w_ada, b_ada, ln_g, ln_b, rel_bias):
    for l in range(DEPTH):
        x = hybrid_layer(x, c, w_in[l], w_out[l], cmp_pe[l], cmp_w1[l], cmp_w2[l],
                         w_ada[l], b_ada[l], ln_g[l], ln_b[l], rel_bias)
    return x


_drawn_inputs = setup_inputs


def setup_inputs(seed=0):
    import zlib

    import numpy as np

    out = dict(_drawn_inputs(seed))
    spreads = {}
    factors = {'c': 2.878,
     'cmp_pe': 8.0,
     'cmp_w1': 4.375,
     'cmp_w2': 3.263,
     'w_ada': 2.789,
     'b_ada': 8.0,
     'ln_g': 5.688,
     'ln_b': 5.839,
     'rel_bias': 8.0}
    for name, (base, spread) in spreads.items():
        noise = np.random.default_rng([zlib.crc32(name.encode()), seed]).standard_normal(out[name].shape)
        drawn = base * np.exp(spread * noise) if base else spread * noise
        out[name] = __import__('jax').numpy.asarray(drawn.astype(out[name].dtype))
    for name, factor in factors.items():
        out[name] = (out[name] * factor).astype(out[name].dtype)
    return out
```

```python
from contextlib import ExitStack

import numpy as np

import concourse.bass as bass
from concourse import mybir

F32 = mybir.dt.float32
F32R = mybir.dt.float32r
ACT = mybir.ActivationFunctionType
ALU = mybir.AluOpType
AX = mybir.AxisListType

P = 128
SEQ = 512
D = 1024
NT = SEQ // P
KT = D // P
HD = 64
H_A = H_B = 8
N_B = 32
MAX_DIST = 2048
DILATED = ((128, 1), (512, 4), (2048, 16))
CMP_LEN, CMP_STRIDE, CMP_HID = 32, 16, 256
N_CMP = SEQ // CMP_STRIDE - 1
ALPHA = 2.0 ** 0.25
LN_EPS = 1e-5
BIG = 1e30

QA, KA, VA, ZA, QB, KVB, GB, ZB = 0, 512, 1024, 1536, 2048, 2560, 3328, 3352
W1ST = GB + 24 - KVB
PAIRS = 8
CW = 384
RAWC = 2 * W1ST
NRAW = 3
TROW = 640


def pieces(c):
    if c < 4:
        return (QB + P * c, ZA + P * c, ZB + P * c)
    return (KA + P * (c - 4), QA + P * (c - 4), VA + P * (c - 4))


def units_of(c):
    if c < 4:
        return [("cmp", c, 0, 0, 0)] + [("att", c, h, br, i) for h in range(2) for br in range(2) for i in range(NT)]
    return [("att", c, h, 0, i) for h in range(2) for i in range(NT)]


UNITS = [u for c in range(PAIRS) for u in units_of(c)]
NU = len(UNITS)
UBASE = [sum(len(units_of(b)) for b in range(c)) for c in range(PAIRS + 1)]
GROUP = []
for _n, _u in enumerate(UNITS):
    GROUP.append(0 if _n == 0 else GROUP[-1] + (_u[0] == "cmp" or _u[4] == 0))


def evac_on_act(n):
    return UNITS[n][0] == "cmp" or UNITS[n][4] in (0, 3)


def group_last(m):
    return m + 1 == NU or GROUP[m + 1] != GROUP[m]


def evacs(n, on_act):
    return sum(evac_on_act(m) == on_act for m in range(n + 1))


def iters(s):
    return 6 if s == 0 else len(units_of(s - 1))


def quantum(s, j):
    return 3 * j / iters(s), 3 * (j + 1) / iters(s)


def tile_ends(s, j):
    a, b = quantum(s, j)
    return [e for e in range(3) if a <= e + 1 - 1e-3 < b]


def raw_order():
    r = [("p1", g, 0) for g in range(4)] + [("ch", 0, 0), ("ch", 0, 1)]
    r += [("w1", 0, 0), ("w1", 0, 1), ("ch", 1, 0), ("w1", 0, 2), ("w1", 1, 0), ("ch", 1, 1), ("w1", 1, 1), ("w1", 1, 2)]
    for s in range(1, 7):
        g = [("gate", 2 * (s - 4), 0)] if s >= 4 else []
        g2 = [("gate", 2 * (s - 4) + 1, 0)] if s >= 4 else []
        r += [("ch", s + 1, 0)] + g + [("ch", s + 1, 1)] + g2
    r += [("wo", 0, 0), ("gate", 6, 0), ("wo", 1, 0), ("gate", 7, 0), ("wo", 2, 0)]
    return r + [("wo", k, 0) for k in range(3, 8)]


RAW = raw_order()
RAWI = {u: n for n, u in enumerate(RAW)}
RAWD = {"p1": 1, "ch": 3, "w1": 1, "gate": 1, "wo": 1}
W1PARTS = ((0, 6), (6, 12), (12, 16))


def raw_count(n):
    return sum(16 * RAWD[RAW[m][0]] for m in range(n % NRAW, n + 1, NRAW))


def split_no(u):
    return {"p1": u[1], "ch": 4 + 2 * u[1] + u[2], "wo": 20 + u[1]}[u[0]]


def at_iter(s, j):
    n = iters(s)
    if s == 0:
        return {1: [("ch", 1, 0)], 4: [("ch", 1, 1)]}.get(j, [])
    if s <= 6:
        plan = [(n // 4, ("ch", s + 1, 0)), (3 * n // 4, ("ch", s + 1, 1))]
        if s >= 4:
            plan += [(n // 4 + 1, ("gate", 2 * (s - 4), 0)), (3 * n // 4 + 1, ("gate", 2 * (s - 4) + 1, 0))]
    elif s == 7:
        plan = [(1, ("wo", 0, 0)), (2, ("gate", 6, 0)), (3, ("wo", 1, 0)), (4, ("gate", 7, 0)), (6, ("wo", 2, 0))]
    else:
        plan = [(k - 3, ("wo", k, 0)) for k in range(3, 8)]
    return [u for k, u in plan if k == j]


def build(nc, x, c_in, w_in, w_out, cmp_pe, cmp_w1, cmp_w2, w_ada, b_ada, ln_g, ln_b, rel_bias, consts, scratch, out):
    with ExitStack() as ctx:
        def sb(name, cols, dt=F32, parts=P):
            return ctx.enter_context(nc.sbuf_tensor(name, [parts, cols], dt))

        def sem(name):
            return ctx.enter_context(nc.semaphore(name))

        w_hi = sb("w_hi", KT * W1ST, F32R)
        w_lo = sb("w_lo", KT * W1ST, F32R)
        raw = sb("raw", NRAW * RAWC)
        with nc.sbuf_tensor("x_tok", [P, NT * D], F32) as x_tok_t:
            x_tok = x_tok_t[:, :].rearrange("p (t d) -> p t d", t=NT)
        h_hi = sb("h_hi", KT * SEQ, F32R)
        h_lo = sb("h_lo", KT * SEQ, F32R)
        with nc.sbuf_tensor("ada", [P, 2 * 4096], F32) as ada_t:
            ada = ada_t[:, :].rearrange("p (b s k f) -> p b s k f", b=2, s=2, k=KT)
        z = sb("z", NT * D)
        kk = sb("kk", 4096, F32R)
        qs = sb("qs", 2048, F32R)
        vb = sb("vb", NT * 4 * 65)
        va = sb("va", 2 * NT * 2 * 65)
        tb_ = sb("tb", 2048)
        lg = sb("lg", 2048)
        pt = sb("pt", 1024)
        os_ = sb("os", NT * D)
        gacc = sb("gacc", D)
        et = sb("et", 1024)
        tmp = sb("tmp", 512)
        tc = sb("tc", 512)
        w2 = sb("w2", 256)
        hs = sb("hs", 2 * 62)
        hsv = sb("hsv", 2 * 2 * 64)
        he = sb("he", 2 * 62)
        kc = sb("kc", 2 * 2 * 32, F32R)
        vc = sb("vc", 2 * P, parts=64)
        acc = sb("acc", 512)
        ident = sb("ident", P)
        flip = sb("flip", P)
        ones = sb("ones", P)
        small = sb("small", 320)
        cT = small[:, 0:8]
        ba = small[:, 8:24]
        ss = small[:, 24:40]
        peT = small[:, 40:72]
        mn = small[:, 72:80]
        mnc = small[:, 80:88]
        rcc = small[:, 88:96]
        rc = small[:, 96:104]
        gates = small[:, 104:200]
        cmask = small[:, 200:204]
        g0 = small[:, 204:236]
        st = small[:, 236:248]
        mv = small[:, 248:250]
        rstd = small[:, 250:254]
        nmr = small[:, 254:258]
        sdv = small[:, 258:262]
        zero1 = small[:, 262:263]

        hiv = h_hi[:, :].rearrange("p (k t) -> p k t", k=KT)
        lov = h_lo[:, :].rearrange("p (k t) -> p k t", k=KT)
        xT = os_[:, :].rearrange("p (k t) -> p k t", k=KT)
        bt = os_[:, 0:2 * 16 * 62].rearrange("p (v k n) -> p v k n", v=2, k=16)
        OS = os_[:, :].rearrange("p (t d) -> p t d", t=NT)
        Z = z[:, :].rearrange("p (t d) -> p t d", t=NT)
        K = kk[:, :].rearrange("p (s a l t) -> p s a l t", s=2, a=2, l=2)
        QS = qs[:, :].rearrange("p (s h t) -> p s h t", s=2, h=2)
        VB = vb[:, :].rearrange("p (t b g d) -> p t b g d", t=NT, b=2, g=2)
        VAv = va[:, :].rearrange("p (s t h d) -> p s t h d", s=2, t=NT, h=2)
        T = tb_[:, :].rearrange("p (s h x) -> p s h x", s=2, h=2)
        Tc = tc[:, :].rearrange("p (s i h n) -> p s i h n", s=2, i=NT, h=2)
        KC = kc[:, :].rearrange("p (l g n) -> p l g n", l=2, g=2)
        W2 = w2[:, :].rearrange("p (v j d) -> p v j d", v=2, j=2)
        HS = hs[:, :].rearrange("p (j n) -> p j n", j=2)
        HSV = hsv[:, :].rearrange("p (j g r n) -> p j g r n", j=2, g=2, r=2)
        HE = he[:, :].rearrange("p (j n) -> p j n", j=2)
        G = gates.rearrange("p (t b h) -> p t b h", t=NT, b=3)
        G0 = g0.rearrange("p (t h) -> p t h", t=NT)
        onehot, rel = lg[0:34, 0:TROW], lg[0:34, TROW:TROW + 16]
        trow = lg[0:16, 704:704 + TROW]
        ba_row, pe_row = lg[0:16, 1344:1472], lg[0:32, 1472:1600]
        OTh = kk[:, 0:2048].rearrange("p (r k t) -> p r k t", r=2, k=KT)
        OTl = kk[:, 2048:4096].rearrange("p (r k t) -> p r k t", r=2, k=KT)
        xr = tb_[:, :].rearrange("p (r d) -> p r d", r=2)
        yt = lg[:, :].rearrange("p (r d) -> p r d", r=2)
        lng, lnb, bgate = raw[:, 0:D], raw[:, D:2 * D], raw[:, 2 * D:3 * D]

        def slot(n):
            return raw[:, (n % NRAW) * RAWC:(n % NRAW + 1) * RAWC]

        def split_at(w, u):
            kind, a, b = u
            if kind == "p1":
                return w[:, 2 * a * W1ST:2 * (a + 1) * W1ST]
            if kind == "ch":
                o = (a % 2) * KT * CW + b * 4 * CW
                return w[:, o:o + 4 * CW]
            return wo_at(w, a)

        def wo_at(w, k):
            if k < 6:
                return w[:, k * D:(k + 1) * D]
            hx = h_hi if w is w_hi else h_lo
            return hx[:, (k - 6) * D:(k - 5) * D]

        def width(u):
            return {"p1": RAWC, "ch": 4 * CW, "wo": D}[u[0]]

        def chunk(w, c, k, a, b):
            o = (c % 2) * KT * CW + k * CW
            return w[:, o + a:o + b]

        ps = ctx.enter_context(nc.psum_tensor("ps", [P, 4096], F32))

        def bank(b, a=0, n=512):
            return ps[:, 512 * b + a:512 * b + a + n]

        S_BANK, T_BANK, O_BANK = 2, 4, 6

        small_in = sem("small_in")
        w2_in = sem("w2_in")
        x_in = sem("x_in")
        ada_in = [sem(f"ada_in{b}") for b in range(2)]
        raw_in = [sem(f"raw_in{b}") for b in range(NRAW)]
        trow_out = sem("trow_out")
        t_in = [sem(f"t_in{b}") for b in range(2)]
        kdup = [sem(f"kdup{b}") for b in range(2)]
        consts_set = sem("consts_set")
        flip_set = sem("flip_set")
        pre_tr = sem("pre_tr")
        pre_ev = sem("pre_ev")
        trow_ev = sem("trow_ev")
        x_tr = sem("x_tr")
        xt_act = sem("xt_act")
        xt_dve = sem("xt_dve")
        ada_acc = sem("ada_acc")
        ada_red = sem("ada_red")
        ss_set = sem("ss_set")
        hhi_set = sem("hhi_set")
        hlo_set = sem("hlo_set")
        hi_set = sem("hi_set")
        lo_set = sem("lo_set")
        p1_used = sem("p1_used")
        tok_ev = sem("tok_ev")
        gb_exp = sem("gb_exp")
        g_set = sem("g_set")
        kb_hi = sem("kb_hi")
        kb_lo = sem("kb_lo")
        bt_set = sem("bt_set")
        w1_used = sem("w1_used")
        he_set = sem("he_set")
        hs_set = sem("hs_set")
        cmp2 = sem("cmp2")
        kc_hi = sem("kc_hi")
        cmp_set = sem("cmp_set")
        pj = sem("pj")
        pj_act = sem("pj_act")
        pj_dve = sem("pj_dve")
        qk_done = sem("qk_done")
        lg_set = sem("lg_set")
        ex_set = sem("ex_set")
        cn_set = sem("cn_set")
        tr_done = sem("tr_done")
        ev_act = sem("ev_act")
        ev_dve = sem("ev_dve")
        pv_done = sem("pv_done")
        og_set = sem("og_set")
        add_done = sem("add_done")
        gated = sem("gated")
        tc_set = sem("tc_set")
        gate_used = sem("gate_used")
        grow = sem("grow")
        g1_set = sem("g1_set")
        res_in = [sem(f"res_in{b}") for b in range(2)]
        ln_in = sem("ln_in")
        ot_tr = sem("ot_tr")
        ot_hi = sem("ot_hi")
        ot_lo = sem("ot_lo")
        y_done = sem("y_done")
        y_read = sem("y_read")
        var_set = sem("var_set")
        sd_set = sem("sd_set")
        nm_set = sem("nm_set")
        norm_set = sem("norm_set")
        aff_set = sem("aff_set")
        out_done = [sem(f"out_done{b}") for b in range(2)]
        dve_step = sem("dve_step")
        act_step = sem("act_step")
        pool_step = sem("pool_step")

        def raw_free(eng, n):
            kind, a, b = RAW[n]
            if kind in ("p1", "ch", "wo"):
                eng.wait_ge(hi_set, split_no(RAW[n]) + 1)
                eng.wait_ge(lo_set, split_no(RAW[n]) + 1)
            elif kind == "w1":
                eng.wait_ge(w1_used, 3 * a + b + 1)
            else:
                eng.wait_ge(gate_used, a + 1)

        def raw_landed(eng, u):
            n = RAWI[u]
            eng.wait_ge(raw_in[n % NRAW], raw_count(n))
            return slot(n)

        def evacuated(eng, n):
            on_act = evac_on_act(n)
            eng.wait_ge(ev_act if on_act else ev_dve, evacs(n, on_act))

        def act_tiles(t):
            return sum(not (m >= 12 and m % 3 == 2) for m in range(t + 1))

        def store(sp, t):
            sp.wait_ge(aff_set, t + 1)
            sp.dma_start(out[0, t * P:(t + 1) * P, :], yt[:, t % 2, :]).then_inc(out_done[t % 2], 16)

        block = ctx.enter_context(nc.Block())

        @block.sync
        def _(sp):
            sp.dma_start(onehot, consts[:, 0:TROW]).then_inc(small_in, 16)
            sp.dma_start(rel[N_B:N_B + 2, :], consts[N_B:N_B + 2, TROW:TROW + 16]).then_inc(small_in, 16)
            sp.dma_start(rel[0:N_B, :], rel_bias).then_inc(small_in, 16)
            sp.dma_start(cT, c_in.rearrange("o (p k) -> (o p) k", k=KT)).then_inc(small_in, 16)
            sp.dma_start(ba_row, b_ada[:, 0:2 * D].rearrange("o (j q) -> (o j) q", q=P)).then_inc(small_in, 16)
            sp.dma_start(pe_row, cmp_pe.rearrange("v (k r) d -> (v k) (r d)", r=2)).then_inc(small_in, 16)

            def load_ada(g):
                if g >= 2:
                    sp.wait_ge(ada_acc, g - 1)
                for s in range(2):
                    src = w_ada[:, s * D + 256 * g:s * D + 256 * (g + 1)].rearrange("(p k) f -> p k f", k=KT)
                    sp.dma_start(ada[:, g % 2, s, :, :], src).then_inc(ada_in[g % 2], 16)

            def load_raw(n):
                if n >= NRAW:
                    raw_free(sp, n - NRAW)
                kind, a, b = RAW[n]
                d, s = slot(n), raw_in[n % NRAW]
                if kind == "p1":
                    sp.dma_start(d.rearrange("p (k f) -> p k f", k=2),
                                 w_in[2 * a * P:2 * (a + 1) * P, KVB:KVB + W1ST]
                                 .rearrange("(k p) f -> p k f", p=P)).then_inc(s, 16)
                elif kind == "ch":
                    dv = d[:, 0:4 * CW].rearrange("p (k f) -> p k f", k=4)
                    for m, col in enumerate(pieces(a)):
                        sp.dma_start(dv[:, :, m * P:(m + 1) * P],
                                     w_in[4 * b * P:4 * (b + 1) * P, col:col + P]
                                     .rearrange("(k p) f -> p k f", p=P)).then_inc(s, 16)
                elif kind == "w1":
                    k0, k1 = W1PARTS[b]
                    sp.dma_start(d[:, 0:(k1 - k0) * CMP_HID].rearrange("p (k f) -> p k f", f=CMP_HID),
                                 cmp_w1[a, k0 * P:k1 * P, :].rearrange("(k p) f -> p k f", p=P)).then_inc(s, 16)
                elif kind == "gate":
                    sp.dma_start(d[:, 0:D], w_ada[:, 2 * D:3 * D].rearrange("(p k) f -> p k f", k=KT)[:, a, :])\
                        .then_inc(s, 16)
                else:
                    sp.dma_start(d[:, 0:D], w_out[a * P:(a + 1) * P, :]).then_inc(s, 16)

            def load_tables(c):
                if c >= 2:
                    sp.wait_ge(lg_set, UBASE[c - 1])
                h0 = H_A + 2 * c if c < 4 else 2 * (c - 4)
                src = bass.AP(scratch.tensor, h0 * TROW, [[1, P], [TROW, 2], [1, SEQ]])
                sp.dma_start(T[:, c % 2, :, :], src).then_inc(t_in[c % 2], 16)

            load_ada(0)
            sp.dma_start(x_tok, x[0].rearrange("(t p) d -> p t d", p=P)).then_inc(x_in, 16)
            load_raw(0)
            load_ada(1)
            load_raw(1)
            load_ada(2)
            load_raw(2)
            load_ada(3)
            load_raw(3)
            sp.dma_start(W2, cmp_w2.rearrange("v (j p) d -> p v j d", p=P)).then_inc(w2_in, 16)
            sp.wait_ge(trow_ev, 1)
            sp.dma_start(scratch, trow).then_inc(trow_out, 16)
            sp.wait_ge(trow_out, 16)
            load_tables(0)
            load_tables(1)
            n = 4
            for s in range(PAIRS + 1):
                if 2 <= s < PAIRS:
                    load_tables(s)
                last = RAWI[{0: ("w1", 1, 2), 7: ("wo", 2, 0), 8: ("wo", 7, 0)}.get(s, ("ch", s + 1, 1))]
                if 4 <= s <= 6:
                    last += 1
                while n <= last:
                    load_raw(n)
                    n += 1
            for m in range(len(RAW) - NRAW, len(RAW)):
                raw_free(sp, m)
            sp.dma_start(bgate, b_ada[0, 2 * D:3 * D].partition_broadcast(P)).then_inc(ln_in, 16)
            sp.dma_start(lng, ln_g[0].partition_broadcast(P)).then_inc(ln_in, 16)
            sp.dma_start(lnb, ln_b[0].partition_broadcast(P)).then_inc(ln_in, 16)
            sp.wait_ge(lg_set, NU)
            for t in range(NT):
                if t >= 2:
                    sp.wait_ge(norm_set, t - 1)
                sp.dma_start(xr[:, t % 2, :], x[0, t * P:(t + 1) * P, :]).then_inc(res_in[t % 2], 16)
                if t >= 2:
                    store(sp, t - 2)
            for t in range(NT - 2, NT):
                store(sp, t)
            for b in range(2):
                sp.wait_ge(out_done[b], 32)

        @block.gpsimd
        def _(pool):
            nc.gpsimd.memset(ident[:, :], 0.0).then_inc(pool_step, 1)
            nc.gpsimd.memset(flip[:, :], 0.0).then_inc(pool_step, 1)
            nc.gpsimd.memset(cmask, 1.0).then_inc(pool_step, 1)
            nc.gpsimd.memset(ones[:, :], 1.0).then_inc(pool_step, 1)
            pool.wait_ge(pool_step, 4)
            nc.gpsimd.affine_select(out=ident[:, :], in_=ident[:, :], compare_op=ALU.not_equal, fill=1.0, base=0,
                                    pattern=[[-1, P]], channel_multiplier=1).then_inc(consts_set, 1)
            nc.gpsimd.affine_select(out=flip[:, :], in_=flip[:, :], compare_op=ALU.not_equal, fill=1.0,
                                    base=-(P - 1), pattern=[[1, P]], channel_multiplier=1).then_inc(flip_set, 1)
            nc.gpsimd.affine_select(out=cmask[:, 0:1], in_=cmask[:, 0:1], compare_op=ALU.is_ge, fill=0.0,
                                    base=-(CMP_LEN - 1), pattern=[[0, 1]], channel_multiplier=1)\
                .then_inc(consts_set, 1)
            nc.gpsimd.memset(tc[:, :], BIG).then_inc(consts_set, 1)
            nc.gpsimd.memset(hsv[:, :], 0.0).then_inc(consts_set, 1)
            nc.gpsimd.memset(kc[:, :].bitcast(F32), 0.0).then_inc(consts_set, 1)
            nc.gpsimd.memset(vc[:, :], 0.0).then_inc(consts_set, 1)
            nc.gpsimd.memset(vb[:, :], 1.0).then_inc(consts_set, 1)
            nc.gpsimd.memset(va[:, :], 1.0).then_inc(consts_set, 1)

            def split_lo(u):
                src = raw_landed(pool, u)
                n = width(u)
                pool.wait_ge(hi_set, split_no(u) + 1)
                nc.gpsimd.tensor_tensor(split_at(w_lo, u), src[:, 0:n], split_at(w_hi, u).bitcast(F32),
                                        ALU.subtract).then_inc(lo_set, 1)

            def compressed_bias(c):
                pool.wait_ge(t_in[c % 2], 16 * (c // 2 + 1))
                if c >= 2:
                    pool.wait_ge(lg_set, UBASE[c - 2] + 1)
                for i in range(NT):
                    n = 8 * i + 7
                    o = SEQ - P + CMP_LEN - 1 - P * i
                    ins = nc.gpsimd.tensor_copy(Tc[:, c % 2, i, :, 0:n],
                                                T[:, c % 2, :, o:o + CMP_STRIDE * (n - 1) + 1:CMP_STRIDE])
                ins.then_inc(tc_set, 1)

            def group_adds(n):
                kind, c, h, br, i = UNITS[n]
                if kind == "att" and c < 4:
                    r = GROUP[n]
                    pool.wait_ge(og_set, r + 1)
                    col = D // 2 + P * c + HD * h
                    if adds[0]:
                        pool.wait_ge(add_done, adds[0])
                    nc.gpsimd.tensor_tensor(OS[:, :, col:col + HD], OS[:, :, col:col + HD],
                                            tmp[:, 256 * (adds[0] % 2):256 * (adds[0] % 2) + 256]
                                            .rearrange("p (t d) -> p t d", t=NT), ALU.add).then_inc(add_done, 1)
                    adds[0] += 1
                if n + 1 == UBASE[c + 1]:
                    col = D // 2 + P * c if c < 4 else P * (c - 4)
                    if c < 4:
                        pool.wait_ge(add_done, adds[0])
                    else:
                        pool.wait_ge(og_set, GROUP[n] + 1)
                    pool.wait_ge(pj_dve, 3 * (c % 4) + 3)
                    nc.gpsimd.tensor_tensor(OS[:, :, col:col + P], OS[:, :, col:col + P], Z[:, :, col:col + P],
                                            ALU.mult).then_inc(gated, 1)

            adds = [0]
            for g in range(4):
                split_lo(("p1", g, 0))
            split_lo(("ch", 0, 0))
            split_lo(("ch", 0, 1))
            n = 0
            for s in range(PAIRS + 1):
                for j in range(iters(s)):
                    if s < 4 and j == iters(s) // 2:
                        compressed_bias(s)
                    for u in at_iter(s, j):
                        if u[0] != "gate":
                            split_lo(u)
                    if s >= 1:
                        m = n - 4
                        if m >= 0 and group_last(m):
                            group_adds(m)
                        n += 1
            for m in range(NU - 4, NU):
                if group_last(m):
                    group_adds(m)
            pool.wait_ge(ln_in, 48)
            for t in range(NT):
                pool.wait_ge(norm_set, t + 1)
                nc.gpsimd.tensor_tensor(yt[:, t % 2, :], yt[:, t % 2, :], lng, ALU.mult).then_inc(pool_step, 1)
                pool.wait_ge(pool_step, 5 + t)
                nc.gpsimd.tensor_tensor(yt[:, t % 2, :], yt[:, t % 2, :], lnb, ALU.add).then_inc(aff_set, 1)

        @block.scalar
        def _(act):
            def split_hi(u):
                src = raw_landed(act, u)
                kind, a, b = u
                if kind == "ch" and a == 0:
                    act.wait_ge(p1_used, 4)
                elif kind == "ch" and a == 1:
                    act.wait_ge(p1_used, KT)
                elif kind == "ch":
                    act.wait_ge(pj, 3 * (a - 1))
                elif kind == "wo":
                    act.wait_ge(pj, 21 if a < 3 else 24)
                n = width(u)
                nc.scalar.activation(split_at(w_hi, u), src[:, 0:n], ACT.Copy).then_inc(hi_set, 1)

            def q_or_k_hi(src, tile0, tile1, scale, s, n, backwards):
                for a, dst in ((0, tile0), (1, tile1)):
                    o = src[HD * a:HD * (a + 1), :]
                    if backwards:
                        o, dst = blocks(o)[:, :, ::-1], blocks(dst)
                    ins = nc.scalar.activation(dst, o, ACT.Copy, scale=scale)
                ins.then_inc(s, n)

            def tile_part(t):
                c, e = t // 3, t % 3
                src = bank(t % 2)
                if c < 4 and e > 0:
                    act.wait_ge(pj, t + 1)
                    if c >= 1:
                        act.wait_ge(pj_dve, t - 2)
                    nc.scalar.activation(et[:, 512 * (e - 1):512 * e], src, ACT.Exp, scale=-1.0).then_inc(pj_act, 1)
                elif (c < 4) or e == 1:
                    act.wait_ge(pj, t + 1)
                    if c >= 2:
                        act.wait_ge(qk_done, UBASE[c - 1])
                    q_or_k_hi(src, QS[0:HD, c % 2, 0, :], QS[HD:P, c % 2, 1, :], -HD ** -0.5, pj_act, 1, True)
                elif e == 0:
                    act.wait_ge(pj, t + 1)
                    act.wait_ge(qk_done, UBASE[2] if c == 4 else UBASE[4] if c == 5 else UBASE[c - 1])
                    q_or_k_hi(src, K[0:HD, c % 2, 0, 0, :], K[HD:P, c % 2, 1, 0, :], 1.0, pj_act, 1, False)

            def double_keys(c):
                act.wait_ge(pj_dve, 3 * c + 1)
                act.dma_start(K[HD:P, c % 2, 0, :, :].bitcast(F32), K[0:HD, c % 2, 0, :, :].bitcast(F32))\
                    .then_inc(kdup[c % 2], 16)
                act.dma_start(K[0:HD, c % 2, 1, :, :].bitcast(F32), K[HD:P, c % 2, 1, :, :].bitcast(F32))\
                    .then_inc(kdup[c % 2], 16)

            def probs(n):
                kind, c, h, br, i = UNITS[n]
                act.wait_ge(lg_set, n + 1)
                if kind == "cmp":
                    v = lg[:, 512 * (n % 4):512 * (n % 4) + 256]
                    nc.scalar.activation(v, v, ACT.Exp, scale=-1.0).then_inc(ex_set, 1)
                else:
                    v = lg[:, 512 * (n % 4):512 * (n % 4) + P * (i + 1)]
                    nc.scalar.activation(v, v, ACT.Exp, bias=mn[:, n % 8:n % 8 + 1], scale=-1.0).then_inc(ex_set, 1)

            def evac(n):
                kind, c, h, br, i = UNITS[n]
                act.wait_ge(tr_done, n + 1)
                if n >= 2:
                    act.wait_ge(pv_done, n - 1)
                w = 512 if kind == "cmp" else P * (i + 1)
                m = HD if kind == "cmp" else P
                nc.scalar.activation(pt[0:m, 512 * (n % 2):512 * (n % 2) + w], bank(T_BANK + n % 2)[0:m, 0:w],
                                     ACT.Copy).then_inc(ev_act, 1)

            for k in range(0, KT, 2):
                act.wait_ge(x_tr, k + 1)
                nc.scalar.activation(xT[:, k, :], bank(k % 4), ACT.Copy).then_inc(xt_act, 1)
            for g in range(4):
                split_hi(("p1", g, 0))
                act.wait_ge(ss_set, g + 1)
                for k in (2 * g, 2 * g + 1):
                    act.wait_ge(xt_dve if k % 2 else xt_act, k // 2 + 1)
                    act.wait_ge(x_tr, KT)
                    nc.scalar.activation(hiv[:, k, :], xT[:, k, :], ACT.Identity, bias=ss[:, k:k + 1],
                                         scale=ss[:, 8 + k:9 + k]).then_inc(hhi_set, 1)
            split_hi(("ch", 0, 0))
            split_hi(("ch", 0, 1))
            act.wait_ge(p1_used, KT)
            act.wait_ge(consts_set, 8)
            for b in range(2):
                nc.scalar.activation(VB[:, 2 * b:2 * b + 2, :, :, 0:HD].rearrange("p t b g d -> p t (b g) d"),
                                     bank(b).rearrange("p (t c d) -> p t c d", t=2, c=4), ACT.Copy)\
                    .then_inc(tok_ev, 1)
            for br in range(2):
                q_or_k_hi(bank(4 + br), K[0:HD, 0, br, 0, :], K[HD:P, 1, br, 0, :], 1.0, kb_hi, 1, False)
            nc.scalar.activation(gates, bank(6, 0, 96), ACT.Exp, scale=-1.0).then_inc(gb_exp, 1)
            act.wait_ge(kb_lo, 2)
            act.dma_start(K[HD:P, 0, :, :, :].bitcast(F32), K[0:HD, 0, :, :, :].bitcast(F32)).then_inc(kdup[0], 16)
            act.dma_start(K[0:HD, 1, :, :, :].bitcast(F32), K[HD:P, 1, :, :, :].bitcast(F32)).then_inc(kdup[1], 16)

            def hidden_exp(v):
                act.wait_ge(w1_used, 3 * (v + 1))
                if v:
                    act.wait_ge(hs_set, 1)
                nc.scalar.activation(HE, ps[:, 2048:3072].rearrange("p (j n) -> p j n", j=2)[:, :, 0:62], ACT.Exp,
                                     scale=-1.0).then_inc(he_set, 1)

            n = 0
            pending = []
            for s in range(PAIRS + 1):
                for j in range(iters(s)):
                    if s >= 1:
                        probs(n)
                        if n >= 2 and evac_on_act(n - 2):
                            evac(n - 2)
                        n += 1
                    for t in pending:
                        tile_part(t)
                    if s >= 4 and s < PAIRS and j >= 2 and tile_ends(s, j - 2) == [0]:
                        double_keys(s)
                    pending = [3 * s + e for e in tile_ends(s, j)] if s < PAIRS else []
                    for u in at_iter(s, j):
                        if u[0] != "gate":
                            split_hi(u)
                    if s == 0 and j == 2:
                        hidden_exp(0)
                    if s == 0 and j == 4:
                        act.wait_ge(cmp2, 1)
                        act.wait_ge(consts_set, 8)
                        src = bank(7)[0:HD, 0:62].rearrange("p (g n) -> p g n", g=2)
                        nc.scalar.activation(KC[0:HD, 0, :, 0:N_CMP], src, ACT.Copy)
                        nc.scalar.activation(KC[HD:P, 0, :, 0:N_CMP], src, ACT.Copy).then_inc(kc_hi, 1)
                    if s == 0 and j == 5:
                        hidden_exp(1)
                for t in pending:
                    tile_part(t)
                pending = []
            for m in (NU - 2, NU - 1):
                if evac_on_act(m):
                    evac(m)
            for t in range(NT + 1):
                if t < NT:
                    act.wait_ge(ot_tr, t + 1)
                    if t >= 2:
                        act.wait_ge(y_done, t - 1)
                    nc.scalar.activation(OTh[:, t % 2, :, :].rearrange("p k t -> p (k t)"), ps[:, 2048:3072],
                                         ACT.Copy).then_inc(ot_hi, 1)
                if t >= 1:
                    act.wait_ge(var_set, t)
                    nc.scalar.activation(sdv[:, t - 1:t], mv[:, 1:2], ACT.Sqrt, bias=zero1).then_inc(sd_set, 1)
                    act.wait_ge(nm_set, t)
                    nc.scalar.activation(yt[:, (t - 1) % 2, :], yt[:, (t - 1) % 2, :], ACT.Identity,
                                         bias=nmr[:, t - 1:t], scale=rstd[:, t - 1:t]).then_inc(norm_set, 1)

        @block.vector
        def _(dve):
            steps = [0]

            def link(ins):
                steps[0] += 1
                ins.then_inc(dve_step, 1)
                dve.wait_ge(dve_step, steps[0])

            link(nc.vector.memset(zero1, 0.0))
            dve.wait_ge(pre_tr, 1)
            nc.vector.tensor_copy(trow, ps[0:16, 2048:2048 + TROW]).then_inc(trow_ev, 1)
            dve.wait_ge(pre_tr, 2)
            nc.vector.tensor_copy(ba[:, 0:8], bank(7, 0, 8))
            nc.vector.tensor_scalar(ba[:, 8:16], bank(7, 8, 8), 1.0, None, ALU.add)
            nc.vector.tensor_copy(peT, bank(7, 16, 32)).then_inc(pre_ev, 1)

            def ada_sums(g):
                dve.wait_ge(ada_in[g % 2], 32 * (g // 2 + 1))
                if g == 0:
                    dve.wait_ge(small_in, 96)
                if g >= 1:
                    dve.wait_ge(ada_red, g)
                a = acc[:, :].rearrange("p (s f) -> p s f", s=2)
                for k in range(KT):
                    src = ada[:, g % 2, :, k, :]
                    if k == 0:
                        ins = nc.vector.tensor_scalar(a, src, cT[:, 0:1], None, ALU.mult)
                    else:
                        ins = nc.vector.scalar_tensor_tensor(out=a, in0=src, scalar=cT[:, k:k + 1], in1=a,
                                                             op0=ALU.mult, op1=ALU.add)
                    if k < KT - 1:
                        link(ins)
                    else:
                        ins.then_inc(ada_acc, 1)

            def shift_scale(g):
                dve.wait_ge(ada_red, g + 1)
                dve.wait_ge(pre_ev, 1)
                sv = ss.rearrange("p (s k) -> p s k", s=2)[:, :, 2 * g:2 * g + 2]
                nc.vector.tensor_tensor(sv, bank(7, 64 + 4 * g, 4).rearrange("p (s k) -> p s k", s=2),
                                        ba.rearrange("p (s k) -> p s k", s=2)[:, :, 2 * g:2 * g + 2],
                                        ALU.add).then_inc(ss_set, 1)

            def h_low(k):
                dve.wait_ge(hhi_set, k + 1)
                link(nc.vector.tensor_scalar(xT[:, k, :], xT[:, k, :], ss[:, 8 + k:9 + k], ss[:, k:k + 1],
                                             ALU.mult, ALU.add))
                nc.vector.tensor_tensor(lov[:, k, :], xT[:, k, :], hiv[:, k, :].bitcast(F32),
                                        ALU.subtract).then_inc(hlo_set, 1)

            ada_sums(0)
            for k in range(1, KT, 2):
                dve.wait_ge(x_tr, k + 1)
                nc.vector.tensor_copy(xT[:, k, :], bank(k % 4)).then_inc(xt_dve, 1)
            for g in range(4):
                shift_scale(g)
                dve.wait_ge(ss_set, g + 1)
                h_low(2 * g)
                h_low(2 * g + 1)
                if g < 3:
                    ada_sums(g + 1)

            def blocks_of(v):
                for par in range(2):
                    for g in range(2):
                        b = ps[HD * g:HD * (g + 1), 512 * (S_BANK + v):512 * (S_BANK + v) + 512]
                        src = bass.AP(b.tensor, b.offset + par, [list(b.ap[0]), [2, 16], [CMP_STRIDE, N_CMP]])
                        pe = peT[HD * par:HD * (par + 1), 16 * v:16 * v + 16].unsqueeze(2)\
                            .to_broadcast([HD, 16, N_CMP])
                        ins = nc.vector.tensor_tensor(bt[HD * par:HD * (par + 1), v, :, N_CMP * g:N_CMP * (g + 1)],
                                                      src, pe, ALU.add)
                ins.then_inc(bt_set, 1)

            def low(dst, src, hi, scale, backwards):
                if backwards:
                    dst, src, hi = blocks(dst), blocks(src)[:, :, ::-1], blocks(hi)
                return nc.vector.scalar_tensor_tensor(out=dst, in0=src, scalar=scale, in1=hi.bitcast(F32),
                                                      op0=ALU.mult, op1=ALU.subtract)

            dve.wait_ge(p1_used, KT)
            blocks_of(0)
            for br in range(2):
                dve.wait_ge(kb_hi, br + 1)
                low(K[0:HD, 0, br, 1, :], bank(4 + br)[0:HD, :], K[0:HD, 0, br, 0, :], 1.0, False)
                low(K[HD:P, 1, br, 1, :], bank(4 + br)[HD:P, :], K[HD:P, 1, br, 0, :], 1.0, False).then_inc(kb_lo, 1)
            blocks_of(1)
            dve.wait_ge(gb_exp, 1)
            link(nc.vector.tensor_scalar(gates, gates, 1.0, None, ALU.add))
            link(nc.vector.reciprocal(gates, gates))
            dve.wait_ge(consts_set, 8)
            nc.vector.tensor_tensor(G0, G[:, :, 0, :], cmask.unsqueeze(2).to_broadcast([P, NT, 8]),
                                    ALU.mult).then_inc(g_set, 1)
            dve.wait_ge(g_set, 1)

            def hidden(v):
                dve.wait_ge(he_set, v + 1)
                link(nc.vector.tensor_scalar(HE, HE, 1.0, None, ALU.add))
                link(nc.vector.reciprocal(HE, HE))
                for jj in range(2):
                    hb = bank(T_BANK + jj, 0, 62)
                    if v == 0:
                        ins = nc.vector.tensor_tensor(HS[:, jj, :], hb, HE[:, jj, :], ALU.mult)
                    else:
                        for r in range(2):
                            ins = nc.vector.tensor_tensor(HSV[:, jj, :, r, 0:N_CMP],
                                                          hb.rearrange("p (g n) -> p g n", g=2),
                                                          HE[:, jj, :].rearrange("p (g n) -> p g n", g=2), ALU.mult)
                ins.then_inc(hs_set, 1)

            def tile_part(t):
                c, e = t // 3, t % 3
                src = bank(t % 2)
                if c < 4 and e > 0:
                    ev = et[:, 512 * (e - 1):512 * e]
                    dve.wait_ge(pj_act, act_tiles(t))
                    link(nc.vector.tensor_scalar(ev, ev, 1.0, None, ALU.add))
                    link(nc.vector.reciprocal(ev, ev))
                    for m in range(2):
                        dst = Z[:, 2 * (e - 1):2 * e, m * 512 + P * c:m * 512 + P * (c + 1)]
                        v = src.rearrange("p (t m d) -> p t m d", t=2, m=2)[:, :, m, :]
                        w = ev.rearrange("p (t m d) -> p t m d", t=2, m=2)[:, :, m, :]
                        ins = nc.vector.tensor_tensor(dst, v, w, ALU.mult)
                    ins.then_inc(pj_dve, 1)
                elif c < 4 or e == 1:
                    dve.wait_ge(pj_act, act_tiles(t))
                    if c >= 2:
                        dve.wait_ge(qk_done, UBASE[c - 1])
                    low(QS[HD:P, c % 2, 0, :], src[0:HD, :], QS[0:HD, c % 2, 0, :], -HD ** -0.5, True)
                    low(QS[0:HD, c % 2, 1, :], src[HD:P, :], QS[HD:P, c % 2, 1, :], -HD ** -0.5, True)\
                        .then_inc(pj_dve, 1)
                elif e == 0:
                    dve.wait_ge(pj_act, act_tiles(t))
                    low(K[0:HD, c % 2, 0, 1, :], src[0:HD, :], K[0:HD, c % 2, 0, 0, :], 1.0, False)
                    low(K[HD:P, c % 2, 1, 1, :], src[HD:P, :], K[HD:P, c % 2, 1, 0, :], 1.0, False)\
                        .then_inc(pj_dve, 1)
                else:
                    dve.wait_ge(pj, t + 1)
                    if c >= 6:
                        dve.wait_ge(pv_done, UBASE[c - 1])
                    nc.vector.tensor_copy(VAv[:, c % 2, :, :, 0:HD],
                                          src.rearrange("p (t h d) -> p t h d", t=NT, h=2)).then_inc(pj_dve, 1)

            def logits(n):
                kind, c, h, br, i = UNITS[n]
                dve.wait_ge(qk_done, n + 1)
                if n >= 4:
                    dve.wait_ge(tr_done, n - 3)
                if kind == "cmp":
                    dve.wait_ge(tc_set, c + 1)
                    v = lg[:, 512 * (n % 4):512 * (n % 4) + 256]
                    v3 = v.rearrange("p (q n) -> p q n", n=32)
                    link(nc.vector.tensor_tensor(v, bank(S_BANK + n % 2, 0, 256),
                                                 tc[:, 256 * (c % 2):256 * (c % 2) + 256], ALU.add))
                    link(nc.vector.tensor_reduce(mnc, v3, AX.X, ALU.min))
                    nc.vector.tensor_tensor(v3, v3, mnc.unsqueeze(2).to_broadcast([P, 8, 32]),
                                            ALU.subtract).then_inc(lg_set, 1)
                else:
                    w = P * (i + 1)
                    if h == 0 and br == 0 and i == 0:
                        dve.wait_ge(t_in[c % 2], 16 * (c // 2 + 1))
                    nc.vector.tensor_tensor_reduce(out=lg[:, 512 * (n % 4):512 * (n % 4) + w],
                                                   in0=bank(S_BANK + n % 2, 0, w),
                                                   in1=T[:, c % 2, h, SEQ - w:SEQ], scale=1.0, scalar=3e38,
                                                   op0=ALU.add, op1=ALU.min,
                                                   accum_out=mn[:, n % 8:n % 8 + 1]).then_inc(lg_set, 1)

            def cmp_norm(n):
                dve.wait_ge(ex_set, n + 1)
                v3 = lg[:, 512 * (n % 4):512 * (n % 4) + 256].rearrange("p (q n) -> p q n", n=32)
                link(nc.vector.tensor_reduce(rcc, v3, AX.X, ALU.add))
                link(nc.vector.reciprocal(rcc, rcc))
                nc.vector.tensor_tensor(v3, v3, rcc.unsqueeze(2).to_broadcast([P, 8, 32]),
                                        ALU.mult).then_inc(cn_set, 1)

            def evac(n):
                kind, c, h, br, i = UNITS[n]
                dve.wait_ge(tr_done, n + 1)
                if n >= 2:
                    dve.wait_ge(pv_done, n - 1)
                w = P * (i + 1)
                nc.vector.tensor_copy(pt[:, 512 * (n % 2):512 * (n % 2) + w], bank(T_BANK + n % 2, 0, w))\
                    .then_inc(ev_dve, 1)

            def group_end(n):
                kind, c, h, br, i = UNITS[n]
                dve.wait_ge(pv_done, n + 1)
                b = bank(O_BANK + GROUP[n] % 2)
                if kind == "cmp":
                    o = OS[:, :, D // 2 + P * c:D // 2 + P * (c + 1)].rearrange("p t (h d) -> p t h d", h=2)
                    nc.vector.tensor_tensor(o, b.rearrange("p (t h d) -> p t h d", t=NT, h=2),
                                            G0[:, :, 2 * c:2 * c + 2].unsqueeze(3).to_broadcast([P, NT, 2, HD]),
                                            ALU.mult).then_inc(og_set, 1)
                    return
                o = b[:, 0:NT * 65].rearrange("p (t d) -> p t d", t=NT)
                link(nc.vector.reciprocal(rc[:, 0:NT].unsqueeze(2), o[:, :, HD:HD + 1]))
                if c < 4:
                    link(nc.vector.tensor_tensor(rc[:, 4:8], rc[:, 0:4], G[:, :, 1 + br, 2 * c + h], ALU.mult))
                    if adds[0] >= 2:
                        dve.wait_ge(add_done, adds[0] - 1)
                    dst = tmp[:, 256 * (adds[0] % 2):256 * (adds[0] % 2) + 256].rearrange("p (t d) -> p t d", t=NT)
                    adds[0] += 1
                    r = rc[:, 4:8]
                else:
                    dst = OS[:, :, P * (c - 4) + HD * h:P * (c - 4) + HD * (h + 1)]
                    r = rc[:, 0:4]
                nc.vector.tensor_tensor(dst, o[:, :, 0:HD], r.unsqueeze(2).to_broadcast([P, NT, HD]),
                                        ALU.mult).then_inc(og_set, 1)

            def gate_sums(u):
                src = raw_landed(dve, u)[:, 0:D]
                k = u[1]
                if k == 0:
                    ins = nc.vector.tensor_scalar(gacc[:, :], src, cT[:, 0:1], None, ALU.mult)
                else:
                    dve.wait_ge(gate_used, k)
                    ins = nc.vector.scalar_tensor_tensor(out=gacc[:, :], in0=src, scalar=cT[:, k:k + 1],
                                                         in1=gacc[:, :], op0=ALU.mult, op1=ALU.add)
                ins.then_inc(gate_used, 1)

            adds = [0]
            n = 0
            pending = []
            for s in range(PAIRS + 1):
                for j in range(iters(s)):
                    if s >= 1:
                        logits(n)
                        if n >= 1 and UNITS[n - 1][0] == "cmp":
                            cmp_norm(n - 1)
                        if n >= 2 and not evac_on_act(n - 2):
                            evac(n - 2)
                        if n >= 4 and group_last(n - 4):
                            group_end(n - 4)
                        n += 1
                    for t in pending:
                        tile_part(t)
                    pending = [3 * s + e for e in tile_ends(s, j)] if s < PAIRS else []
                    for u in at_iter(s, j):
                        if u[0] == "gate":
                            gate_sums(u)
                    if s == 0 and j == 2:
                        hidden(0)
                    if s == 0 and j == 4:
                        dve.wait_ge(kc_hi, 1)
                        src = bank(7)[0:HD, 0:62].rearrange("p (g n) -> p g n", g=2)
                        for half in (0, HD):
                            ins = nc.vector.scalar_tensor_tensor(
                                out=KC[half:half + HD, 1, :, 0:N_CMP], in0=src, scalar=1.0,
                                in1=KC[0:HD, 0, :, 0:N_CMP].bitcast(F32), op0=ALU.mult, op1=ALU.subtract)
                        ins.then_inc(cmp_set, 1)
                    if s == 0 and j == 5:
                        hidden(1)
                        dve.wait_ge(cmp2, 2)
                        for g in range(2):
                            for r in range(2):
                                ins = nc.vector.tensor_copy(vc[32 * r:32 * r + 32, P * g + HD * r:P * g + HD * r + HD],
                                                            bank(6)[32 * r:32 * r + 32, HD * g:HD * g + HD])
                        ins.then_inc(cmp_set, 1)
                for t in pending:
                    tile_part(t)
                pending = []
            for m in (NU - 2, NU - 1):
                if not evac_on_act(m):
                    evac(m)
            for m in range(NU - 4, NU):
                if group_last(m):
                    group_end(m)
            dve.wait_ge(ln_in, 48)
            dve.wait_ge(grow, 1)
            nc.vector.scalar_tensor_tensor(out=et[:, :], in0=ps[:, 0:1024], scalar=1.0, in1=bgate, op0=ALU.add,
                                           op1=ALU.add).then_inc(g1_set, 1)
            dve.wait_ge(g1_set, 1)
            for t in range(NT + 1):
                if t < NT:
                    dve.wait_ge(ot_hi, t + 1)
                    nc.vector.tensor_tensor(OTl[:, t % 2, :, :].rearrange("p k t -> p (k t)"), ps[:, 2048:3072],
                                            OTh[:, t % 2, :, :].rearrange("p k t -> p (k t)").bitcast(F32),
                                            ALU.subtract).then_inc(ot_lo, 1)
                if t >= 1:
                    q = t - 1
                    y = yt[:, q % 2, :]
                    dve.wait_ge(y_done, t)
                    if q >= 2:
                        dve.wait_ge(out_done[q % 2], 16)
                    yb = ps[:, 1024 * (q % 2):1024 * (q % 2) + 1024]
                    nc.vector.tensor_tensor(y, yb, et[:, :], ALU.mult).then_inc(y_read, 1)
                    dve.wait_ge(y_read, t)
                    dve.wait_ge(res_in[q % 2], 16 * (q // 2 + 1))
                    link(nc.vector.scalar_tensor_tensor(out=y, in0=xr[:, q % 2, :], scalar=ALPHA, in1=y,
                                                        op0=ALU.mult, op1=ALU.add))
                    nc.vector.bn_stats(st[:, 0:6], y[:, 0:512])
                    link(nc.vector.bn_stats(st[:, 6:12], y[:, 512:1024]))
                    link(nc.vector.bn_aggr(mv, st))
                    nc.vector.tensor_scalar(mv[:, 1:2], mv[:, 1:2], LN_EPS, None, ALU.add).then_inc(var_set, 1)
                    dve.wait_ge(sd_set, t)
                    link(nc.vector.reciprocal(rstd[:, q:q + 1], sdv[:, q:q + 1]))
                    nc.vector.scalar_tensor_tensor(out=nmr[:, q:q + 1], in0=mv[:, 0:1], scalar=-1.0,
                                                   in1=rstd[:, q:q + 1], op0=ALU.mult, op1=ALU.mult)\
                        .then_inc(nm_set, 1)
                    dve.wait_ge(nm_set, t)

        @block.tensor
        def _(pe):
            mm = nc.tensor.matmul
            pe.wait_ge(small_in, 96)
            mm(ps[0:16, 2048:2048 + 512], rel, onehot[:, 0:512], start=True, stop=True)
            mm(ps[0:16, 2560:2560 + TROW - 512], rel, onehot[:, 512:TROW], start=True, stop=True).then_inc(pre_tr, 1)
            pe.wait_ge(consts_set, 1)
            nc.tensor.transpose(bank(7, 0, 16), ba_row, ident[0:16, 0:16])
            nc.tensor.transpose(bank(7, 16, 32), pe_row, ident[0:32, 0:32]).then_inc(pre_tr, 1)
            pe.wait_ge(x_in, 16)
            for k in range(KT):
                if k >= 4:
                    m = k - 4
                    pe.wait_ge(xt_dve if m % 2 else xt_act, m // 2 + 1)
                for t in range(NT):
                    ins = nc.tensor.transpose(bank(k % 4, P * t, P), x_tok[:, t, P * k:P * (k + 1)], ident[:, :])
                ins.then_inc(x_tr, 1)

            def three(dst, ah, al, bh, bl, start, stop, shared=False):
                mm(dst, ah, bh, start=start, stop=False, skip_group_check=shared)
                mm(dst, ah, bl, start=False, stop=False, skip_group_check=shared)
                return mm(dst, al, bh, start=False, stop=stop, skip_group_check=shared)

            def col(w, k, a, b):
                return w[:, k * W1ST + a:k * W1ST + b]

            for g in range(4):
                pe.wait_ge(ada_acc, g + 1)
                pe.wait_ge(pre_ev, 1)
                if g >= 1:
                    pe.wait_ge(ss_set, g)
                for q in range(4):
                    s, e = q // 2, q % 2
                    ins = mm(bank(7, 64 + 4 * g + q, 1), acc[:, 256 * s + P * e:256 * s + P * (e + 1)],
                             ones[:, 0:1], start=True, stop=True)
                ins.then_inc(ada_red, 1)
                if g == 0:
                    pe.wait_ge(xt_act, 4)
                    pe.wait_ge(xt_dve, 4)
                    pe.wait_ge(trow_ev, 1)
                pe.wait_ge(hi_set, g + 1)
                pe.wait_ge(lo_set, g + 1)
                for k in (2 * g, 2 * g + 1):
                    pe.wait_ge(hhi_set, k + 1)
                    pe.wait_ge(hlo_set, k + 1)
                    last = k == KT - 1
                    for b, a in ((2, 0), (3, 128), (4, 256), (5, 512)):
                        three(bank(b), col(w_hi, k, a, a + P), col(w_lo, k, a, a + P), hiv[:, k, :], lov[:, k, :],
                              k == 0, last)
                    for t in range(NT):
                        ht, lt = hiv[:, k, P * t:P * (t + 1)], lov[:, k, P * t:P * (t + 1)]
                        for q, a in ((0, 384), (1, 640)):
                            three(bank(t // 2, 256 * (t % 2) + P * q, P), ht, lt, col(w_hi, k, a, a + P),
                                  col(w_lo, k, a, a + P), k == 0 and t % 2 == 0 and q == 0, last, True)
                        ins = three(bank(6, 24 * t, 24), ht, lt, col(w_hi, k, 768, 792), col(w_lo, k, 768, 792),
                                    k == 0 and t == 0, last, True)
                    ins.then_inc(p1_used, 1)

            def tile_range(t, lo, hi):
                c, e = t // 3, t % 3
                by_token = c < 4 and e > 0 or c >= 4 and e == 2
                groups = [(k,) for k in range(KT)] if not by_token else \
                    [(tt, k) for tt in (range(2 * (e - 1), 2 * e) if c < 4 else range(NT)) for k in range(KT)]
                n = len(groups)
                for m, gr in enumerate(groups):
                    if not lo <= m / n < hi:
                        continue
                    k = gr[-1]
                    if m == 0:
                        if t < 2:
                            pe.wait_ge(tok_ev, t + 1)
                        else:
                            pe.wait_ge(pj_dve, t - 1)
                    if e == 0 and k % 4 == 0 and not by_token:
                        pe.wait_ge(hi_set, 4 + 2 * c + k // 4 + 1)
                        pe.wait_ge(lo_set, 4 + 2 * c + k // 4 + 1)
                    if not by_token:
                        ins = three(bank(t % 2), chunk(w_hi, c, k, P * e, P * e + P),
                                    chunk(w_lo, c, k, P * e, P * e + P), hiv[:, k, :], lov[:, k, :],
                                    k == 0, k == KT - 1)
                    else:
                        tt = gr[0]
                        a, b = (P, 3 * P) if c < 4 else (2 * P, 3 * P)
                        w = b - a
                        o = (tt % 2 if c < 4 else tt) * w
                        ins = three(bank(t % 2, o, w), hiv[:, k, P * tt:P * (tt + 1)], lov[:, k, P * tt:P * (tt + 1)],
                                    chunk(w_hi, c, k, a, b), chunk(w_lo, c, k, a, b), k == 0, k == KT - 1)
                    if m == n - 1:
                        ins.then_inc(pj, 1)

            def project(s, j):
                a, b = quantum(s, j)
                for e in range(3):
                    lo, hi = a - e, b - e
                    if hi > 0 and lo < 1:
                        tile_range(3 * s + e, lo, hi)

            def compress1(v, part):
                src = raw_landed(pe, ("w1", v, part))
                if part == 0:
                    pe.wait_ge(bt_set, v + 1)
                    if v == 0:
                        pe.wait_ge(kb_lo, 2)
                    else:
                        pe.wait_ge(hs_set, 1)
                k0, k1 = W1PARTS[part]
                for k in range(k0, k1):
                    for jj in range(2):
                        o = (k - k0) * CMP_HID + P * jj
                        ins = mm(bank(T_BANK + jj, 0, 62), src[:, o:o + P], bt[:, v, k, :], start=k == 0, stop=k == 15)
                ins.then_inc(w1_used, 1)

            def compress2(v):
                pe.wait_ge(hs_set, v + 1)
                if v == 0:
                    pe.wait_ge(w2_in, 16)
                    pe.wait_ge(ss_set, 4)
                    for jj in range(2):
                        ins = mm(bank(7)[0:HD, 0:62], W2[:, 0, jj, :], HS[:, jj, :], start=jj == 0, stop=jj == 1)
                else:
                    pe.wait_ge(gb_exp, 1)
                    for g in range(2):
                        for jj in range(2):
                            ins = mm(bank(6)[0:HD, HD * g:HD * (g + 1)],
                                     HSV[:, jj, g, :, :].rearrange("p r n -> p (r n)"), W2[:, 1, jj, :],
                                     start=jj == 0, stop=jj == 1)
                ins.then_inc(cmp2, 1)

            def scores(n):
                kind, c, h, br, i = UNITS[n]
                if n < 2:
                    pe.wait_ge(bt_set, 2)
                else:
                    pe.wait_ge(lg_set, n - 1)
                if n == UBASE[c]:
                    pe.wait_ge(pj_dve, 3 * c + (1 if c < 4 else 2))
                    if c < 4:
                        pe.wait_ge(cmp_set, 1)
                    pe.wait_ge(kdup[c // 2 if c < 4 else c % 2], 16 if c < 4 else 16 + 32 * (c // 2 - 1))
                b = S_BANK + n % 2
                if kind == "cmp":
                    for i in range(NT):
                        for h in range(2):
                            qt = QS[:, c % 2, h, P * i:P * (i + 1)]
                            o = bank(b, (2 * i + h) * 32, 32)
                            mm(o, qt, KC[:, 0, c // 2, :], start=True, stop=False)
                            ins = mm(o, qt, KC[:, 1, c // 2, :], start=False, stop=True)
                else:
                    w = P * (i + 1)
                    qt = QS[:, c % 2, h, P * i:P * (i + 1)]
                    sl, a = (c // 2, br) if c < 4 else (c % 2, h)
                    mm(bank(b, 0, w), qt, K[:, sl, a, 0, 0:w], start=True, stop=False)
                    ins = mm(bank(b, 0, w), qt, K[:, sl, a, 1, 0:w], start=False, stop=True)
                ins.then_inc(qk_done, 1)

            def turn(n):
                kind, c, h, br, i = UNITS[n]
                if kind == "cmp":
                    pe.wait_ge(cn_set, c + 1)
                else:
                    pe.wait_ge(ex_set, n + 1)
                if n < 2:
                    pe.wait_ge(hs_set, 2)
                else:
                    evacuated(pe, n - 2)
                src = lg[:, 512 * (n % 4):512 * (n % 4) + 512]
                b = T_BANK + n % 2
                if kind == "cmp":
                    for i in range(NT):
                        ins = nc.tensor.transpose(bank(b, P * i, P)[0:HD, :], src[:, HD * i:HD * (i + 1)], flip[:, :])
                else:
                    for m in range(i + 1):
                        ins = nc.tensor.transpose(bank(b, P * m, P), src[:, P * m:P * (m + 1)], flip[:, :])
                ins.then_inc(tr_done, 1)

            def values(n):
                kind, c, h, br, i = UNITS[n]
                evacuated(pe, n)
                gi = GROUP[n]
                if n == 0 or GROUP[n - 1] != gi:
                    pe.wait_ge(cmp_set, 2)
                    pe.wait_ge(tok_ev, 2)
                    if c >= 4:
                        pe.wait_ge(pj_dve, 3 * c + 3)
                    if gi >= 2:
                        pe.wait_ge(og_set, gi - 1)
                b = O_BANK + gi % 2
                src = pt[:, 512 * (n % 2):512 * (n % 2) + 512]
                if kind == "cmp":
                    for i in range(NT):
                        ins = mm(bank(b, P * i, P), src[0:HD, P * i:P * (i + 1)], vc[:, P * (c // 2):P * (c // 2 + 1)],
                                 start=True, stop=True)
                else:
                    for m in range(i + 1):
                        v = VB[:, m, br, c // 2, :] if c < 4 else VAv[:, c % 2, m, h, :]
                        ins = mm(bank(b, 65 * i, 65), src[:, P * m:P * (m + 1)], v, start=m == 0, stop=m == i)
                ins.then_inc(pv_done, 1)

            pe.wait_ge(flip_set, 1)
            n = 0
            for s in range(PAIRS + 1):
                for j in range(iters(s)):
                    if s >= 1:
                        scores(n)
                    if s < PAIRS:
                        project(s, j)
                    if s == 0:
                        compress1(j // 3, j % 3)
                        if j == 3:
                            compress2(0)
                        if j == 5:
                            compress2(1)
                    else:
                        if s == PAIRS and j == 0:
                            pe.wait_ge(gate_used, KT)
                            pe.wait_ge(pj_dve, 24)
                            mm(bank(0), ones[:, :], gacc[:, 0:512], start=True, stop=True)
                            mm(bank(1), ones[:, :], gacc[:, 512:1024], start=True, stop=True).then_inc(grow, 1)
                        if n >= 2:
                            turn(n - 2)
                        if n >= 3:
                            values(n - 3)
                        n += 1
            turn(NU - 2)
            values(NU - 3)
            turn(NU - 1)
            values(NU - 2)
            values(NU - 1)
            pe.wait_ge(gated, PAIRS)
            pe.wait_ge(hi_set, 28)
            pe.wait_ge(lo_set, 28)

            def turn_out(t):
                if t == 0:
                    evacuated(pe, NU - 1)
                    evacuated(pe, NU - 2)
                else:
                    pe.wait_ge(ot_hi, t)
                    pe.wait_ge(ot_lo, t)
                for k in range(KT):
                    ins = nc.tensor.transpose(bank(T_BANK + k // 4, P * (k % 4), P), OS[:, t, P * k:P * (k + 1)],
                                              ident[:, :])
                ins.then_inc(ot_tr, 1)

            turn_out(0)
            for t in range(NT):
                pe.wait_ge(ot_hi, t + 1)
                pe.wait_ge(ot_lo, t + 1)
                if t + 1 < NT:
                    turn_out(t + 1)
                if t == 0:
                    pe.wait_ge(g1_set, 1)
                if t >= 2:
                    pe.wait_ge(y_read, t - 1)
                for k in range(KT):
                    oh, ol = OTh[:, t % 2, k, :], OTl[:, t % 2, k, :]
                    for half in range(2):
                        b = bank(2 * (t % 2) + half)
                        wh = wo_at(w_hi, k)[:, 512 * half:512 * (half + 1)]
                        wl = wo_at(w_lo, k)[:, 512 * half:512 * (half + 1)]
                        ins = three(b, oh, ol, wh, wl, k == 0, k == KT - 1)
                ins.then_inc(y_done, 1)


def blocks(ap):
    return ap.rearrange("p (i t) -> p i t", t=P)


def shape_constants():
    k = np.arange(TROW)
    d = SEQ - 1 - k
    dm = np.maximum(d, 1)
    exact = N_B // 2
    large = exact + (np.log(dm.astype(np.float32) / np.float32(exact)) / np.log(MAX_DIST / exact)
                     * (N_B - exact)).astype(np.int32)
    bucket = np.where(d < exact, np.maximum(d, 0), np.minimum(large, N_B - 1))
    t = np.zeros((N_B + 2, TROW + 16), np.float32)
    t[bucket, k] = -1.0
    seen = sum(((d >= 0) & (d <= w) & (d % dil == 0)).astype(np.int64) for w, dil in DILATED)
    t[N_B, :TROW] = np.where(seen > 0, -np.log(np.maximum(seen, 1)), BIG)
    t[N_B + 1, :TROW] = np.where(d >= 0, 0.0, BIG)
    t[N_B, TROW:TROW + H_A] = 1.0
    t[N_B + 1, TROW + H_A:] = 1.0
    return t


def kernel(**inputs):
    import concourse.bacc as bacc
    from concourse.bass_utils import run_bass_kernel_spmd

    nc = bacc.Bacc("TRN2", target_bir_lowering=False, num_devices=1)
    arrays, aps = {}, {}
    for name in ("x", "c", "w_in", "w_out", "cmp_pe", "cmp_w1", "cmp_w2", "w_ada", "b_ada", "ln_g", "ln_b", "rel_bias"):
        a = np.ascontiguousarray(inputs[name])
        if name in ("w_in", "w_out", "cmp_pe", "cmp_w1", "cmp_w2", "w_ada"):
            a = a[0]
        arrays["in_" + name] = a
        aps[name] = nc.dram_tensor("in_" + name, a.shape, F32, kind="ExternalInput").ap()
    arrays["in_consts"] = shape_constants()
    consts = nc.dram_tensor("in_consts", arrays["in_consts"].shape, F32, kind="ExternalInput").ap()
    scratch = nc.dram_tensor("bias_rows", (16, TROW), F32, kind="Internal").ap()
    out = nc.dram_tensor("out", (1, SEQ, D), F32, kind="ExternalOutput").ap()
    build(nc, aps["x"], aps["c"], aps["w_in"], aps["w_out"], aps["cmp_pe"], aps["cmp_w1"], aps["cmp_w2"],
          aps["w_ada"], aps["b_ada"], aps["ln_g"], aps["ln_b"], aps["rel_bias"], consts, scratch, out)
    r = run_bass_kernel_spmd(nc, [arrays], core_ids=[0])
    return r.results[0]["out"]
```

```python
from contextlib import ExitStack

import numpy as np

import concourse.bass as bass
from concourse import mybir

F32 = mybir.dt.float32
F32R = mybir.dt.float32r
ACT = mybir.ActivationFunctionType
ALU = mybir.AluOpType
AX = mybir.AxisListType

P = 128
SEQ = 512
D = 1024
NT = SEQ // P
KT = D // P
HD = 64
H_A = H_B = 8
N_B = 32
MAX_DIST = 2048
DILATED = ((128, 1), (512, 4), (2048, 16))
CMP_LEN, CMP_STRIDE, CMP_HID = 32, 16, 256
N_CMP = SEQ // CMP_STRIDE - 1
ALPHA = 2.0 ** 0.25
LN_EPS = 1e-5
BIG = 1e30

QA, KA, VA, ZA, QB, KVB, GB, ZB = 0, 512, 1024, 1536, 2048, 2560, 3328, 3352
W1ST = GB + 24 - KVB
PAIRS = 8
CW = 384
RAWC = 2 * W1ST
NRAW = 3
TROW = 640


CHUNKS = (
    ((QB, ZA, ZB), (("q", 0, 0), ("z", 0, 0), ("z", 0, 1))),
    ((QB + P, ZA + P, ZB + P), (("q", 1, 0), ("z", 1, 0), ("z", 1, 1))),
    ((QB + 2 * P, ZA + 2 * P, ZB + 2 * P), (("q", 2, 0), ("z", 2, 0), ("z", 2, 1))),
    ((QB + 3 * P, VA, VA + P), (("q", 3, 0), ("v", 0, 0), ("v", 0, 1))),
    ((KA, QA, KA + P), (("k", 4, 0), ("q", 4, 0), ("k", 5, 0))),
    ((QA + P, VA + 2 * P, VA + 3 * P), (("q", 5, 0), ("v", 1, 0), ("v", 1, 1))),
    ((KA + 2 * P, QA + 2 * P, KA + 3 * P), (("k", 6, 0), ("q", 6, 0), ("k", 7, 0))),
    ((QA + 3 * P, ZA + 3 * P, ZB + 3 * P), (("q", 7, 0), ("z", 3, 0), ("z", 3, 1))),
)
TILES = [t for _, ts in CHUNKS for t in ts]
TILE = {t: n for n, t in enumerate(TILES)}


def units_of(c):
    if c < 4:
        return [("cmp", c, 0, 0, 0)] + [("att", c, h, br, i) for h in range(2) for br in range(2) for i in range(NT)]
    return [("att", c, h, 0, i) for h in range(2) for i in range(NT)]


LAG_T = 3
LAG_V = 4
UNITS = [u for c in range(PAIRS) for u in units_of(c)]
NU = len(UNITS)
UBASE = [sum(len(units_of(b)) for b in range(c)) for c in range(PAIRS + 1)]
GROUP = []
for _n, _u in enumerate(UNITS):
    GROUP.append(0 if _n == 0 else GROUP[-1] + (_u[0] == "cmp" or _u[4] == 0))


def evac_on_act(n):
    return UNITS[n][0] == "cmp" or UNITS[n][4] in (0, 3)


def group_last(m):
    return m + 1 == NU or GROUP[m + 1] != GROUP[m]


def evacs(n, on_act):
    return sum(evac_on_act(m) == on_act for m in range(n + 1))


def iters(s):
    return 6 if s == 0 else len(units_of(s - 1))


def quantum(s, j):
    return 3 * j / iters(s), 3 * (j + 1) / iters(s)


def ended(s, j, lag):
    j -= lag
    while j < 0:
        s -= 1
        if s < 0:
            return []
        j += iters(s)
    if s >= PAIRS:
        return []
    a, b = quantum(s, j)
    return [3 * s + e for e in range(3) if a <= e + 1 - 1e-3 < b]


def raw_order():
    r = [("p1", g, 0) for g in range(4)] + [("ch", 0, 0), ("ch", 0, 1)]
    r += [("w1", 0, 0), ("w1", 0, 1), ("ch", 1, 0), ("w1", 0, 2), ("w1", 1, 0), ("ch", 1, 1), ("w1", 1, 1), ("w1", 1, 2)]
    for s in range(1, 7):
        g = [("gate", 2 * (s - 4), 0)] if s >= 4 else []
        g2 = [("gate", 2 * (s - 4) + 1, 0)] if s >= 4 else []
        r += [("ch", s + 1, 0)] + g + [("ch", s + 1, 1)] + g2
    r += [("wo", 0, 0), ("gate", 6, 0), ("wo", 1, 0), ("gate", 7, 0), ("wo", 2, 0)]
    return r + [("wo", k, 0) for k in range(3, 8)]


RAW = raw_order()
RAWI = {u: n for n, u in enumerate(RAW)}
RAWD = {"p1": 1, "ch": 3, "w1": 1, "gate": 1, "wo": 1}
W1PARTS = ((0, 6), (6, 12), (12, 16))


def raw_count(n):
    return sum(16 * RAWD[RAW[m][0]] for m in range(n % NRAW, n + 1, NRAW))


def split_no(u):
    return {"p1": u[1], "ch": 4 + 2 * u[1] + u[2], "wo": 20 + u[1]}[u[0]]


def at_iter(s, j):
    n = iters(s)
    if s == 0:
        return {1: [("ch", 1, 0)], 4: [("ch", 1, 1)]}.get(j, [])
    if s <= 6:
        plan = [(n // 4, ("ch", s + 1, 0)), (3 * n // 4, ("ch", s + 1, 1))]
        if s >= 4:
            plan += [(n // 4 + 1, ("gate", 2 * (s - 4), 0)), (3 * n // 4 + 1, ("gate", 2 * (s - 4) + 1, 0))]
    elif s == 7:
        plan = [(1, ("wo", 0, 0)), (2, ("gate", 6, 0)), (3, ("wo", 1, 0)), (4, ("gate", 7, 0)), (6, ("wo", 2, 0))]
    else:
        plan = [(k - 3, ("wo", k, 0)) for k in range(3, 8)]
    return [u for k, u in plan if k == j]


def build(nc, x, c_in, w_in, w_out, cmp_pe, cmp_w1, cmp_w2, w_ada, b_ada, ln_g, ln_b, rel_bias, consts, scratch, out):
    with ExitStack() as ctx:
        def sb(name, cols, dt=F32, parts=P):
            return ctx.enter_context(nc.sbuf_tensor(name, [parts, cols], dt))

        def sem(name):
            return ctx.enter_context(nc.semaphore(name))

        w_hi = sb("w_hi", KT * W1ST, F32R)
        w_lo = sb("w_lo", KT * W1ST, F32R)
        raw = sb("raw", NRAW * RAWC)
        with nc.sbuf_tensor("x_tok", [P, NT * D], F32) as x_tok_t:
            x_tok = x_tok_t[:, :].rearrange("p (t d) -> p t d", t=NT)
        h_hi = sb("h_hi", KT * SEQ, F32R)
        h_lo = sb("h_lo", KT * SEQ, F32R)
        with nc.sbuf_tensor("ada", [P, 2 * 4096], F32) as ada_t:
            ada = ada_t[:, :].rearrange("p (b s k f) -> p b s k f", b=2, s=2, k=KT)
        z = sb("z", NT * D)
        kk = sb("kk", 4096, F32R)
        qs = sb("qs", 2048, F32R)
        vb = sb("vb", NT * 4 * 65)
        va = sb("va", 2 * NT * 2 * 65)
        tb_ = sb("tb", 2048)
        lg = sb("lg", 2048)
        pt = sb("pt", 1024)
        os_ = sb("os", NT * D)
        gacc = sb("gacc", D)
        et = sb("et", 1024)
        tmp = sb("tmp", 512)
        tc = sb("tc", 512)
        w2 = sb("w2", 256)
        hs = sb("hs", 2 * 62)
        hsv = sb("hsv", 2 * 2 * 64)
        he = sb("he", 2 * 62)
        kc = sb("kc", 2 * 2 * 32, F32R)
        vc = sb("vc", 2 * P, parts=64)
        acc = sb("acc", 512)
        ident = sb("ident", P)
        flip = sb("flip", P)
        ones = sb("ones", P)
        small = sb("small", 320)
        cT = small[:, 0:8]
        ba = small[:, 8:24]
        ss = small[:, 24:40]
        peT = small[:, 40:72]
        mn = small[:, 72:80]
        mnc = small[:, 80:88]
        rcc = small[:, 88:96]
        rcs = small[:, 272:288]
        gates = small[:, 104:200]
        cmask = small[:, 200:204]
        g0 = small[:, 204:236]
        st = small[:, 236:248]
        mv = small[:, 248:250]
        rstd = small[:, 250:254]
        nmr = small[:, 254:258]
        sdv = small[:, 258:262]
        zero1 = small[:, 262:263]

        hiv = h_hi[:, :].rearrange("p (k t) -> p k t", k=KT)
        lov = h_lo[:, :].rearrange("p (k t) -> p k t", k=KT)
        xT = os_[:, :].rearrange("p (k t) -> p k t", k=KT)
        bt = os_[:, 0:2 * 16 * 62].rearrange("p (v k n) -> p v k n", v=2, k=16)
        OS = os_[:, :].rearrange("p (t d) -> p t d", t=NT)
        Z = z[:, :].rearrange("p (t d) -> p t d", t=NT)
        K = kk[:, :].rearrange("p (s a l t) -> p s a l t", s=2, a=2, l=2)
        QS = qs[:, :].rearrange("p (s h t) -> p s h t", s=2, h=2)
        VB = vb[:, :].rearrange("p (t b g d) -> p t b g d", t=NT, b=2, g=2)
        VAv = [w[:, :].rearrange("p (s t h d) -> p s t h d", s=2, t=NT, h=2) for w in (va, vb)]
        T = tb_[:, :].rearrange("p (s h x) -> p s h x", s=2, h=2)
        Tc = tc[:, :].rearrange("p (s i h n) -> p s i h n", s=2, i=NT, h=2)
        KC = kc[:, :].rearrange("p (l g n) -> p l g n", l=2, g=2)
        W2 = w2[:, :].rearrange("p (v j d) -> p v j d", v=2, j=2)
        HS = hs[:, :].rearrange("p (j n) -> p j n", j=2)
        HSV = hsv[:, :].rearrange("p (j g r n) -> p j g r n", j=2, g=2, r=2)
        HE = he[:, :].rearrange("p (j n) -> p j n", j=2)
        G = gates.rearrange("p (t b h) -> p t b h", t=NT, b=3)
        G0 = g0.rearrange("p (t h) -> p t h", t=NT)
        onehot, rel = lg[0:34, 0:TROW], lg[0:34, TROW:TROW + 16]
        trow = lg[0:16, 704:704 + TROW]
        ba_row, pe_row = lg[0:16, 1344:1472], lg[0:32, 1472:1600]
        OTh = kk[:, 0:2048].rearrange("p (r k t) -> p r k t", r=2, k=KT)
        OTl = kk[:, 2048:4096].rearrange("p (r k t) -> p r k t", r=2, k=KT)
        xr = tb_[:, :].rearrange("p (r d) -> p r d", r=2)
        yt = lg[:, :].rearrange("p (r d) -> p r d", r=2)
        lng, lnb, bgate = raw[:, 0:D], raw[:, D:2 * D], raw[:, 2 * D:3 * D]

        def slot(n):
            return raw[:, (n % NRAW) * RAWC:(n % NRAW + 1) * RAWC]

        def split_at(w, u):
            kind, a, b = u
            if kind == "p1":
                return w[:, 2 * a * W1ST:2 * (a + 1) * W1ST]
            if kind == "ch":
                o = (a % 2) * KT * CW + b * 4 * CW
                return w[:, o:o + 4 * CW]
            return wo_at(w, a)

        def wo_at(w, k):
            if k < 6:
                return w[:, k * D:(k + 1) * D]
            hx = h_hi if w is w_hi else h_lo
            return hx[:, (k - 6) * D:(k - 5) * D]

        def width(u):
            return {"p1": RAWC, "ch": 4 * CW, "wo": D}[u[0]]

        def chunk(w, c, k, a, b):
            o = (c % 2) * KT * CW + k * CW
            return w[:, o + a:o + b]

        ps = ctx.enter_context(nc.psum_tensor("ps", [P, 4096], F32))

        def bank(b, a=0, n=512):
            return ps[:, 512 * b + a:512 * b + a + n]

        S_BANK, T_BANK, O_BANK = 2, 4, 6

        small_in = sem("small_in")
        w2_in = sem("w2_in")
        x_in = [sem(f"x_in{half}") for half in range(2)]
        ada_in = [[sem(f"ada_in{b}{half}") for half in range(2)] for b in range(2)]
        raw_in = [sem(f"raw_in{b}") for b in range(NRAW)]
        trow_out = sem("trow_out")
        t_in = [sem(f"t_in{b}") for b in range(2)]
        kdup = [sem(f"kdup{b}") for b in range(2)]
        consts_set = sem("consts_set")
        flip_set = sem("flip_set")
        pre_tr = sem("pre_tr")
        pre_ev = sem("pre_ev")
        trow_ev = sem("trow_ev")
        x_tr = sem("x_tr")
        xt_act = sem("xt_act")
        xt_dve = sem("xt_dve")
        ada_acc = sem("ada_acc")
        ada_red = sem("ada_red")
        ss_set = sem("ss_set")
        hhi_set = sem("hhi_set")
        hlo_set = sem("hlo_set")
        hi_set = sem("hi_set")
        lo_set = sem("lo_set")
        p1_used = sem("p1_used")
        tok_ev = sem("tok_ev")
        gb_exp = sem("gb_exp")
        gb_tr = sem("gb_tr")
        g_set = sem("g_set")
        kb_hi = sem("kb_hi")
        kb_lo = sem("kb_lo")
        bt_set = sem("bt_set")
        w1_used = sem("w1_used")
        he_set = sem("he_set")
        hs_set = sem("hs_set")
        cmp2 = sem("cmp2")
        kc_hi = sem("kc_hi")
        cmp_set = sem("cmp_set")
        pj = sem("pj")
        pj_act = sem("pj_act")
        pj_dve = sem("pj_dve")
        qk_done = sem("qk_done")
        lg_set = sem("lg_set")
        ex_set = sem("ex_set")
        cn_set = sem("cn_set")
        tr_done = sem("tr_done")
        ev_act = sem("ev_act")
        ev_dve = sem("ev_dve")
        pv_done = sem("pv_done")
        og_set = sem("og_set")
        add_done = sem("add_done")
        gated = sem("gated")
        tc_set = sem("tc_set")
        gate_used = sem("gate_used")
        grow = sem("grow")
        g1_set = sem("g1_set")
        res_in = [sem(f"res_in{b}") for b in range(2)]
        ln_in = sem("ln_in")
        ot_tr = sem("ot_tr")
        ot_hi = sem("ot_hi")
        ot_lo = sem("ot_lo")
        y_done = sem("y_done")
        y_read = sem("y_read")
        var_set = sem("var_set")
        sd_set = sem("sd_set")
        nm_set = sem("nm_set")
        norm_set = sem("norm_set")
        aff_set = sem("aff_set")
        out_done = [sem(f"out_done{b}") for b in range(2)]
        dve_step = sem("dve_step")
        act_step = sem("act_step")
        pool_step = sem("pool_step")

        def raw_free(eng, n):
            kind, a, b = RAW[n]
            if kind in ("p1", "ch", "wo"):
                eng.wait_ge(hi_set, split_no(RAW[n]) + 1)
                eng.wait_ge(lo_set, split_no(RAW[n]) + 1)
            elif kind == "w1":
                eng.wait_ge(w1_used, 3 * a + b + 1)
            else:
                eng.wait_ge(gate_used, a + 1)

        def raw_landed(eng, u):
            n = RAWI[u]
            eng.wait_ge(raw_in[n % NRAW], raw_count(n))
            return slot(n)

        def evacuated(eng, n):
            on_act = evac_on_act(n)
            eng.wait_ge(ev_act if on_act else ev_dve, evacs(n, on_act))

        def act_tiles(t):
            return sum(TILES[m][0] != "v" for m in range(t + 1))

        def store(sp, t):
            sp.wait_ge(aff_set, t + 1)
            sp.dma_start(out[0, t * P:(t + 1) * P, :], yt[:, t % 2, :]).then_inc(out_done[t % 2], 16)

        block = ctx.enter_context(nc.Block())

        @block.sync
        def _(sp):
            sp.dma_start(onehot, consts[:, 0:TROW]).then_inc(small_in, 16)
            sp.dma_start(rel[N_B:N_B + 2, :], consts[N_B:N_B + 2, TROW:TROW + 16]).then_inc(small_in, 16)
            sp.dma_start(rel[0:N_B, :], rel_bias).then_inc(small_in, 16)
            sp.dma_start(cT, c_in.rearrange("o (p k) -> (o p) k", k=KT)).then_inc(small_in, 16)
            sp.dma_start(ba_row, b_ada[:, 0:2 * D].rearrange("o (j q) -> (o j) q", q=P)).then_inc(small_in, 16)
            sp.dma_start(pe_row, cmp_pe.rearrange("v (k r) d -> (v k) (r d)", r=2)).then_inc(small_in, 16)

            def load_ada(g):
                if g >= 2:
                    sp.wait_ge(ada_acc, g - 1)
                for half in range(2):
                    k4 = slice(4 * half, 4 * half + 4)
                    for s in range(2):
                        src = w_ada[:, s * D + 256 * g:s * D + 256 * (g + 1)].rearrange("(p k) f -> p k f", k=KT)
                        sp.dma_start(ada[:, g % 2, s, k4, :], src[:, k4, :]).then_inc(ada_in[g % 2][half], 16)

            def load_raw(n):
                if n >= NRAW:
                    raw_free(sp, n - NRAW)
                kind, a, b = RAW[n]
                d, s = slot(n), raw_in[n % NRAW]
                if kind == "p1":
                    sp.dma_start(d.rearrange("p (k f) -> p k f", k=2),
                                 w_in[2 * a * P:2 * (a + 1) * P, KVB:KVB + W1ST]
                                 .rearrange("(k p) f -> p k f", p=P)).then_inc(s, 16)
                elif kind == "ch":
                    dv = d[:, 0:4 * CW].rearrange("p (k f) -> p k f", k=4)
                    for m, col in enumerate(CHUNKS[a][0]):
                        sp.dma_start(dv[:, :, m * P:(m + 1) * P],
                                     w_in[4 * b * P:4 * (b + 1) * P, col:col + P]
                                     .rearrange("(k p) f -> p k f", p=P)).then_inc(s, 16)
                elif kind == "w1":
                    k0, k1 = W1PARTS[b]
                    sp.dma_start(d[:, 0:(k1 - k0) * CMP_HID].rearrange("p (k f) -> p k f", f=CMP_HID),
                                 cmp_w1[a, k0 * P:k1 * P, :].rearrange("(k p) f -> p k f", p=P)).then_inc(s, 16)
                elif kind == "gate":
                    sp.dma_start(d[:, 0:D], w_ada[:, 2 * D:3 * D].rearrange("(p k) f -> p k f", k=KT)[:, a, :])\
                        .then_inc(s, 16)
                else:
                    sp.dma_start(d[:, 0:D], w_out[a * P:(a + 1) * P, :]).then_inc(s, 16)

            def load_tables(c):
                if c >= 2:
                    sp.wait_ge(lg_set, UBASE[c - 1])
                h0 = H_A + 2 * c if c < 4 else 2 * (c - 4)
                src = bass.AP(scratch.tensor, h0 * TROW, [[1, P], [TROW, 2], [1, SEQ]])
                sp.dma_start(T[:, c % 2, :, :], src).then_inc(t_in[c % 2], 16)

            for half in range(2):
                f = slice(512 * half, 512 * half + 512)
                sp.dma_start(x_tok[:, :, f], x[0].rearrange("(t p) d -> p t d", p=P)[:, :, f]).then_inc(x_in[half], 16)
            load_ada(0)
            load_raw(0)
            load_ada(1)
            load_raw(1)
            load_ada(2)
            load_raw(2)
            load_ada(3)
            load_raw(3)
            sp.dma_start(W2, cmp_w2.rearrange("v (j p) d -> p v j d", p=P)).then_inc(w2_in, 16)
            sp.wait_ge(trow_ev, 1)
            sp.dma_start(scratch, trow).then_inc(trow_out, 16)
            sp.wait_ge(trow_out, 16)
            load_tables(0)
            load_tables(1)
            n = 4
            for s in range(PAIRS + 1):
                if 2 <= s < PAIRS:
                    load_tables(s)
                last = RAWI[{0: ("w1", 1, 2), 7: ("wo", 2, 0), 8: ("wo", 7, 0)}.get(s, ("ch", s + 1, 1))]
                if 4 <= s <= 6:
                    last += 1
                while n <= last:
                    load_raw(n)
                    n += 1
            for m in range(len(RAW) - NRAW, len(RAW)):
                raw_free(sp, m)
            sp.dma_start(bgate, b_ada[0, 2 * D:3 * D].partition_broadcast(P)).then_inc(ln_in, 16)
            sp.dma_start(lng, ln_g[0].partition_broadcast(P)).then_inc(ln_in, 16)
            sp.dma_start(lnb, ln_b[0].partition_broadcast(P)).then_inc(ln_in, 16)
            sp.wait_ge(lg_set, NU)
            for t in range(NT):
                if t >= 2:
                    sp.wait_ge(norm_set, t - 1)
                sp.dma_start(xr[:, t % 2, :], x[0, t * P:(t + 1) * P, :]).then_inc(res_in[t % 2], 16)
                if t >= 2:
                    store(sp, t - 2)
            for t in range(NT - 2, NT):
                store(sp, t)
            for b in range(2):
                sp.wait_ge(out_done[b], 32)

        @block.gpsimd
        def _(pool):
            nc.gpsimd.memset(ident[:, :], 0.0).then_inc(pool_step, 1)
            nc.gpsimd.memset(flip[:, :], 0.0).then_inc(pool_step, 1)
            nc.gpsimd.memset(cmask, 1.0).then_inc(pool_step, 1)
            nc.gpsimd.memset(ones[:, :], 1.0).then_inc(pool_step, 1)
            pool.wait_ge(pool_step, 4)
            nc.gpsimd.affine_select(out=ident[:, :], in_=ident[:, :], compare_op=ALU.not_equal, fill=1.0, base=0,
                                    pattern=[[-1, P]], channel_multiplier=1).then_inc(consts_set, 1)
            nc.gpsimd.affine_select(out=flip[:, :], in_=flip[:, :], compare_op=ALU.not_equal, fill=1.0,
                                    base=-(P - 1), pattern=[[1, P]], channel_multiplier=1).then_inc(flip_set, 1)
            nc.gpsimd.affine_select(out=cmask[:, 0:1], in_=cmask[:, 0:1], compare_op=ALU.is_ge, fill=0.0,
                                    base=-(CMP_LEN - 1), pattern=[[0, 1]], channel_multiplier=1)\
                .then_inc(consts_set, 1)
            nc.gpsimd.memset(tc[:, :], BIG).then_inc(consts_set, 1)
            nc.gpsimd.memset(hsv[:, :], 0.0).then_inc(consts_set, 1)
            nc.gpsimd.memset(kc[:, :].bitcast(F32), 0.0).then_inc(consts_set, 1)
            nc.gpsimd.memset(vc[:, :], 0.0).then_inc(consts_set, 1)
            nc.gpsimd.memset(vb[:, :], 1.0).then_inc(consts_set, 1)
            nc.gpsimd.memset(va[:, :], 1.0).then_inc(consts_set, 1)

            def split_lo(u):
                src = raw_landed(pool, u)
                n = width(u)
                pool.wait_ge(hi_set, split_no(u) + 1)
                nc.gpsimd.tensor_tensor(split_at(w_lo, u), src[:, 0:n], split_at(w_hi, u).bitcast(F32),
                                        ALU.subtract).then_inc(lo_set, 1)

            def compressed_bias(c):
                pool.wait_ge(t_in[c % 2], 16 * (c // 2 + 1))
                if c >= 2:
                    pool.wait_ge(lg_set, UBASE[c - 2] + 1)
                for i in range(NT):
                    n = 8 * i + 7
                    o = SEQ - P + CMP_LEN - 1 - P * i
                    ins = nc.gpsimd.tensor_copy(Tc[:, c % 2, i, :, 0:n],
                                                T[:, c % 2, :, o:o + CMP_STRIDE * (n - 1) + 1:CMP_STRIDE])
                ins.then_inc(tc_set, 1)

            def group_adds(n):
                kind, c, h, br, i = UNITS[n]
                if kind == "att" and c < 4:
                    r = GROUP[n]
                    pool.wait_ge(og_set, r + 1)
                    col = D // 2 + P * c + HD * h
                    if adds[0]:
                        pool.wait_ge(add_done, adds[0])
                    nc.gpsimd.tensor_tensor(OS[:, :, col:col + HD], OS[:, :, col:col + HD],
                                            tmp[:, 256 * (adds[0] % 2):256 * (adds[0] % 2) + 256]
                                            .rearrange("p (t d) -> p t d", t=NT), ALU.add).then_inc(add_done, 1)
                    adds[0] += 1
                if n + 1 == UBASE[c + 1] and c != 3:
                    pool.wait_ge(og_set, GROUP[n] + 1)
                    if c < 4:
                        pool.wait_ge(add_done, adds[0])
                    gate_pair(c)

            def gate_pair(c):
                col = D // 2 + P * c if c < 4 else P * (c - 4)
                pool.wait_ge(pj_dve, TILE["z", c % 4, 1] + 1)
                nc.gpsimd.tensor_tensor(OS[:, :, col:col + P], OS[:, :, col:col + P], Z[:, :, col:col + P],
                                        ALU.mult).then_inc(gated, 1)

            adds = [0]
            for g in range(4):
                split_lo(("p1", g, 0))
            split_lo(("ch", 0, 0))
            split_lo(("ch", 0, 1))
            n = 0
            for s in range(PAIRS + 1):
                for j in range(iters(s)):
                    if s < 4 and j == iters(s) // 2:
                        compressed_bias(s)
                    for u in at_iter(s, j):
                        if u[0] != "gate":
                            split_lo(u)
                    if s >= 1:
                        m = n - LAG_V - 1
                        if m >= 0 and group_last(m):
                            group_adds(m)
                        if s == PAIRS and j == 2:
                            pool.wait_ge(add_done, adds[0])
                            gate_pair(3)
                        n += 1
            for m in range(NU - LAG_V - 1, NU):
                if group_last(m):
                    group_adds(m)
            pool.wait_ge(ln_in, 48)
            for t in range(NT):
                pool.wait_ge(norm_set, t + 1)
                nc.gpsimd.tensor_tensor(yt[:, t % 2, :], yt[:, t % 2, :], lng, ALU.mult).then_inc(pool_step, 1)
                pool.wait_ge(pool_step, 5 + t)
                nc.gpsimd.tensor_tensor(yt[:, t % 2, :], yt[:, t % 2, :], lnb, ALU.add).then_inc(aff_set, 1)

        @block.scalar
        def _(act):
            def split_hi(u):
                src = raw_landed(act, u)
                kind, a, b = u
                if kind == "ch" and a == 0:
                    act.wait_ge(p1_used, 4)
                elif kind == "ch" and a == 1:
                    act.wait_ge(p1_used, KT)
                elif kind == "ch":
                    act.wait_ge(pj, 3 * (a - 1))
                elif kind == "wo":
                    act.wait_ge(pj, 21 if a < 3 else 24)
                n = width(u)
                nc.scalar.activation(split_at(w_hi, u), src[:, 0:n], ACT.Copy).then_inc(hi_set, 1)

            def q_or_k_hi(src, tile0, tile1, scale, s, n, backwards):
                for a, dst in ((0, tile0), (1, tile1)):
                    o = src[HD * a:HD * (a + 1), :]
                    if backwards:
                        o, dst = blocks(o)[:, :, ::-1], blocks(dst)
                    ins = nc.scalar.activation(dst, o, ACT.Copy, scale=scale)
                ins.then_inc(s, n)

            def tile_part(t):
                kind, c, part = TILES[t]
                src = bank(t % 2)
                if kind == "v":
                    return
                act.wait_ge(pj, t + 1)
                if kind == "z":
                    if c >= 1:
                        act.wait_ge(pj_dve, TILE["z", c - 1, part] + 1)
                    nc.scalar.activation(et[:, 512 * part:512 * part + 512], src, ACT.Tanh, scale=0.5)\
                        .then_inc(pj_act, 1)
                elif kind == "q":
                    if c >= 2:
                        act.wait_ge(qk_done, UBASE[c - 1])
                    q_or_k_hi(src, QS[0:HD, c % 2, 0, :], QS[HD:P, c % 2, 1, :], -HD ** -0.5, pj_act, 1, True)
                else:
                    act.wait_ge(qk_done, UBASE[{4: 2, 5: 4, 6: 5, 7: 6}[c]])
                    q_or_k_hi(src, K[0:HD, c % 2, 0, 0, :], K[HD:P, c % 2, 1, 0, :], 1.0, pj_act, 1, False)

            def double_keys(t):
                kind, c, part = TILES[t]
                act.wait_ge(pj_dve, t + 1)
                act.dma_start(K[HD:P, c % 2, 0, :, :].bitcast(F32), K[0:HD, c % 2, 0, :, :].bitcast(F32))\
                    .then_inc(kdup[c % 2], 16)
                act.dma_start(K[0:HD, c % 2, 1, :, :].bitcast(F32), K[HD:P, c % 2, 1, :, :].bitcast(F32))\
                    .then_inc(kdup[c % 2], 16)

            def probs(n):
                kind, c, h, br, i = UNITS[n]
                act.wait_ge(lg_set, n + 1)
                if kind == "cmp":
                    v = lg[:, 512 * (n % 4):512 * (n % 4) + 256]
                    nc.scalar.activation(v, v, ACT.Exp, scale=-1.0).then_inc(ex_set, 1)
                else:
                    v = lg[:, 512 * (n % 4):512 * (n % 4) + P * (i + 1)]
                    nc.scalar.activation(v, v, ACT.Exp, bias=mn[:, n % 8:n % 8 + 1], scale=-1.0).then_inc(ex_set, 1)

            def evac(n):
                kind, c, h, br, i = UNITS[n]
                act.wait_ge(tr_done, n + 1)
                if n >= 2:
                    act.wait_ge(pv_done, n - 1)
                w = 512 if kind == "cmp" else P * (i + 1)
                m = HD if kind == "cmp" else P
                nc.scalar.activation(pt[0:m, 512 * (n % 2):512 * (n % 2) + w], bank(T_BANK + n % 2)[0:m, 0:w],
                                     ACT.Copy).then_inc(ev_act, 1)

            for k in range(0, KT, 2):
                act.wait_ge(x_tr, k + 1)
                nc.scalar.activation(xT[:, k, :], bank(k % 4), ACT.Copy).then_inc(xt_act, 1)
            for g in range(4):
                split_hi(("p1", g, 0))
                act.wait_ge(ss_set, g + 1)
                for k in (2 * g, 2 * g + 1):
                    act.wait_ge(xt_dve if k % 2 else xt_act, k // 2 + 1)
                    act.wait_ge(x_tr, KT)
                    nc.scalar.activation(hiv[:, k, :], xT[:, k, :], ACT.Identity, bias=ss[:, k:k + 1],
                                         scale=ss[:, 8 + k:9 + k]).then_inc(hhi_set, 1)
            split_hi(("ch", 0, 0))
            split_hi(("ch", 0, 1))
            act.wait_ge(p1_used, KT)
            act.wait_ge(consts_set, 8)
            for b in range(2):
                nc.scalar.activation(VB[:, 2 * b:2 * b + 2, :, :, 0:HD].rearrange("p t b g d -> p t (b g) d"),
                                     bank(b).rearrange("p (t c d) -> p t c d", t=2, c=4), ACT.Copy)\
                    .then_inc(tok_ev, 1)
            for br in range(2):
                q_or_k_hi(bank(4 + br), K[0:HD, 0, br, 0, :], K[HD:P, 1, br, 0, :], 1.0, kb_hi, 1, False)
            nc.scalar.activation(tmp[96:120, :], bank(6)[96:120, :], ACT.Exp, scale=-1.0).then_inc(gb_exp, 1)
            act.wait_ge(kb_lo, 2)
            act.dma_start(K[HD:P, 0, :, :, :].bitcast(F32), K[0:HD, 0, :, :, :].bitcast(F32)).then_inc(kdup[0], 16)
            act.dma_start(K[0:HD, 1, :, :, :].bitcast(F32), K[HD:P, 1, :, :, :].bitcast(F32)).then_inc(kdup[1], 16)

            def hidden_exp(v):
                act.wait_ge(w1_used, 3 * (v + 1))
                if v:
                    act.wait_ge(hs_set, 1)
                nc.scalar.activation(HE, ps[:, 2048:3072].rearrange("p (j n) -> p j n", j=2)[:, :, 0:62], ACT.Exp,
                                     scale=-1.0).then_inc(he_set, 1)

            n = 0
            for s in range(PAIRS + 1):
                for j in range(iters(s)):
                    if s >= 1:
                        probs(n)
                        if n >= LAG_T and evac_on_act(n - LAG_T):
                            evac(n - LAG_T)
                        n += 1
                    for t in ended(s, j, 2):
                        if TILES[t][0] == "k":
                            double_keys(t)
                    for t in ended(s, j, 1):
                        tile_part(t)
                    for u in at_iter(s, j):
                        if u[0] != "gate":
                            split_hi(u)
                    if s == 0 and j == 2:
                        hidden_exp(0)
                    if s == 0 and j == 4:
                        act.wait_ge(cmp2, 1)
                        act.wait_ge(consts_set, 8)
                        src = bank(7)[0:HD, 0:62].rearrange("p (g n) -> p g n", g=2)
                        nc.scalar.activation(KC[0:HD, 0, :, 0:N_CMP], src, ACT.Copy)
                        nc.scalar.activation(KC[HD:P, 0, :, 0:N_CMP], src, ACT.Copy).then_inc(kc_hi, 1)
                    if s == 0 and j == 5:
                        hidden_exp(1)
            for m in range(NU - LAG_T, NU):
                if evac_on_act(m):
                    evac(m)
            for t in range(NT + 1):
                if t < NT:
                    act.wait_ge(ot_tr, t + 1)
                    if t >= 2:
                        act.wait_ge(y_done, t - 1)
                    nc.scalar.activation(OTh[:, t % 2, :, :].rearrange("p k t -> p (k t)"), ps[:, 2048:3072],
                                         ACT.Copy, scale=0.5).then_inc(ot_hi, 1)
                if t >= 1:
                    act.wait_ge(var_set, t)
                    nc.scalar.activation(sdv[:, t - 1:t], mv[:, 1:2], ACT.Sqrt, bias=zero1).then_inc(sd_set, 1)
                    act.wait_ge(nm_set, t)
                    nc.scalar.activation(yt[:, (t - 1) % 2, :], yt[:, (t - 1) % 2, :], ACT.Identity,
                                         bias=nmr[:, t - 1:t], scale=rstd[:, t - 1:t]).then_inc(norm_set, 1)

        @block.vector
        def _(dve):
            steps = [0]

            def link(ins):
                steps[0] += 1
                ins.then_inc(dve_step, 1)
                dve.wait_ge(dve_step, steps[0])

            link(nc.vector.memset(zero1, 0.0))
            dve.wait_ge(pre_tr, 1)
            nc.vector.tensor_copy(trow, ps[0:16, 2048:2048 + TROW]).then_inc(trow_ev, 1)
            dve.wait_ge(pre_tr, 2)
            nc.vector.tensor_copy(ba[:, 0:8], bank(7, 0, 8))
            nc.vector.tensor_scalar(ba[:, 8:16], bank(7, 8, 8), 1.0, None, ALU.add)
            nc.vector.tensor_copy(peT, bank(7, 16, 32)).then_inc(pre_ev, 1)

            def ada_sums(g):
                dve.wait_ge(ada_in[g % 2][0], 32 * (g // 2 + 1))
                if g == 0:
                    dve.wait_ge(small_in, 96)
                if g >= 1:
                    dve.wait_ge(ada_red, g)
                a = acc[:, :].rearrange("p (s f) -> p s f", s=2)
                for k in range(KT):
                    src = ada[:, g % 2, :, k, :]
                    if k == 4:
                        dve.wait_ge(ada_in[g % 2][1], 32 * (g // 2 + 1))
                    if k == 0:
                        ins = nc.vector.tensor_scalar(a, src, cT[:, 0:1], None, ALU.mult)
                    else:
                        ins = nc.vector.scalar_tensor_tensor(out=a, in0=src, scalar=cT[:, k:k + 1], in1=a,
                                                             op0=ALU.mult, op1=ALU.add)
                    if k < KT - 1:
                        link(ins)
                    else:
                        ins.then_inc(ada_acc, 1)

            def shift_scale(g):
                dve.wait_ge(ada_red, g + 1)
                dve.wait_ge(pre_ev, 1)
                sv = ss.rearrange("p (s k) -> p s k", s=2)[:, :, 2 * g:2 * g + 2]
                nc.vector.tensor_tensor(sv, bank(7, 64 + 4 * g, 4).rearrange("p (s k) -> p s k", s=2),
                                        ba.rearrange("p (s k) -> p s k", s=2)[:, :, 2 * g:2 * g + 2],
                                        ALU.add).then_inc(ss_set, 1)

            def h_low(k):
                dve.wait_ge(hhi_set, k + 1)
                link(nc.vector.tensor_scalar(xT[:, k, :], xT[:, k, :], ss[:, 8 + k:9 + k], ss[:, k:k + 1],
                                             ALU.mult, ALU.add))
                nc.vector.tensor_tensor(lov[:, k, :], xT[:, k, :], hiv[:, k, :].bitcast(F32),
                                        ALU.subtract).then_inc(hlo_set, 1)

            for k in range(1, KT, 2):
                dve.wait_ge(x_tr, k + 1)
                nc.vector.tensor_copy(xT[:, k, :], bank(k % 4)).then_inc(xt_dve, 1)
            ada_sums(0)
            for g in range(4):
                shift_scale(g)
                dve.wait_ge(ss_set, g + 1)
                h_low(2 * g)
                h_low(2 * g + 1)
                if g < 3:
                    ada_sums(g + 1)

            def blocks_of(v):
                for par in range(2):
                    for g in range(2):
                        b = ps[HD * g:HD * (g + 1), 512 * (S_BANK + v):512 * (S_BANK + v) + 512]
                        src = bass.AP(b.tensor, b.offset + par, [list(b.ap[0]), [2, 16], [CMP_STRIDE, N_CMP]])
                        pe = peT[HD * par:HD * (par + 1), 16 * v:16 * v + 16].unsqueeze(2)\
                            .to_broadcast([HD, 16, N_CMP])
                        ins = nc.vector.tensor_tensor(bt[HD * par:HD * (par + 1), v, :, N_CMP * g:N_CMP * (g + 1)],
                                                      src, pe, ALU.add)
                ins.then_inc(bt_set, 1)

            def low(dst, src, hi, scale, backwards):
                if backwards:
                    dst, src, hi = blocks(dst), blocks(src)[:, :, ::-1], blocks(hi)
                return nc.vector.scalar_tensor_tensor(out=dst, in0=src, scalar=scale, in1=hi.bitcast(F32),
                                                      op0=ALU.mult, op1=ALU.subtract)

            dve.wait_ge(p1_used, KT)
            blocks_of(0)
            for br in range(2):
                dve.wait_ge(kb_hi, br + 1)
                low(K[0:HD, 0, br, 1, :], bank(4 + br)[0:HD, :], K[0:HD, 0, br, 0, :], 1.0, False)
                low(K[HD:P, 1, br, 1, :], bank(4 + br)[HD:P, :], K[HD:P, 1, br, 0, :], 1.0, False).then_inc(kb_lo, 1)
            blocks_of(1)
            dve.wait_ge(gb_tr, 1)
            link(nc.vector.tensor_scalar(gates, bank(6, 0, 96), 1.0, None, ALU.add))
            link(nc.vector.reciprocal(gates, gates))
            dve.wait_ge(consts_set, 8)
            nc.vector.tensor_tensor(G0, G[:, :, 0, :], cmask.unsqueeze(2).to_broadcast([P, NT, 8]),
                                    ALU.mult).then_inc(g_set, 1)
            dve.wait_ge(g_set, 1)

            def hidden(v):
                dve.wait_ge(he_set, v + 1)
                link(nc.vector.tensor_scalar(HE, HE, 1.0, None, ALU.add))
                link(nc.vector.reciprocal(HE, HE))
                for jj in range(2):
                    hb = bank(T_BANK + jj, 0, 62)
                    if v == 0:
                        ins = nc.vector.tensor_tensor(HS[:, jj, :], hb, HE[:, jj, :], ALU.mult)
                    else:
                        for r in range(2):
                            ins = nc.vector.tensor_tensor(HSV[:, jj, :, r, 0:N_CMP],
                                                          hb.rearrange("p (g n) -> p g n", g=2),
                                                          HE[:, jj, :].rearrange("p (g n) -> p g n", g=2), ALU.mult)
                ins.then_inc(hs_set, 1)

            def tile_part(t):
                kind, c, part = TILES[t]
                src = bank(t % 2)
                if kind != "v":
                    dve.wait_ge(pj_act, act_tiles(t))
                if kind == "z":
                    ev = et[:, 512 * part:512 * part + 512]
                    for m in range(2):
                        dst = Z[:, 2 * part:2 * part + 2, m * 512 + P * c:m * 512 + P * (c + 1)]
                        v = src.rearrange("p (t m d) -> p t m d", t=2, m=2)[:, :, m, :]
                        w = ev.rearrange("p (t m d) -> p t m d", t=2, m=2)[:, :, m, :]
                        ins = nc.vector.scalar_tensor_tensor(out=dst, in0=w, scalar=1.0, in1=v, op0=ALU.add,
                                                             op1=ALU.mult)
                elif kind == "q":
                    low(QS[HD:P, c % 2, 0, :], src[0:HD, :], QS[0:HD, c % 2, 0, :], -HD ** -0.5, True)
                    ins = low(QS[0:HD, c % 2, 1, :], src[HD:P, :], QS[HD:P, c % 2, 1, :], -HD ** -0.5, True)
                elif kind == "k":
                    low(K[0:HD, c % 2, 0, 1, :], src[0:HD, :], K[0:HD, c % 2, 0, 0, :], 1.0, False)
                    ins = low(K[HD:P, c % 2, 1, 1, :], src[HD:P, :], K[HD:P, c % 2, 1, 0, :], 1.0, False)
                else:
                    dve.wait_ge(pj, t + 1)
                    if c == 1:
                        dve.wait_ge(pv_done, UBASE[4])
                    for pp in range(2):
                        ins = nc.vector.tensor_copy(
                            VAv[c][:, pp, 2 * part:2 * part + 2, :, 0:HD],
                            src.rearrange("p (t q h d) -> p t q h d", t=2, q=2, h=2)[:, :, pp, :, :])
                ins.then_inc(pj_dve, 1)

            def logits(n):
                kind, c, h, br, i = UNITS[n]
                dve.wait_ge(qk_done, n + 1)
                if n >= 4:
                    dve.wait_ge(tr_done, n - 3)
                if kind == "cmp":
                    dve.wait_ge(tc_set, c + 1)
                    v = lg[:, 512 * (n % 4):512 * (n % 4) + 256]
                    v3 = v.rearrange("p (q n) -> p q n", n=32)
                    link(nc.vector.tensor_tensor(v, bank(S_BANK + n % 2, 0, 256),
                                                 tc[:, 256 * (c % 2):256 * (c % 2) + 256], ALU.add))
                    link(nc.vector.tensor_reduce(mnc, v3, AX.X, ALU.min))
                    nc.vector.tensor_tensor(v3, v3, mnc.unsqueeze(2).to_broadcast([P, 8, 32]),
                                            ALU.subtract).then_inc(lg_set, 1)
                else:
                    w = P * (i + 1)
                    if h == 0 and br == 0 and i == 0:
                        dve.wait_ge(t_in[c % 2], 16 * (c // 2 + 1))
                    nc.vector.tensor_tensor_reduce(out=lg[:, 512 * (n % 4):512 * (n % 4) + w],
                                                   in0=bank(S_BANK + n % 2, 0, w),
                                                   in1=T[:, c % 2, h, SEQ - w:SEQ], scale=1.0, scalar=3e38,
                                                   op0=ALU.add, op1=ALU.min,
                                                   accum_out=mn[:, n % 8:n % 8 + 1]).then_inc(lg_set, 1)

            def cmp_norm(n):
                dve.wait_ge(ex_set, n + 1)
                v3 = lg[:, 512 * (n % 4):512 * (n % 4) + 256].rearrange("p (q n) -> p q n", n=32)
                link(nc.vector.tensor_reduce(rcc, v3, AX.X, ALU.add))
                link(nc.vector.reciprocal(rcc, rcc))
                nc.vector.tensor_tensor(v3, v3, rcc.unsqueeze(2).to_broadcast([P, 8, 32]),
                                        ALU.mult).then_inc(cn_set, 1)

            def evac(n):
                kind, c, h, br, i = UNITS[n]
                dve.wait_ge(tr_done, n + 1)
                if n >= 2:
                    dve.wait_ge(pv_done, n - 1)
                w = P * (i + 1)
                nc.vector.tensor_copy(pt[:, 512 * (n % 2):512 * (n % 2) + w], bank(T_BANK + n % 2, 0, w))\
                    .then_inc(ev_dve, 1)

            def group_end(n):
                kind, c, h, br, i = UNITS[n]
                dve.wait_ge(pv_done, n + 1)
                b = bank(O_BANK + GROUP[n] % 2)
                if kind == "cmp":
                    o = OS[:, :, D // 2 + P * c:D // 2 + P * (c + 1)].rearrange("p t (h d) -> p t h d", h=2)
                    nc.vector.tensor_tensor(o, b.rearrange("p (t h d) -> p t h d", t=NT, h=2),
                                            G0[:, :, 2 * c:2 * c + 2].unsqueeze(3).to_broadcast([P, NT, 2, HD]),
                                            ALU.mult).then_inc(og_set, 1)
                    return
                o = b[:, 0:NT * 65].rearrange("p (t d) -> p t d", t=NT)
                rc = rcs[:, 8 * (GROUP[n] % 2):8 * (GROUP[n] % 2) + 8]
                link(nc.vector.reciprocal(rc[:, 0:NT].unsqueeze(2), o[:, :, HD:HD + 1]))
                if c < 4:
                    link(nc.vector.tensor_tensor(rc[:, 4:8], rc[:, 0:4], G[:, :, 1 + br, 2 * c + h], ALU.mult))
                    if adds[0] >= 2:
                        dve.wait_ge(add_done, adds[0] - 1)
                    dst = tmp[:, 256 * (adds[0] % 2):256 * (adds[0] % 2) + 256].rearrange("p (t d) -> p t d", t=NT)
                    adds[0] += 1
                    r = rc[:, 4:8]
                else:
                    dst = OS[:, :, P * (c - 4) + HD * h:P * (c - 4) + HD * (h + 1)]
                    r = rc[:, 0:4]
                nc.vector.tensor_tensor(dst, o[:, :, 0:HD], r.unsqueeze(2).to_broadcast([P, NT, HD]),
                                        ALU.mult).then_inc(og_set, 1)

            def gate_sums(u):
                src = raw_landed(dve, u)[:, 0:D]
                k = u[1]
                if k == 0:
                    ins = nc.vector.tensor_scalar(gacc[:, :], src, cT[:, 0:1], None, ALU.mult)
                else:
                    dve.wait_ge(gate_used, k)
                    ins = nc.vector.scalar_tensor_tensor(out=gacc[:, :], in0=src, scalar=cT[:, k:k + 1],
                                                         in1=gacc[:, :], op0=ALU.mult, op1=ALU.add)
                ins.then_inc(gate_used, 1)

            adds = [0]
            n = 0
            for s in range(PAIRS + 1):
                for j in range(iters(s)):
                    if s >= 1:
                        logits(n)
                        if n >= 1 and UNITS[n - 1][0] == "cmp":
                            cmp_norm(n - 1)
                        if n >= LAG_T and not evac_on_act(n - LAG_T):
                            evac(n - LAG_T)
                        if n > LAG_V and group_last(n - LAG_V - 1):
                            group_end(n - LAG_V - 1)
                        n += 1
                    for t in ended(s, j, 1):
                        tile_part(t)
                    for u in at_iter(s, j):
                        if u[0] == "gate":
                            gate_sums(u)
                    if s == 0 and j == 2:
                        hidden(0)
                    if s == 0 and j == 4:
                        dve.wait_ge(kc_hi, 1)
                        src = bank(7)[0:HD, 0:62].rearrange("p (g n) -> p g n", g=2)
                        for half in (0, HD):
                            ins = nc.vector.scalar_tensor_tensor(
                                out=KC[half:half + HD, 1, :, 0:N_CMP], in0=src, scalar=1.0,
                                in1=KC[0:HD, 0, :, 0:N_CMP].bitcast(F32), op0=ALU.mult, op1=ALU.subtract)
                        ins.then_inc(cmp_set, 1)
                    if s == 0 and j == 5:
                        hidden(1)
                        dve.wait_ge(cmp2, 2)
                        for g in range(2):
                            for r in range(2):
                                ins = nc.vector.tensor_copy(vc[32 * r:32 * r + 32, P * g + HD * r:P * g + HD * r + HD],
                                                            bank(6)[32 * r:32 * r + 32, HD * g:HD * g + HD])
                        ins.then_inc(cmp_set, 1)
            for m in range(NU - LAG_T, NU):
                if not evac_on_act(m):
                    evac(m)
            for m in range(NU - LAG_V - 1, NU):
                if group_last(m):
                    group_end(m)
            dve.wait_ge(ln_in, 48)
            dve.wait_ge(grow, 1)
            nc.vector.scalar_tensor_tensor(out=et[:, :], in0=ps[:, 0:1024], scalar=1.0, in1=bgate, op0=ALU.add,
                                           op1=ALU.add).then_inc(g1_set, 1)
            dve.wait_ge(g1_set, 1)
            for t in range(NT + 1):
                if t < NT:
                    dve.wait_ge(ot_hi, t + 1)
                    nc.vector.scalar_tensor_tensor(
                        out=OTl[:, t % 2, :, :].rearrange("p k t -> p (k t)"), in0=ps[:, 2048:3072], scalar=0.5,
                        in1=OTh[:, t % 2, :, :].rearrange("p k t -> p (k t)").bitcast(F32), op0=ALU.mult,
                        op1=ALU.subtract).then_inc(ot_lo, 1)
                if t >= 1:
                    q = t - 1
                    y = yt[:, q % 2, :]
                    dve.wait_ge(y_done, t)
                    if q >= 2:
                        dve.wait_ge(out_done[q % 2], 16)
                    yb = ps[:, 1024 * (q % 2):1024 * (q % 2) + 1024]
                    nc.vector.tensor_tensor(y, yb, et[:, :], ALU.mult).then_inc(y_read, 1)
                    dve.wait_ge(y_read, t)
                    dve.wait_ge(res_in[q % 2], 16 * (q // 2 + 1))
                    link(nc.vector.scalar_tensor_tensor(out=y, in0=xr[:, q % 2, :], scalar=ALPHA, in1=y,
                                                        op0=ALU.mult, op1=ALU.add))
                    nc.vector.bn_stats(st[:, 0:6], y[:, 0:512])
                    link(nc.vector.bn_stats(st[:, 6:12], y[:, 512:1024]))
                    link(nc.vector.bn_aggr(mv, st))
                    nc.vector.tensor_scalar(mv[:, 1:2], mv[:, 1:2], LN_EPS, None, ALU.add).then_inc(var_set, 1)
                    dve.wait_ge(sd_set, t)
                    link(nc.vector.reciprocal(rstd[:, q:q + 1], sdv[:, q:q + 1]))
                    nc.vector.scalar_tensor_tensor(out=nmr[:, q:q + 1], in0=mv[:, 0:1], scalar=-1.0,
                                                   in1=rstd[:, q:q + 1], op0=ALU.mult, op1=ALU.mult)\
                        .then_inc(nm_set, 1)
                    dve.wait_ge(nm_set, t)

        @block.tensor
        def _(pe):
            mm = nc.tensor.matmul
            pe.wait_ge(small_in, 96)
            mm(ps[0:16, 2048:2048 + 512], rel, onehot[:, 0:512], start=True, stop=True)
            mm(ps[0:16, 2560:2560 + TROW - 512], rel, onehot[:, 512:TROW], start=True, stop=True).then_inc(pre_tr, 1)
            pe.wait_ge(consts_set, 1)
            nc.tensor.transpose(bank(7, 0, 16), ba_row, ident[0:16, 0:16])
            nc.tensor.transpose(bank(7, 16, 32), pe_row, ident[0:32, 0:32]).then_inc(pre_tr, 1)
            for k in range(KT):
                if k % 4 == 0:
                    pe.wait_ge(x_in[k // 4], 16)
                if k >= 4:
                    m = k - 4
                    pe.wait_ge(xt_dve if m % 2 else xt_act, m // 2 + 1)
                for t in range(NT):
                    ins = nc.tensor.transpose(bank(k % 4, P * t, P), x_tok[:, t, P * k:P * (k + 1)], ident[:, :])
                ins.then_inc(x_tr, 1)

            def three(dst, ah, al, bh, bl, start, stop, shared=False):
                mm(dst, ah, bh, start=start, stop=False, skip_group_check=shared)
                mm(dst, ah, bl, start=False, stop=False, skip_group_check=shared)
                return mm(dst, al, bh, start=False, stop=stop, skip_group_check=shared)

            def col(w, k, a, b):
                return w[:, k * W1ST + a:k * W1ST + b]

            def v_cols(w, k):
                a = w[:, k * W1ST + 3 * P:k * W1ST + 4 * P]
                return bass.AP(a.tensor, a.offset, [list(a.ap[0]), [2 * P, 2], [1, P]])

            def ada_total(g):
                pe.wait_ge(ada_acc, g + 1)
                if g >= 1:
                    pe.wait_ge(ss_set, g)
                for q in range(4):
                    s, e = q // 2, q % 2
                    ins = mm(bank(7, 64 + 4 * g + q, 1), acc[:, 256 * s + P * e:256 * s + P * (e + 1)],
                             ones[:, 0:1], start=True, stop=True)
                ins.then_inc(ada_red, 1)

            pe.wait_ge(pre_ev, 1)
            ada_total(0)
            pe.wait_ge(xt_act, 4)
            pe.wait_ge(xt_dve, 4)
            pe.wait_ge(trow_ev, 1)
            for g in range(4):
                pe.wait_ge(hi_set, g + 1)
                pe.wait_ge(lo_set, g + 1)
                for k in (2 * g, 2 * g + 1):
                    pe.wait_ge(hhi_set, k + 1)
                    pe.wait_ge(hlo_set, k + 1)
                    last = k == KT - 1
                    for b, a in ((2, 0), (3, 128), (4, 256), (5, 512)):
                        three(bank(b), col(w_hi, k, a, a + P), col(w_lo, k, a, a + P), hiv[:, k, :], lov[:, k, :],
                              k == 0, last)
                    if k % 2 and g < 3:
                        ada_total(g + 1)
                    for t in range(NT):
                        three(bank(t // 2, 256 * (t % 2), 256), hiv[:, k, P * t:P * (t + 1)],
                              lov[:, k, P * t:P * (t + 1)], v_cols(w_hi, k), v_cols(w_lo, k),
                              k == 0 and t % 2 == 0, last, True)
                    three(bank(6)[0:120, :], col(w_hi, k, W1ST - 120, W1ST), col(w_lo, k, W1ST - 120, W1ST),
                          hiv[:, k, :], lov[:, k, :], k == 0, last).then_inc(p1_used, 1)

            def gates_by_token():
                pe.wait_ge(gb_exp, 1)
                for t in range(NT):
                    ins = nc.tensor.transpose(bank(6, 24 * t, 24), tmp[96:120, P * t:P * (t + 1)],
                                              ident[96:120, 96:120])
                ins.then_inc(gb_tr, 1)

            def tile_range(t, lo, hi):
                c, e = t // 3, t % 3
                by_token = TILES[t][0] in "zv"
                part = TILES[t][2]
                groups = [(tt, k) for tt in range(2 * part, 2 * part + 2) for k in range(KT)] if by_token else \
                    [(0, k) for k in range(KT)]
                n = len(groups)
                for m, (tt, k) in enumerate(groups):
                    if not lo <= m / n < hi:
                        continue
                    if m == 0:
                        if t < 2:
                            pe.wait_ge(tok_ev, t + 1)
                        else:
                            pe.wait_ge(pj_dve, t - 1)
                    if e == 0 and k % 4 == 0:
                        pe.wait_ge(hi_set, 4 + 2 * c + k // 4 + 1)
                        pe.wait_ge(lo_set, 4 + 2 * c + k // 4 + 1)
                    if not by_token:
                        ins = three(bank(t % 2), chunk(w_hi, c, k, P * e, P * e + P),
                                    chunk(w_lo, c, k, P * e, P * e + P), hiv[:, k, :], lov[:, k, :],
                                    k == 0, k == KT - 1)
                    else:
                        ins = three(bank(t % 2, 256 * (tt % 2), 256), hiv[:, k, P * tt:P * (tt + 1)],
                                    lov[:, k, P * tt:P * (tt + 1)], chunk(w_hi, c, k, P, 3 * P),
                                    chunk(w_lo, c, k, P, 3 * P), k == 0, k == KT - 1)
                    if m == n - 1:
                        ins.then_inc(pj, 1)

            def project(s, j):
                a, b = quantum(s, j)
                for e in range(3):
                    lo, hi = a - e, b - e
                    if hi > 0 and lo < 1:
                        tile_range(3 * s + e, lo, hi)

            def compress1(v, part):
                src = raw_landed(pe, ("w1", v, part))
                if part == 0:
                    pe.wait_ge(bt_set, v + 1)
                    if v == 0:
                        pe.wait_ge(kb_lo, 2)
                    else:
                        pe.wait_ge(hs_set, 1)
                k0, k1 = W1PARTS[part]
                for k in range(k0, k1):
                    for jj in range(2):
                        o = (k - k0) * CMP_HID + P * jj
                        ins = mm(bank(T_BANK + jj, 0, 62), src[:, o:o + P], bt[:, v, k, :], start=k == 0, stop=k == 15)
                ins.then_inc(w1_used, 1)

            def compress2(v):
                pe.wait_ge(hs_set, v + 1)
                if v == 0:
                    pe.wait_ge(w2_in, 16)
                    pe.wait_ge(ss_set, 4)
                    for jj in range(2):
                        ins = mm(bank(7)[0:HD, 0:62], W2[:, 0, jj, :], HS[:, jj, :], start=jj == 0, stop=jj == 1)
                else:
                    pe.wait_ge(g_set, 1)
                    for g in range(2):
                        for jj in range(2):
                            ins = mm(bank(6)[0:HD, HD * g:HD * (g + 1)],
                                     HSV[:, jj, g, :, :].rearrange("p r n -> p (r n)"), W2[:, 1, jj, :],
                                     start=jj == 0, stop=jj == 1)
                ins.then_inc(cmp2, 1)

            def scores(n):
                kind, c, h, br, i = UNITS[n]
                if n < 2:
                    pe.wait_ge(bt_set, 2)
                else:
                    pe.wait_ge(lg_set, n - 1)
                if n == UBASE[c]:
                    pe.wait_ge(pj_dve, TILE["q", c, 0] + 1)
                    if c < 4:
                        pe.wait_ge(cmp_set, 1)
                    pe.wait_ge(kdup[c // 2 if c < 4 else c % 2], 16 if c < 4 else 16 + 32 * (c // 2 - 1))
                b = S_BANK + n % 2
                if kind == "cmp":
                    for i in range(NT):
                        for h in range(2):
                            qt = QS[:, c % 2, h, P * i:P * (i + 1)]
                            o = bank(b, (2 * i + h) * 32, 32)
                            mm(o, qt, KC[:, 0, c // 2, :], start=True, stop=False)
                            ins = mm(o, qt, KC[:, 1, c // 2, :], start=False, stop=True)
                else:
                    w = P * (i + 1)
                    qt = QS[:, c % 2, h, P * i:P * (i + 1)]
                    sl, a = (c // 2, br) if c < 4 else (c % 2, h)
                    mm(bank(b, 0, w), qt, K[:, sl, a, 0, 0:w], start=True, stop=False)
                    ins = mm(bank(b, 0, w), qt, K[:, sl, a, 1, 0:w], start=False, stop=True)
                ins.then_inc(qk_done, 1)

            def turn(n):
                kind, c, h, br, i = UNITS[n]
                if kind == "cmp":
                    pe.wait_ge(cn_set, c + 1)
                else:
                    pe.wait_ge(ex_set, n + 1)
                if n < 2:
                    pe.wait_ge(hs_set, 2)
                else:
                    evacuated(pe, n - 2)
                src = lg[:, 512 * (n % 4):512 * (n % 4) + 512]
                b = T_BANK + n % 2
                if kind == "cmp":
                    for i in range(NT):
                        ins = nc.tensor.transpose(bank(b, P * i, P)[0:HD, :], src[:, HD * i:HD * (i + 1)], flip[:, :])
                else:
                    for m in range(i + 1):
                        ins = nc.tensor.transpose(bank(b, P * m, P), src[:, P * m:P * (m + 1)], flip[:, :])
                ins.then_inc(tr_done, 1)

            def values(n):
                kind, c, h, br, i = UNITS[n]
                evacuated(pe, n)
                gi = GROUP[n]
                if n == 0 or GROUP[n - 1] != gi:
                    pe.wait_ge(cmp_set, 2)
                    pe.wait_ge(tok_ev, 2)
                    if c >= 4:
                        pe.wait_ge(pj_dve, TILE["v", c // 2 - 2, 1] + 1)
                    if gi >= 2:
                        pe.wait_ge(og_set, gi - 1)
                b = O_BANK + gi % 2
                src = pt[:, 512 * (n % 2):512 * (n % 2) + 512]
                if kind == "cmp":
                    for i in range(NT):
                        ins = mm(bank(b, P * i, P), src[0:HD, P * i:P * (i + 1)], vc[:, P * (c // 2):P * (c // 2 + 1)],
                                 start=True, stop=True)
                else:
                    for m in range(i + 1):
                        v = VB[:, m, br, c // 2, :] if c < 4 else VAv[c // 2 - 2][:, c % 2, m, h, :]
                        ins = mm(bank(b, 65 * i, 65), src[:, P * m:P * (m + 1)], v, start=m == 0, stop=m == i)
                ins.then_inc(pv_done, 1)

            pe.wait_ge(flip_set, 1)
            gates_by_token()
            n = 0
            for s in range(PAIRS + 1):
                for j in range(iters(s)):
                    if s >= 1:
                        scores(n)
                    if s < PAIRS:
                        project(s, j)
                    if s == 0:
                        compress1(j // 3, j % 3)
                        if j == 3:
                            compress2(0)
                        if j == 5:
                            compress2(1)
                    else:
                        if s == PAIRS and j == 2:
                            pe.wait_ge(gate_used, KT)
                            pe.wait_ge(pj_dve, 24)
                            mm(bank(0), ones[:, :], gacc[:, 0:512], start=True, stop=True)
                            mm(bank(1), ones[:, :], gacc[:, 512:1024], start=True, stop=True).then_inc(grow, 1)
                        if n >= LAG_T:
                            turn(n - LAG_T)
                        if n >= LAG_V:
                            values(n - LAG_V)
                        n += 1
            for n in range(NU, NU + LAG_V):
                if n - LAG_T < NU:
                    turn(n - LAG_T)
                values(n - LAG_V)
            pe.wait_ge(gated, PAIRS)
            pe.wait_ge(hi_set, 28)
            pe.wait_ge(lo_set, 28)

            def turn_out(t):
                if t == 0:
                    evacuated(pe, NU - 1)
                    evacuated(pe, NU - 2)
                else:
                    pe.wait_ge(ot_hi, t)
                    pe.wait_ge(ot_lo, t)
                for k in range(KT):
                    ins = nc.tensor.transpose(bank(T_BANK + k // 4, P * (k % 4), P), OS[:, t, P * k:P * (k + 1)],
                                              ident[:, :])
                ins.then_inc(ot_tr, 1)

            turn_out(0)
            for t in range(NT):
                pe.wait_ge(ot_hi, t + 1)
                pe.wait_ge(ot_lo, t + 1)
                if t + 1 < NT:
                    turn_out(t + 1)
                if t == 0:
                    pe.wait_ge(g1_set, 1)
                if t >= 2:
                    pe.wait_ge(y_read, t - 1)
                for k in range(KT):
                    oh, ol = OTh[:, t % 2, k, :], OTl[:, t % 2, k, :]
                    for half in range(2):
                        b = bank(2 * (t % 2) + half)
                        wh = wo_at(w_hi, k)[:, 512 * half:512 * (half + 1)]
                        wl = wo_at(w_lo, k)[:, 512 * half:512 * (half + 1)]
                        ins = three(b, oh, ol, wh, wl, k == 0, k == KT - 1)
                ins.then_inc(y_done, 1)


def blocks(ap):
    return ap.rearrange("p (i t) -> p i t", t=P)


def shape_constants():
    k = np.arange(TROW)
    d = SEQ - 1 - k
    dm = np.maximum(d, 1)
    exact = N_B // 2
    large = exact + (np.log(dm.astype(np.float32) / np.float32(exact)) / np.log(MAX_DIST / exact)
                     * (N_B - exact)).astype(np.int32)
    bucket = np.where(d < exact, np.maximum(d, 0), np.minimum(large, N_B - 1))
    t = np.zeros((N_B + 2, TROW + 16), np.float32)
    t[bucket, k] = -1.0
    seen = sum(((d >= 0) & (d <= w) & (d % dil == 0)).astype(np.int64) for w, dil in DILATED)
    t[N_B, :TROW] = np.where(seen > 0, -np.log(np.maximum(seen, 1)), BIG)
    t[N_B + 1, :TROW] = np.where(d >= 0, 0.0, BIG)
    t[N_B, TROW:TROW + H_A] = 1.0
    t[N_B + 1, TROW + H_A:] = 1.0
    return t


def kernel(**inputs):
    import concourse.bacc as bacc
    from concourse.bass_utils import run_bass_kernel_spmd

    nc = bacc.Bacc("TRN2", target_bir_lowering=False, num_devices=1)
    arrays, aps = {}, {}
    for name in ("x", "c", "w_in", "w_out", "cmp_pe", "cmp_w1", "cmp_w2", "w_ada", "b_ada", "ln_g", "ln_b", "rel_bias"):
        a = np.ascontiguousarray(inputs[name])
        if name in ("w_in", "w_out", "cmp_pe", "cmp_w1", "cmp_w2", "w_ada"):
            a = a[0]
        arrays["in_" + name] = a
        aps[name] = nc.dram_tensor("in_" + name, a.shape, F32, kind="ExternalInput").ap()
    arrays["in_consts"] = shape_constants()
    consts = nc.dram_tensor("in_consts", arrays["in_consts"].shape, F32, kind="ExternalInput").ap()
    scratch = nc.dram_tensor("bias_rows", (16, TROW), F32, kind="Internal").ap()
    out = nc.dram_tensor("out", (1, SEQ, D), F32, kind="ExternalOutput").ap()
    build(nc, aps["x"], aps["c"], aps["w_in"], aps["w_out"], aps["cmp_pe"], aps["cmp_w1"], aps["cmp_w2"],
          aps["w_ada"], aps["b_ada"], aps["ln_g"], aps["ln_b"], aps["rel_bias"], consts, scratch, out)
    r = run_bass_kernel_spmd(nc, [arrays], core_ids=[0])
    return r.results[0]["out"]
```

```python
from contextlib import ExitStack

import numpy as np

import concourse.bass as bass
from concourse import mybir

F32 = mybir.dt.float32
F32R = mybir.dt.float32r
ACT = mybir.ActivationFunctionType
ALU = mybir.AluOpType
AX = mybir.AxisListType

P = 128
SEQ = 512
D = 1024
NT = SEQ // P
KT = D // P
HD = 64
H_A = H_B = 8
N_B = 32
MAX_DIST = 2048
DILATED = ((128, 1), (512, 4), (2048, 16))
CMP_LEN, CMP_STRIDE, CMP_HID = 32, 16, 256
N_CMP = SEQ // CMP_STRIDE - 1
ALPHA = 2.0 ** 0.25
LN_EPS = 1e-5
BIG = 1e30

QA, KA, VA, ZA, QB, KVB, GB, ZB = 0, 512, 1024, 1536, 2048, 2560, 3328, 3352
W1ST = GB + 24 - KVB
PIECES = ((0, 0, 3 * P), (4 * P, 3 * P, P), (3 * P, 4 * P, P), (5 * P, 5 * P, W1ST - 5 * P))
TOK_BANK = (0, 1, 6, 7)
PAIRS = 8
CW = 384
RAWC = 2 * W1ST
NRAW = 3
STORES = (2, 0, 1, 3)
DVE_LAST = (2, 1, 3)
POOL_COLS = (D, 384)
TROW = 640


CHUNKS = (
    ((QB, ZA, ZB), (("q", 0, 0), ("z", 0, 0), ("z", 0, 1))),
    ((QB + P, ZA + P, ZB + P), (("q", 1, 0), ("z", 1, 0), ("z", 1, 1))),
    ((QB + 2 * P, ZA + 2 * P, ZB + 2 * P), (("q", 2, 0), ("z", 2, 0), ("z", 2, 1))),
    ((QB + 3 * P, VA, VA + P), (("q", 3, 0), ("v", 0, 0), ("v", 0, 1))),
    ((KA, QA, KA + P), (("k", 4, 0), ("q", 4, 0), ("k", 5, 0))),
    ((QA + P, VA + 2 * P, VA + 3 * P), (("q", 5, 0), ("v", 1, 0), ("v", 1, 1))),
    ((KA + 2 * P, QA + 2 * P, KA + 3 * P), (("k", 6, 0), ("q", 6, 0), ("k", 7, 0))),
    ((QA + 3 * P, ZA + 3 * P, ZB + 3 * P), (("q", 7, 0), ("z", 3, 0), ("z", 3, 1))),
)
TILES = [t for _, ts in CHUNKS for t in ts]
TILE = {t: n for n, t in enumerate(TILES)}


def units_of(c):
    if c < 4:
        return [("cmp", c, 0, 0, 0)] + [("att", c, h, br, i) for h in range(2) for br in range(2) for i in range(NT)]
    return [("att", c, h, 0, i) for h in range(2) for i in range(NT)]


LAG_T = 3
LAG_V = 5
N_PT = 3
UNITS = [u for c in range(PAIRS) for u in units_of(c)]
NU = len(UNITS)
UBASE = [sum(len(units_of(b)) for b in range(c)) for c in range(PAIRS + 1)]
GROUP = []
for _n, _u in enumerate(UNITS):
    GROUP.append(0 if _n == 0 else GROUP[-1] + (_u[0] == "cmp" or _u[4] == 0))


def evac_on_act(n):
    return UNITS[n][0] == "cmp" or UNITS[n][4] in (0, 3)


def group_last(m):
    return m + 1 == NU or GROUP[m + 1] != GROUP[m]


def evacs(n, on_act):
    return sum(evac_on_act(m) == on_act for m in range(n + 1))


def iters(s):
    return 6 if s == 0 else len(units_of(s - 1))


def quantum(s, j):
    return 3 * j / iters(s), 3 * (j + 1) / iters(s)


def ended(s, j, lag):
    j -= lag
    while j < 0:
        s -= 1
        if s < 0:
            return []
        j += iters(s)
    if s >= PAIRS:
        return []
    a, b = quantum(s, j)
    return [3 * s + e for e in range(3) if a <= e + 1 - 1e-3 < b]


WO = (4, 5, 6, 0, 1, 7, 2, 3)
N_EARLY = 5
SCALE_AT = {(7, 0): 0, (7, 2): 1, (7, 3): 2, (7, 5): 3, (7, 6): 4, (8, 1): 5, (8, 2): 6, (8, 4): 7}
OUT_PAIRS = (0, 1, 2, 4, 5, 3, 6, 7)
SPARE = {(4, 7): ("gate", 0), (4, 11): ("gate", 1), (5, 2): ("out", 0), (5, 6): ("out", 1), (6, 2): ("out", 2),
         (6, 7): ("out", 3), (7, 7): ("out", 4), (8, 3): ("out", 5), (8, 7): ("out", 6)}
AFTER = {(s, j + 1) if j + 1 < iters(s) else (s + 1, 0): v for (s, j), v in SPARE.items()}


def plan(s):
    n = iters(s)
    if s == 0:
        return [(1, ("ch", 1, 0)), (4, ("ch", 1, 1))]
    if s <= 6:
        p = [(n // 4, ("ch", s + 1, 0)), (3 * n // 4, ("ch", s + 1, 1))]
        if s <= 3:
            p += [(n // 4 + 2 + 3 * m, ("gate", 3 * (s - 1) + m, 0)) for m in range(3)]
        return sorted(p)
    if s == 7:
        return [(1 + 2 * q, ("wo", q, 0)) for q in range(3)]
    return [(0, ("wo", 3, 0)), (0, ("wo", 4, 0)), (2, ("wo", 5, 0)), (3, ("wo", 6, 0)), (5, ("wo", 7, 0))]


def at_iter(s, j):
    return [u for k, u in plan(s) if k == j]


RAW = [("p1", g, 0) for g in range(4)] + [("ch", 0, 0), ("ch", 0, 1)]
RAW += [("w1", 0, 0), ("w1", 0, 1), ("ch", 1, 0), ("w1", 0, 2), ("w1", 1, 0), ("ch", 1, 1), ("w1", 1, 1), ("w1", 1, 2)]
RAW += [u for s in range(1, PAIRS + 1) for _, u in plan(s)]
RAWI = {u: n for n, u in enumerate(RAW)}
RAWD = {"p1": len(PIECES), "ch": 3, "w1": 1, "gate": 1, "wo": 1}
W1PARTS = ((0, 6), (6, 12), (12, 16))


def raw_count(n):
    return sum(16 * RAWD[RAW[m][0]] for m in range(n % NRAW, n + 1, NRAW))


def split_no(u):
    return {"ch": 2 * u[1] + u[2], "wo": 2 * PAIRS + u[1]}[u[0]]


def build(nc, x, c_in, w_in, w_out, cmp_pe, cmp_w1, cmp_w2, w_ada, b_ada, ln_g, ln_b, rel_bias, consts, scratch, out):
    with ExitStack() as ctx:
        def sb(name, cols, dt=F32, parts=P):
            return ctx.enter_context(nc.sbuf_tensor(name, [parts, cols], dt))

        def sem(name):
            return ctx.enter_context(nc.semaphore(name))

        with nc.sbuf_tensor("x_tok", [P, 2 * KT * W1ST], F32) as x_tok_t:
            x_tok = [x_tok_t[:, (h + 1) * KT * W1ST - NT * 512:(h + 1) * KT * W1ST]
                     .rearrange("p (t d) -> p t d", t=NT) for h in range(2)]
        w_hi = sb("w_hi", KT * W1ST, F32R)
        w_lo = sb("w_lo", KT * W1ST, F32R)
        raw = sb("raw", NRAW * RAWC)
        with nc.sbuf_tensor("y_rows", [P, 2 * NT * D], F32) as y_rows:
            pass
        h_hi = sb("h_hi", KT * SEQ, F32R)
        h_lo = sb("h_lo", KT * SEQ, F32R)
        with nc.sbuf_tensor("ada", [P, 2 * 4096], F32) as ada_t:
            ada = ada_t[:, :].rearrange("p (b s k f) -> p b s k f", b=2, s=2, k=KT)
        with nc.sbuf_tensor("z", [P, NT * D], F32) as z:
            pass
        ot_l = sb("ot_l", NT * D, F32R)
        kk = sb("kk", 4096, F32R)
        qs = sb("qs", 2048, F32R)
        vb = sb("vb", NT * 4 * 65)
        va = sb("va", 2 * NT * 2 * 65)
        tb_ = sb("tb", 2048)
        lg = sb("lg", 2048)
        pt = sb("pt", N_PT * 512)
        with nc.sbuf_tensor("os", [P, NT * D], F32) as os_:
            pass
        ot_h = sb("ot_h", NT * D, F32R)
        gacc = sb("gacc", D)
        et = sb("et", 1024)
        tmp = sb("tmp", 512)
        tc = sb("tc", 512)
        w2 = sb("w2", 256)
        hs = sb("hs", 2 * 62)
        hsv = sb("hsv", 2 * 2 * 64)
        he = sb("he", 2 * 62)
        kc = sb("kc", 2 * 2 * 32, F32R)
        vc = sb("vc", 2 * P, parts=64)
        acc = sb("acc", 512)
        ident = sb("ident", P)
        flip = sb("flip", P)
        ones = sb("ones", P)
        small = sb("small", 320)
        cT = small[:, 0:8]
        ba = small[:, 8:24]
        ss = small[:, 24:40]
        peT = small[:, 40:72]
        mn = small[:, 72:80]
        mnc = small[:, 80:88]
        rcc = small[:, 88:96]
        rcs = small[:, 272:288]
        gates = small[:, 104:200]
        cmask = small[:, 200:204]
        g0 = small[:, 204:236]
        ysum = small[:, 236:240]
        nmean = small[:, 240:244]
        sq = small[:, 244:248]
        rstd = small[:, 250:254]
        nmr = small[:, 254:258]
        sdv = small[:, 258:262]
        eps = small[:, 263:264]
        vrow = gacc[:, :]

        hiv = h_hi[:, :].rearrange("p (k t) -> p k t", k=KT)
        lov = h_lo[:, :].rearrange("p (k t) -> p k t", k=KT)
        xT = os_[:, :].rearrange("p (k t) -> p k t", k=KT)
        bt = os_[:, 0:2 * 16 * 62].rearrange("p (v k n) -> p v k n", v=2, k=16)
        OS = os_[:, :].rearrange("p (t d) -> p t d", t=NT)
        Z = z[:, :].rearrange("p (t d) -> p t d", t=NT)
        K = kk[:, :].rearrange("p (s a l t) -> p s a l t", s=2, a=2, l=2)
        QS = qs[:, :].rearrange("p (s h t) -> p s h t", s=2, h=2)
        VB = vb[:, :].rearrange("p (t b g d) -> p t b g d", t=NT, b=2, g=2)
        VAv = [w[:, :].rearrange("p (s t h d) -> p s t h d", s=2, t=NT, h=2) for w in (va, vb)]
        T = tb_[:, :].rearrange("p (s h x) -> p s h x", s=2, h=2)
        Tc = tc[:, :].rearrange("p (s i h n) -> p s i h n", s=2, i=NT, h=2)
        KC = kc[:, :].rearrange("p (l g n) -> p l g n", l=2, g=2)
        W2 = w2[:, :].rearrange("p (v j d) -> p v j d", v=2, j=2)
        HS = hs[:, :].rearrange("p (j n) -> p j n", j=2)
        HSV = hsv[:, :].rearrange("p (j g r n) -> p j g r n", j=2, g=2, r=2)
        HE = he[:, :].rearrange("p (j n) -> p j n", j=2)
        G = gates.rearrange("p (t b h) -> p t b h", t=NT, b=3)
        G0 = g0.rearrange("p (t h) -> p t h", t=NT)
        onehot, rel = lg[0:34, 0:TROW], lg[0:34, TROW:TROW + 16]
        trow = lg[0:16, 704:704 + TROW]
        ba_row, pe_row = lg[0:16, 1344:1472], lg[0:32, 1472:1600]
        OTh = ot_h[:, :].rearrange("p (t d) -> p t d", t=NT)
        OTl = ot_l[:, :].rearrange("p (t d) -> p t d", t=NT)
        lng, lnb = raw[:, 0:D], raw[:, D:2 * D]

        def out_tile(pair):
            return pair - 4 if pair >= 4 else pair + 4

        def rows(t):
            o = (2 + t % 2 + 4 * (t // 2)) * D
            return y_rows[:, o:o + D]

        def slot(n):
            return raw[:, (n % NRAW) * RAWC:(n % NRAW + 1) * RAWC]

        def split_at(w, u):
            kind, a, b = u
            if kind == "ch":
                o = (a % 2) * KT * CW + b * 4 * CW
                return w[:, o:o + 4 * CW]
            return wo_at(w, a)

        def wo_at(w, k):
            if k < 6:
                return w[:, k * D:(k + 1) * D]
            hx = h_hi if w is w_hi else h_lo
            return hx[:, (k - 6) * D:(k - 5) * D]

        def width(u):
            return {"ch": 4 * CW, "wo": D}[u[0]]

        def chunk(w, c, k, a, b):
            o = (c % 2) * KT * CW + k * CW
            return w[:, o + a:o + b]

        ps = ctx.enter_context(nc.psum_tensor("ps", [P, 4096], F32))

        def bank(b, a=0, n=512):
            return ps[:, 512 * b + a:512 * b + a + n]

        S_BANK, T_BANK, O_BANK = 2, 4, 6
        HID_BANK = (6, 2)
        CMP_BANK = (4, 5)
        LATE_BANK = (2, 0, 4, 6)
        EARLY_EV = {2: (1,), **{j: (j - 1,) for j in range(3, 2 * NT)}}

        def x_bank(k):
            return (2, 3, 4, 5, 0, 1, 6, 7)[k]

        def spare_bank(s, j):
            n = UBASE[s - 1] + j - LAG_V
            return O_BANK + (GROUP[n] + 1) % 2

        out_bank_of = {v: spare_bank(*k) for k, v in SPARE.items()}

        def out_bank(i):
            return out_bank_of["out", i] if i < PAIRS - 1 else O_BANK + (GROUP[NU - 1] + 1) % 2

        def gate_bank(half):
            return out_bank_of["gate", half]

        small_in = sem("small_in")
        cvec_in = sem("cvec_in")
        w2_in = sem("w2_in")
        x_in = [sem(f"x_in{half}") for half in range(2)]
        ada_in = [[sem(f"ada_in{b}{half}") for half in range(2)] for b in range(2)]
        raw_in = [sem(f"raw_in{b}") for b in range(NRAW)]
        trow_out = sem("trow_out")
        t_in = [sem(f"t_in{b}") for b in range(2)]
        kdup = [sem(f"kdup{b}") for b in range(2)]
        consts_set = sem("consts_set")
        flip_set = sem("flip_set")
        pre_tr = sem("pre_tr")
        pre_ev = sem("pre_ev")
        trow_ev = sem("trow_ev")
        x_tr = sem("x_tr")
        xt_act = sem("xt_act")
        ada_acc = sem("ada_acc")
        ada_red = sem("ada_red")
        ss_set = sem("ss_set")
        hhi_set = sem("hhi_set")
        hlo_dve = sem("hlo_dve")
        hlo_pool = sem("hlo_pool")
        hf_set = sem("hf_set")
        p1_hi = sem("p1_hi")
        p1_lo = sem("p1_lo")
        hi_set = sem("hi_set")
        lo_set = sem("lo_set")
        p1_used = sem("p1_used")
        tok_ev = sem("tok_ev")
        gb_exp = sem("gb_exp")
        g_set = sem("g_set")
        kb_hi = sem("kb_hi")
        kb_lo = sem("kb_lo")
        bt_set = sem("bt_set")
        w1_used = sem("w1_used")
        he_set = sem("he_set")
        hs_set = sem("hs_set")
        cmp2 = sem("cmp2")
        kc_hi = sem("kc_hi")
        cmp_set = sem("cmp_set")
        pj = sem("pj")
        pj_act = sem("pj_act")
        pj_dve = sem("pj_dve")
        qk_done = sem("qk_done")
        lg_set = sem("lg_set")
        ex_set = sem("ex_set")
        cn_set = sem("cn_set")
        tr_done = sem("tr_done")
        ev_act = sem("ev_act")
        ev_dve = sem("ev_dve")
        pv_done = sem("pv_done")
        og_set = sem("og_set")
        add_done = sem("add_done")
        gated = sem("gated")
        tc_set = sem("tc_set")
        gate_used = sem("gate_used")
        grow = sem("grow")
        g1_set = sem("g1_set")
        wo_scaled = sem("wo_scaled")
        res_in = [sem(f"res_in{t}") for t in range(NT)]
        ln_in = sem("ln_in")
        ot_tr = sem("ot_tr")
        ot_hi = sem("ot_hi")
        ot_lo = sem("ot_lo")
        ya_done = sem("ya_done")
        ya_ev = sem("ya_ev")
        y_done = sem("y_done")
        mean_set = sem("mean_set")
        sd_set = sem("sd_set")
        rstd_set = sem("rstd_set")
        nmr_set = sem("nmr_set")
        norm_set = sem("norm_set")
        aff_set = sem("aff_set")
        aff_dve = sem("aff_dve")
        out_done = sem("out_done")
        dve_step = sem("dve_step")
        act_step = sem("act_step")
        pool_step = sem("pool_step")

        def raw_free(eng, n):
            kind, a, b = RAW[n]
            if kind == "p1":
                eng.wait_ge(p1_hi, 2 * a + 2)
                eng.wait_ge(p1_lo, 2 * a + 2)
            elif kind in ("ch", "wo"):
                eng.wait_ge(hi_set, split_no(RAW[n]) + 1)
                eng.wait_ge(lo_set, split_no(RAW[n]) + 1)
            elif kind == "w1":
                eng.wait_ge(w1_used, 3 * a + b + 1)
            else:
                eng.wait_ge(gate_used, a + 1)

        def raw_landed(eng, u):
            n = RAWI[u]
            eng.wait_ge(raw_in[n % NRAW], raw_count(n))
            return slot(n)

        def evacuated(eng, n):
            on_act = evac_on_act(n)
            eng.wait_ge(ev_act if on_act else ev_dve, evacs(n, on_act))

        def act_tiles(t):
            return sum(TILES[m][0] != "v" for m in range(t + 1))

        def store(sp, t):
            if t < len(POOL_COLS):
                sp.wait_ge(aff_set, t + 1)
            if t in DVE_LAST:
                sp.wait_ge(aff_dve, DVE_LAST.index(t) + 1)
            if t == STORES[-1]:
                for half in range(2):
                    f = slice(512 * half, 512 * half + 512)
                    if half:
                        sp.wait_ge(aff_dve, len(DVE_LAST) + 1)
                    sp.dma_start(out[0, t * P:(t + 1) * P, f], rows(t)[:, f]).then_inc(out_done, 16)
            else:
                sp.dma_start(out[0, t * P:(t + 1) * P, :], rows(t)).then_inc(out_done, 16)

        block = ctx.enter_context(nc.Block())

        @block.sync
        def _(sp):
            sp.dma_start(cT, c_in.rearrange("o (p k) -> (o p) k", k=KT)).then_inc(cvec_in, 16)

            def load_ada(g):
                if g >= 2:
                    sp.wait_ge(ada_acc, g - 1)
                for half in range(2):
                    k4 = slice(4 * half, 4 * half + 4)
                    for s in range(2):
                        src = w_ada[:, s * D + 256 * g:s * D + 256 * (g + 1)].rearrange("(p k) f -> p k f", k=KT)
                        sp.dma_start(ada[:, g % 2, s, k4, :], src[:, k4, :]).then_inc(ada_in[g % 2][half], 16)

            def load_raw(n):
                if n >= NRAW:
                    raw_free(sp, n - NRAW)
                kind, a, b = RAW[n]
                d, s = slot(n), raw_in[n % NRAW]
                if kind == "p1":
                    for o, to, w in PIECES:
                        sp.dma_start(d.rearrange("p (k f) -> p k f", k=2)[:, :, to:to + w],
                                     w_in[2 * a * P:2 * (a + 1) * P, KVB + o:KVB + o + w]
                                     .rearrange("(k p) f -> p k f", p=P)).then_inc(s, 16)
                elif kind == "ch":
                    dv = d[:, 0:4 * CW].rearrange("p (k f) -> p k f", k=4)
                    for m, col in enumerate(CHUNKS[a][0]):
                        sp.dma_start(dv[:, :, m * P:(m + 1) * P],
                                     w_in[4 * b * P:4 * (b + 1) * P, col:col + P]
                                     .rearrange("(k p) f -> p k f", p=P)).then_inc(s, 16)
                elif kind == "w1":
                    k0, k1 = W1PARTS[b]
                    sp.dma_start(d[:, 0:(k1 - k0) * CMP_HID].rearrange("p (k f) -> p k f", f=CMP_HID),
                                 cmp_w1[a, k0 * P:k1 * P, :].rearrange("(k p) f -> p k f", p=P)).then_inc(s, 16)
                elif kind == "gate" and a == KT:
                    sp.dma_start(d[0:1, 0:D], b_ada[:, 2 * D:3 * D]).then_inc(s, 16)
                elif kind == "gate":
                    sp.dma_start(d[:, 0:D], w_ada[:, 2 * D:3 * D].rearrange("(p k) f -> p k f", k=KT)[:, a, :])\
                        .then_inc(s, 16)
                else:
                    sp.dma_start(d[:, 0:D], w_out[WO[a] * P:(WO[a] + 1) * P, :]).then_inc(s, 16)

            def load_tables(c):
                if c >= 2:
                    sp.wait_ge(lg_set, UBASE[c - 1])
                h0 = H_A + 2 * c if c < 4 else 2 * (c - 4)
                src = bass.AP(scratch.tensor, h0 * TROW, [[1, P], [TROW, 2], [1, SEQ]])
                sp.dma_start(T[:, c % 2, :, :], src).then_inc(t_in[c % 2], 16)

            def load_x(half):
                sp.dma_start(x_tok[half], x[0, :, 512 * half:512 * half + 512].rearrange("(t p) d -> p t d", p=P))\
                    .then_inc(x_in[half], 16)

            load_x(0)
            load_ada(0)
            load_raw(0)
            load_x(1)
            for g in range(1, 4):
                load_ada(g)
                load_raw(g)
            sp.dma_start(W2, cmp_w2.rearrange("v (j p) d -> p v j d", p=P)).then_inc(w2_in, 16)
            sp.wait_ge(trow_ev, 1)
            sp.dma_start(scratch, trow).then_inc(trow_out, 16)
            sp.wait_ge(trow_out, 16)
            load_tables(0)
            load_tables(1)
            n = 4
            for s in range(PAIRS + 1):
                if 2 <= s < PAIRS:
                    load_tables(s)
                last = RAWI[plan(s)[-1][1]] if s else RAWI["w1", 1, 2]
                while n <= last:
                    if n == RAWI["wo", 6, 0]:
                        sp.wait_ge(pj, 24)
                        for t in range(NT):
                            sp.dma_start(rows(t), x[0, t * P:(t + 1) * P, :]).then_inc(res_in[t], 16)
                    load_raw(n)
                    n += 1
            for m in range(len(RAW) - NRAW, len(RAW)):
                raw_free(sp, m)
            sp.dma_start(lng, ln_g[0].partition_broadcast(P)).then_inc(ln_in, 16)
            sp.dma_start(lnb, ln_b[0].partition_broadcast(P)).then_inc(ln_in, 16)
            for t in STORES:
                store(sp, t)
            sp.wait_ge(out_done, 16 * (NT + 1))

        @block.gpsimd
        def _(pool):
            nc.gpsimd.memset(ident[:, :], 0.0).then_inc(pool_step, 1)
            nc.gpsimd.memset(flip[:, :], 0.0).then_inc(pool_step, 1)
            nc.gpsimd.memset(cmask, 1.0).then_inc(pool_step, 1)
            nc.gpsimd.memset(ones[:, :], 1.0).then_inc(pool_step, 1)
            pool.wait_ge(pool_step, 4)
            nc.gpsimd.affine_select(out=ident[:, :], in_=ident[:, :], compare_op=ALU.not_equal, fill=1.0, base=0,
                                    pattern=[[-1, P]], channel_multiplier=1).then_inc(consts_set, 1)
            nc.gpsimd.affine_select(out=flip[:, :], in_=flip[:, :], compare_op=ALU.not_equal, fill=1.0,
                                    base=-(P - 1), pattern=[[1, P]], channel_multiplier=1).then_inc(flip_set, 1)
            nc.gpsimd.affine_select(out=cmask[:, 0:1], in_=cmask[:, 0:1], compare_op=ALU.is_ge, fill=0.0,
                                    base=-(CMP_LEN - 1), pattern=[[0, 1]], channel_multiplier=1)\
                .then_inc(consts_set, 1)
            nc.gpsimd.memset(tc[:, :], BIG).then_inc(consts_set, 1)
            nc.gpsimd.memset(hsv[:, :], 0.0).then_inc(consts_set, 1)
            nc.gpsimd.memset(kc[:, :].bitcast(F32), 0.0).then_inc(consts_set, 1)
            nc.gpsimd.memset(vc[:, :], 0.0).then_inc(consts_set, 1)
            nc.gpsimd.memset(vb[:, :], 1.0).then_inc(consts_set, 1)
            nc.gpsimd.memset(va[:, :], 1.0).then_inc(consts_set, 1)

            def split_lo(u):
                src = raw_landed(pool, u)
                n = width(u)
                pool.wait_ge(hi_set, split_no(u) + 1)
                nc.gpsimd.tensor_tensor(split_at(w_lo, u), src[:, 0:n], split_at(w_hi, u).bitcast(F32),
                                        ALU.subtract).then_inc(lo_set, 1)

            def compressed_bias(c):
                pool.wait_ge(t_in[c % 2], 16 * (c // 2 + 1))
                if c >= 2:
                    pool.wait_ge(lg_set, UBASE[c - 2] + 1)
                for i in range(NT):
                    n = 8 * i + 7
                    o = SEQ - P + CMP_LEN - 1 - P * i
                    ins = nc.gpsimd.tensor_copy(Tc[:, c % 2, i, :, 0:n],
                                                T[:, c % 2, :, o:o + CMP_STRIDE * (n - 1) + 1:CMP_STRIDE])
                ins.then_inc(tc_set, 1)

            def group_adds(n):
                kind, c, h, br, i = UNITS[n]
                if kind == "att" and c < 4:
                    r = GROUP[n]
                    pool.wait_ge(og_set, r + 1)
                    col = D // 2 + P * c + HD * h
                    if adds[0]:
                        pool.wait_ge(add_done, adds[0])
                    nc.gpsimd.tensor_tensor(OS[:, :, col:col + HD], OS[:, :, col:col + HD],
                                            tmp[:, 256 * (adds[0] % 2):256 * (adds[0] % 2) + 256]
                                            .rearrange("p (t d) -> p t d", t=NT), ALU.add).then_inc(add_done, 1)
                    adds[0] += 1
                if n + 1 == UBASE[c + 1] and c != 3:
                    pool.wait_ge(og_set, GROUP[n] + 1)
                    if c < 4:
                        pool.wait_ge(add_done, adds[0])
                    gate_pair(c)

            def gate_pair(c):
                col = D // 2 + P * c if c < 4 else P * (c - 4)
                pool.wait_ge(pj_dve, TILE["z", c % 4, 1] + 1)
                nc.gpsimd.tensor_tensor(OS[:, :, col:col + P], OS[:, :, col:col + P], Z[:, :, col:col + P],
                                        ALU.mult).then_inc(gated, 1)

            adds = [0]
            def h_low(k):
                pool.wait_ge(hf_set, k // 2 + 1)
                nc.gpsimd.tensor_tensor(lov[:, k, :], xT[:, k, :], hiv[:, k, :].bitcast(F32),
                                        ALU.subtract).then_inc(hlo_pool, 1)

            def split_lo_first(g):
                src = raw_landed(pool, ("p1", g, 0))
                for e in range(2):
                    o = (2 * g + e) * W1ST
                    pool.wait_ge(p1_hi, 2 * g + e + 1)
                    nc.gpsimd.tensor_tensor(w_lo[:, o:o + W1ST], src[:, e * W1ST:(e + 1) * W1ST],
                                            w_hi[:, o:o + W1ST].bitcast(F32), ALU.subtract).then_inc(p1_lo, 1)

            split_lo_first(0)
            for g in range(4):
                h_low(2 * g + 1)
                if g < 3:
                    split_lo_first(g + 1)
            split_lo(("ch", 0, 0))
            split_lo(("ch", 0, 1))
            n = 0
            for s in range(PAIRS + 1):
                for j in range(iters(s)):
                    if s < 4 and j == iters(s) // 2:
                        compressed_bias(s)
                    for u in at_iter(s, j):
                        if u[0] != "gate":
                            split_lo(u)
                    if s >= 1:
                        m = n - LAG_V - 1
                        if m >= 0 and group_last(m):
                            group_adds(m)
                        if s == PAIRS and j == 1:
                            pool.wait_ge(add_done, adds[0])
                            gate_pair(3)
                        n += 1
            for m in range(NU - LAG_V - 1, NU):
                if group_last(m):
                    group_adds(m)
            pool.wait_ge(ln_in, 32)
            for t, w in enumerate(POOL_COLS):
                pool.wait_ge(norm_set, t + 1)
                y = rows(t)[:, 0:w]
                nc.gpsimd.tensor_tensor(y, y, lng[:, 0:w], ALU.mult).then_inc(pool_step, 1)
                pool.wait_ge(pool_step, 5 + t)
                nc.gpsimd.tensor_tensor(y, y, lnb[:, 0:w], ALU.add).then_inc(aff_set, 1)

        @block.scalar
        def _(act):
            def split_hi(u):
                kind, a, b = u
                src = raw_landed(act, u)
                if kind == "wo":
                    act.wait_ge(wo_scaled, a + 1)
                if kind == "ch" and a == 0:
                    act.wait_ge(p1_used, 4)
                elif kind == "ch" and a == 1:
                    act.wait_ge(p1_used, KT)
                elif kind == "ch":
                    act.wait_ge(pj, 3 * (a - 1))
                elif kind == "wo":
                    act.wait_ge(pj, 21 if a < 3 else 24)
                n = width(u)
                nc.scalar.activation(split_at(w_hi, u), src[:, 0:n], ACT.Copy).then_inc(hi_set, 1)

            def q_or_k_hi(src, tile0, tile1, scale, s, n, backwards):
                for a, dst in ((0, tile0), (1, tile1)):
                    o = src[HD * a:HD * (a + 1), :]
                    if backwards:
                        o, dst = blocks(o)[:, :, ::-1], blocks(dst)
                    ins = nc.scalar.activation(dst, o, ACT.Copy, scale=scale)
                ins.then_inc(s, n)

            def tile_part(t):
                kind, c, part = TILES[t]
                src = bank(t % 2)
                if kind == "v":
                    return
                act.wait_ge(pj, t + 1)
                if kind == "z":
                    if c >= 1:
                        act.wait_ge(pj_dve, TILE["z", c - 1, part] + 1)
                    nc.scalar.activation(et[:, 512 * part:512 * part + 512], src, ACT.Tanh, scale=0.5)\
                        .then_inc(pj_act, 1)
                elif kind == "q":
                    if c >= 2:
                        act.wait_ge(qk_done, UBASE[c - 1])
                    q_or_k_hi(src, QS[0:HD, c % 2, 0, :], QS[HD:P, c % 2, 1, :], -HD ** -0.5, pj_act, 1, True)
                else:
                    act.wait_ge(qk_done, UBASE[{4: 2, 5: 4, 6: 5, 7: 6}[c]])
                    q_or_k_hi(src, K[0:HD, c % 2, 0, 0, :], K[HD:P, c % 2, 1, 0, :], 1.0, pj_act, 1, False)

            def double_keys(t):
                kind, c, part = TILES[t]
                act.wait_ge(pj_dve, t + 1)
                act.dma_start(K[HD:P, c % 2, 0, :, :].bitcast(F32), K[0:HD, c % 2, 0, :, :].bitcast(F32))\
                    .then_inc(kdup[c % 2], 16)
                act.dma_start(K[0:HD, c % 2, 1, :, :].bitcast(F32), K[HD:P, c % 2, 1, :, :].bitcast(F32))\
                    .then_inc(kdup[c % 2], 16)

            def probs(n):
                kind, c, h, br, i = UNITS[n]
                act.wait_ge(lg_set, n + 1)
                if kind == "cmp":
                    v = lg[:, 512 * (n % 4):512 * (n % 4) + 256]
                    nc.scalar.activation(v, v, ACT.Exp, scale=-1.0).then_inc(ex_set, 1)
                else:
                    v = lg[:, 512 * (n % 4):512 * (n % 4) + P * (i + 1)]
                    nc.scalar.activation(v, v, ACT.Exp, bias=mn[:, n % 8:n % 8 + 1], scale=-1.0).then_inc(ex_set, 1)

            def evac(n):
                kind, c, h, br, i = UNITS[n]
                act.wait_ge(tr_done, n + 1)
                if n >= N_PT:
                    act.wait_ge(pv_done, n - N_PT + 1)
                w = 512 if kind == "cmp" else P * (i + 1)
                m = HD if kind == "cmp" else P
                nc.scalar.activation(pt[0:m, 512 * (n % N_PT):512 * (n % N_PT) + w], bank(T_BANK + n % 2)[0:m, 0:w],
                                     ACT.Copy).then_inc(ev_act, 1)

            def out_hi(i):
                k = out_tile(OUT_PAIRS[i])
                act.wait_ge(ot_tr, i + 1)
                nc.scalar.activation(OTh[:, :, P * k:P * (k + 1)], blocks(bank(out_bank(i))), ACT.Copy, scale=0.5)\
                    .then_inc(ot_hi, 1)

            def x_out(k):
                act.wait_ge(x_tr, k + 1)
                nc.scalar.activation(xT[:, k, :], bank(x_bank(k)), ACT.Copy).then_inc(xt_act, 1)

            act.dma_start(onehot, consts[:, 0:TROW]).then_inc(small_in, 16)
            act.dma_start(rel[N_B:N_B + 2, :], consts[N_B:N_B + 2, TROW:TROW + 16]).then_inc(small_in, 16)
            act.dma_start(rel[0:N_B, :], rel_bias).then_inc(small_in, 16)
            act.dma_start(ba_row, b_ada[:, 0:2 * D].rearrange("o (j q) -> (o j) q", q=P)).then_inc(small_in, 16)
            act.dma_start(pe_row, cmp_pe.rearrange("v (k r) d -> (v k) (r d)", r=2)).then_inc(small_in, 16)
            def split_hi_first(g):
                src = raw_landed(act, ("p1", g, 0))
                for e in range(2):
                    o = (2 * g + e) * W1ST
                    nc.scalar.activation(w_hi[:, o:o + W1ST], src[:, e * W1ST:(e + 1) * W1ST], ACT.Copy)\
                        .then_inc(p1_hi, 1)

            split_hi_first(0)
            for k in range(4):
                x_out(k)
            for g in range(4):
                act.wait_ge(ss_set, g + 1)
                for k in (2 * g, 2 * g + 1):
                    act.wait_ge(xt_act, k + 1)
                    nc.scalar.activation(hiv[:, k, :], xT[:, k, :], ACT.Identity, bias=ss[:, k:k + 1],
                                         scale=ss[:, 8 + k:9 + k]).then_inc(hhi_set, 1)
                nc.scalar.activation(xT[:, k, :], xT[:, k, :], ACT.Identity, bias=ss[:, k:k + 1],
                                     scale=ss[:, 8 + k:9 + k]).then_inc(hf_set, 1)
                if g == 0:
                    for k in range(4, KT):
                        x_out(k)
                if g < 3:
                    act.wait_ge(x_tr, KT)
                    split_hi_first(g + 1)
            split_hi(("ch", 0, 0))
            split_hi(("ch", 0, 1))
            act.wait_ge(p1_used, KT)
            act.wait_ge(consts_set, 8)
            for half in range(2):
                t, b = 2 * half, TOK_BANK[2 * half]
                nc.scalar.activation(gates[:, 24 * t:24 * (t + 2)].rearrange("p (t f) -> p t f", t=2),
                                     ps[:, 512 * b:512 * (b + 2)].rearrange("p (t f) -> p t f", t=2)[:, :, 256:280],
                                     ACT.Exp, scale=-1.0).then_inc(gb_exp, 1)
                for t in range(t, t + 2):
                    nc.scalar.activation(VB[:, t, :, :, 0:HD].rearrange("p b g d -> p (b g) d"),
                                         bank(TOK_BANK[t], 0, 256).rearrange("p (c d) -> p c d", c=4), ACT.Copy)\
                        .then_inc(tok_ev, 1)
            for br in range(2):
                q_or_k_hi(bank(4 + br), K[0:HD, 0, br, 0, :], K[HD:P, 1, br, 0, :], 1.0, kb_hi, 1, False)
            act.wait_ge(kb_lo, 2)
            act.dma_start(K[HD:P, 0, :, :, :].bitcast(F32), K[0:HD, 0, :, :, :].bitcast(F32)).then_inc(kdup[0], 16)
            act.dma_start(K[0:HD, 1, :, :, :].bitcast(F32), K[HD:P, 1, :, :, :].bitcast(F32)).then_inc(kdup[1], 16)

            def hidden_exp(v):
                act.wait_ge(w1_used, 3 * (v + 1))
                if v:
                    act.wait_ge(hs_set, 1)
                o = 512 * HID_BANK[v]
                nc.scalar.activation(HE, ps[:, o:o + 1024].rearrange("p (j n) -> p j n", j=2)[:, :, 0:62], ACT.Exp,
                                     scale=-1.0).then_inc(he_set, 1)

            n = 0
            for s in range(PAIRS + 1):
                for j in range(iters(s)):
                    if s >= 1:
                        probs(n)
                        if n >= LAG_T and evac_on_act(n - LAG_T):
                            evac(n - LAG_T)
                        if AFTER.get((s, j), ("", 0))[0] == "out":
                            out_hi(AFTER[s, j][1])
                        n += 1
                    for t in ended(s, j, 2):
                        if TILES[t][0] == "k":
                            double_keys(t)
                    for t in ended(s, j, 1):
                        tile_part(t)
                    for u in at_iter(s, j):
                        if u[0] != "gate":
                            split_hi(u)
                    if s == 0 and j == 2:
                        hidden_exp(0)
                    if s == 0 and j == 4:
                        act.wait_ge(cmp2, 1)
                        act.wait_ge(consts_set, 8)
                        src = bank(CMP_BANK[0])[0:HD, 0:62].rearrange("p (g n) -> p g n", g=2)
                        nc.scalar.activation(KC[0:HD, 0, :, 0:N_CMP], src, ACT.Copy)
                        nc.scalar.activation(KC[HD:P, 0, :, 0:N_CMP], src, ACT.Copy).then_inc(kc_hi, 1)
                    if s == 0 and j == 5:
                        hidden_exp(1)
            out_hi(PAIRS - 2)
            for m in range(NU - LAG_T, NU):
                if evac_on_act(m):
                    evac(m)
            out_hi(PAIRS - 1)
            nc.scalar.activation(sdv[:, 0:1], eps, ACT.Sqrt, bias=eps).then_inc(act_step, 1)
            act.wait_ge(act_step, 1)
            for t in range(NT):
                act.wait_ge(mean_set, t + 1)
                act.wait_ge(act_step, t + 1)
                nc.scalar.activation(et[:, :], rows(t), ACT.Square, bias=nmean[:, t:t + 1],
                                     accum_out=sq[:, t:t + 1]).then_inc(act_step, 1)
                act.wait_ge(act_step, t + 2)
                nc.scalar.activation(sdv[:, t:t + 1], sq[:, t:t + 1], ACT.Sqrt, bias=eps, scale=1.0 / D)\
                    .then_inc(sd_set, 1)
                if 1 <= t <= len(POOL_COLS):
                    act.wait_ge(nmr_set, t)
                    nc.scalar.activation(rows(t - 1), rows(t - 1), ACT.Identity, bias=nmr[:, t - 1:t],
                                         scale=rstd[:, t - 1:t]).then_inc(norm_set, 1)

        @block.vector
        def _(dve):
            steps = [0]

            def link(ins):
                steps[0] += 1
                ins.then_inc(dve_step, 1)
                dve.wait_ge(dve_step, steps[0])

            link(nc.vector.memset(eps, LN_EPS))
            def ada_sums(g):
                dve.wait_ge(ada_in[g % 2][0], 32 * (g // 2 + 1))
                if g == 0:
                    dve.wait_ge(cvec_in, 16)
                if g >= 1:
                    dve.wait_ge(ada_red, g)
                a = acc[:, :].rearrange("p (s f) -> p s f", s=2)
                for k in range(KT):
                    src = ada[:, g % 2, :, k, :]
                    if k == 4:
                        dve.wait_ge(ada_in[g % 2][1], 32 * (g // 2 + 1))
                    if k == 0:
                        ins = nc.vector.tensor_scalar(a, src, cT[:, 0:1], None, ALU.mult)
                    else:
                        ins = nc.vector.scalar_tensor_tensor(out=a, in0=src, scalar=cT[:, k:k + 1], in1=a,
                                                             op0=ALU.mult, op1=ALU.add)
                    if k < KT - 1:
                        link(ins)
                    else:
                        ins.then_inc(ada_acc, 1)

            def shift_scale(g):
                dve.wait_ge(ada_red, g + 1)
                dve.wait_ge(pre_ev, 1)
                sv = ss.rearrange("p (s k) -> p s k", s=2)[:, :, 2 * g:2 * g + 2]
                nc.vector.tensor_tensor(sv, bank(7, 320 + 4 * g, 4).rearrange("p (s k) -> p s k", s=2),
                                        ba.rearrange("p (s k) -> p s k", s=2)[:, :, 2 * g:2 * g + 2],
                                        ALU.add).then_inc(ss_set, 1)

            def h_low(k):
                dve.wait_ge(xt_act, k + 1)
                link(nc.vector.tensor_scalar(tmp[:, :], xT[:, k, :], ss[:, 8 + k:9 + k], ss[:, k:k + 1],
                                             ALU.mult, ALU.add))
                dve.wait_ge(hhi_set, k + 1)
                nc.vector.tensor_tensor(lov[:, k, :], tmp[:, :], hiv[:, k, :].bitcast(F32),
                                        ALU.subtract).then_inc(hlo_dve, 1)

            ada_sums(0)
            dve.wait_ge(pre_tr, 1)
            nc.vector.tensor_copy(trow, ps[0:16, 0:TROW]).then_inc(trow_ev, 1)
            dve.wait_ge(pre_tr, 2)
            nc.vector.tensor_copy(ba[:, 0:8], bank(6, 0, 8))
            nc.vector.tensor_scalar(ba[:, 8:16], bank(6, 8, 8), 1.0, None, ALU.add)
            nc.vector.tensor_copy(peT, bank(6, 16, 32)).then_inc(pre_ev, 1)
            for g in range(4):
                shift_scale(g)
                dve.wait_ge(ss_set, g + 1)
                if g:
                    dve.wait_ge(hlo_dve, g)
                h_low(2 * g)
                if g < 3:
                    ada_sums(g + 1)

            def blocks_of(v):
                for par in range(2):
                    for g in range(2):
                        b = ps[HD * g:HD * (g + 1), 512 * (S_BANK + v):512 * (S_BANK + v) + 512]
                        src = bass.AP(b.tensor, b.offset + par, [list(b.ap[0]), [2, 16], [CMP_STRIDE, N_CMP]])
                        pe = peT[HD * par:HD * (par + 1), 16 * v:16 * v + 16].unsqueeze(2)\
                            .to_broadcast([HD, 16, N_CMP])
                        ins = nc.vector.tensor_tensor(bt[HD * par:HD * (par + 1), v, :, N_CMP * g:N_CMP * (g + 1)],
                                                      src, pe, ALU.add)
                ins.then_inc(bt_set, 1)

            def low(dst, src, hi, scale, backwards):
                if backwards:
                    dst, src, hi = blocks(dst), blocks(src)[:, :, ::-1], blocks(hi)
                return nc.vector.scalar_tensor_tensor(out=dst, in0=src, scalar=scale, in1=hi.bitcast(F32),
                                                      op0=ALU.mult, op1=ALU.subtract)

            dve.wait_ge(p1_used, KT)
            blocks_of(0)
            for br in range(2):
                dve.wait_ge(kb_hi, br + 1)
                low(K[0:HD, 0, br, 1, :], bank(4 + br)[0:HD, :], K[0:HD, 0, br, 0, :], 1.0, False)
                low(K[HD:P, 1, br, 1, :], bank(4 + br)[HD:P, :], K[HD:P, 1, br, 0, :], 1.0, False).then_inc(kb_lo, 1)
            blocks_of(1)
            dve.wait_ge(gb_exp, 2)
            link(nc.vector.tensor_scalar(gates, gates, 1.0, None, ALU.add))
            link(nc.vector.reciprocal(gates, gates))
            dve.wait_ge(consts_set, 8)
            nc.vector.tensor_tensor(G0, G[:, :, 0, :], cmask.unsqueeze(2).to_broadcast([P, NT, 8]),
                                    ALU.mult).then_inc(g_set, 1)
            dve.wait_ge(g_set, 1)

            def hidden(v):
                dve.wait_ge(he_set, v + 1)
                link(nc.vector.tensor_scalar(HE, HE, 1.0, None, ALU.add))
                link(nc.vector.reciprocal(HE, HE))
                for jj in range(2):
                    hb = bank(HID_BANK[v] + jj, 0, 62)
                    if v == 0:
                        ins = nc.vector.tensor_tensor(HS[:, jj, :], hb, HE[:, jj, :], ALU.mult)
                    else:
                        for r in range(2):
                            ins = nc.vector.tensor_tensor(HSV[:, jj, :, r, 0:N_CMP],
                                                          hb.rearrange("p (g n) -> p g n", g=2),
                                                          HE[:, jj, :].rearrange("p (g n) -> p g n", g=2), ALU.mult)
                ins.then_inc(hs_set, 1)

            def tile_part(t):
                kind, c, part = TILES[t]
                src = bank(t % 2)
                if kind != "v":
                    dve.wait_ge(pj_act, act_tiles(t))
                if kind == "z":
                    ev = et[:, 512 * part:512 * part + 512]
                    for m in range(2):
                        dst = Z[:, 2 * part:2 * part + 2, m * 512 + P * c:m * 512 + P * (c + 1)]
                        v = src.rearrange("p (t m d) -> p t m d", t=2, m=2)[:, :, m, :]
                        w = ev.rearrange("p (t m d) -> p t m d", t=2, m=2)[:, :, m, :]
                        ins = nc.vector.scalar_tensor_tensor(out=dst, in0=w, scalar=1.0, in1=v, op0=ALU.add,
                                                             op1=ALU.mult)
                elif kind == "q":
                    low(QS[HD:P, c % 2, 0, :], src[0:HD, :], QS[0:HD, c % 2, 0, :], -HD ** -0.5, True)
                    ins = low(QS[0:HD, c % 2, 1, :], src[HD:P, :], QS[HD:P, c % 2, 1, :], -HD ** -0.5, True)
                elif kind == "k":
                    low(K[0:HD, c % 2, 0, 1, :], src[0:HD, :], K[0:HD, c % 2, 0, 0, :], 1.0, False)
                    ins = low(K[HD:P, c % 2, 1, 1, :], src[HD:P, :], K[HD:P, c % 2, 1, 0, :], 1.0, False)
                else:
                    dve.wait_ge(pj, t + 1)
                    if c == 1:
                        dve.wait_ge(pv_done, UBASE[4])
                    for pp in range(2):
                        ins = nc.vector.tensor_copy(
                            VAv[c][:, pp, 2 * part:2 * part + 2, :, 0:HD],
                            src.rearrange("p (t q h d) -> p t q h d", t=2, q=2, h=2)[:, :, pp, :, :])
                ins.then_inc(pj_dve, 1)

            def logits(n):
                kind, c, h, br, i = UNITS[n]
                dve.wait_ge(qk_done, n + 1)
                if n >= 4:
                    dve.wait_ge(tr_done, n - 3)
                if kind == "cmp":
                    dve.wait_ge(tc_set, c + 1)
                    v = lg[:, 512 * (n % 4):512 * (n % 4) + 256]
                    v3 = v.rearrange("p (q n) -> p q n", n=32)
                    s4 = bank(S_BANK + n % 2).rearrange("p (q l n) -> p q l n", l=2, n=32)
                    link(nc.vector.tensor_tensor(v3, s4[:, :, 1, :], tc[:, 256 * (c % 2):256 * (c % 2) + 256]
                                                 .rearrange("p (q n) -> p q n", n=32), ALU.add))
                    link(nc.vector.tensor_tensor(v3, s4[:, :, 0, :], v3, ALU.add))
                    link(nc.vector.tensor_reduce(mnc, v3, AX.X, ALU.min))
                    nc.vector.tensor_tensor(v3, v3, mnc.unsqueeze(2).to_broadcast([P, 8, 32]),
                                            ALU.subtract).then_inc(lg_set, 1)
                else:
                    w = P * (i + 1)
                    if h == 0 and br == 0 and i == 0:
                        dve.wait_ge(t_in[c % 2], 16 * (c // 2 + 1))
                    nc.vector.tensor_tensor_reduce(out=lg[:, 512 * (n % 4):512 * (n % 4) + w],
                                                   in0=bank(S_BANK + n % 2, 0, w),
                                                   in1=T[:, c % 2, h, SEQ - w:SEQ], scale=1.0, scalar=3e38,
                                                   op0=ALU.add, op1=ALU.min,
                                                   accum_out=mn[:, n % 8:n % 8 + 1]).then_inc(lg_set, 1)

            def cmp_norm(n):
                dve.wait_ge(ex_set, n + 1)
                v3 = lg[:, 512 * (n % 4):512 * (n % 4) + 256].rearrange("p (q n) -> p q n", n=32)
                link(nc.vector.tensor_reduce(rcc, v3, AX.X, ALU.add))
                link(nc.vector.reciprocal(rcc, rcc))
                nc.vector.tensor_tensor(v3, v3, rcc.unsqueeze(2).to_broadcast([P, 8, 32]),
                                        ALU.mult).then_inc(cn_set, 1)

            def evac(n):
                kind, c, h, br, i = UNITS[n]
                dve.wait_ge(tr_done, n + 1)
                if n >= N_PT:
                    dve.wait_ge(pv_done, n - N_PT + 1)
                w = P * (i + 1)
                nc.vector.tensor_copy(pt[:, 512 * (n % N_PT):512 * (n % N_PT) + w], bank(T_BANK + n % 2, 0, w))\
                    .then_inc(ev_dve, 1)

            def group_end(n):
                kind, c, h, br, i = UNITS[n]
                dve.wait_ge(pv_done, n + 1)
                b = bank(O_BANK + GROUP[n] % 2)
                if kind == "cmp":
                    o = OS[:, :, D // 2 + P * c:D // 2 + P * (c + 1)].rearrange("p t (h d) -> p t h d", h=2)
                    nc.vector.tensor_tensor(o, b.rearrange("p (t h d) -> p t h d", t=NT, h=2),
                                            G0[:, :, 2 * c:2 * c + 2].unsqueeze(3).to_broadcast([P, NT, 2, HD]),
                                            ALU.mult).then_inc(og_set, 1)
                    return
                o = b[:, 0:NT * 65].rearrange("p (t d) -> p t d", t=NT)
                rc = rcs[:, 8 * (GROUP[n] % 2):8 * (GROUP[n] % 2) + 8]
                link(nc.vector.reciprocal(rc[:, 0:NT].unsqueeze(2), o[:, :, HD:HD + 1]))
                if c < 4:
                    link(nc.vector.tensor_tensor(rc[:, 4:8], rc[:, 0:4], G[:, :, 1 + br, 2 * c + h], ALU.mult))
                    if adds[0] >= 2:
                        dve.wait_ge(add_done, adds[0] - 1)
                    dst = tmp[:, 256 * (adds[0] % 2):256 * (adds[0] % 2) + 256].rearrange("p (t d) -> p t d", t=NT)
                    adds[0] += 1
                    r = rc[:, 4:8]
                else:
                    dst = OS[:, :, P * (c - 4) + HD * h:P * (c - 4) + HD * (h + 1)]
                    r = rc[:, 0:4]
                nc.vector.tensor_tensor(dst, o[:, :, 0:HD], r.unsqueeze(2).to_broadcast([P, NT, HD]),
                                        ALU.mult).then_inc(og_set, 1)

            def gate_sums(u):
                k = u[1]
                src = raw_landed(dve, u)
                if k >= 1:
                    dve.wait_ge(gate_used, k)
                if k == 0:
                    ins = nc.vector.tensor_scalar(gacc[:, :], src[:, 0:D], cT[:, 0:1], None, ALU.mult)
                elif k < KT:
                    ins = nc.vector.scalar_tensor_tensor(out=gacc[:, :], in0=src[:, 0:D], scalar=cT[:, k:k + 1],
                                                         in1=gacc[:, :], op0=ALU.mult, op1=ALU.add)
                else:
                    ins = nc.vector.tensor_tensor(gacc[0:1, :], gacc[0:1, :], src[0:1, 0:D], ALU.add)
                ins.then_inc(gate_used, 1)

            def gate_row(half):
                dve.wait_ge(grow, half + 1)
                nc.vector.tensor_scalar(gacc[:, 512 * half:512 * half + 512], bank(gate_bank(half)), 1.0, None,
                                        ALU.add).then_inc(g1_set, 1)

            def scale_wo(u):
                src = raw_landed(dve, u)[:, 0:D]
                dve.wait_ge(g1_set, 2)
                nc.vector.tensor_tensor(src, src, gacc[:, :], ALU.mult).then_inc(wo_scaled, 1)

            def out_lo(i):
                k = out_tile(OUT_PAIRS[i])
                dve.wait_ge(ot_hi, i + 1)
                nc.vector.scalar_tensor_tensor(out=OTl[:, :, P * k:P * (k + 1)], in0=blocks(bank(out_bank(i))),
                                               scalar=0.5, in1=OTh[:, :, P * k:P * (k + 1)].bitcast(F32), op0=ALU.mult,
                                               op1=ALU.subtract).then_inc(ot_lo, 1)

            def early(q):
                y = rows(q // 2)[:, 512 * (q % 2):512 * (q % 2) + 512]
                dve.wait_ge(res_in[q // 2], 16)
                dve.wait_ge(ya_done, q + 1)
                nc.vector.scalar_tensor_tensor(out=y, in0=y, scalar=ALPHA, in1=bank(q % 2), op0=ALU.mult,
                                               op1=ALU.add).then_inc(ya_ev, 1)

            adds = [0]
            n = 0
            for s in range(PAIRS + 1):
                for j in range(iters(s)):
                    if s >= 1:
                        if (s, j) == (PAIRS, 2):
                            early(0)
                        logits(n)
                        if n >= 1 and UNITS[n - 1][0] == "cmp":
                            cmp_norm(n - 1)
                        if s == PAIRS:
                            for q in EARLY_EV.get(j, ()):
                                early(q)
                        if n >= LAG_T and not evac_on_act(n - LAG_T):
                            evac(n - LAG_T)
                        if n > LAG_V and group_last(n - LAG_V - 1):
                            group_end(n - LAG_V - 1)
                        kind, i = AFTER.get((s, j), ("", 0))
                        if kind == "gate":
                            gate_row(i)
                        elif kind == "out":
                            out_lo(i)
                        n += 1
                    for t in ended(s, j, 1):
                        tile_part(t)
                    for u in at_iter(s, j):
                        if u[0] == "gate":
                            gate_sums(u)
                    if (s, j) in SCALE_AT:
                        scale_wo(("wo", SCALE_AT[s, j], 0))
                    if s == 0 and j == 2:
                        hidden(0)
                    if s == 0 and j == 4:
                        dve.wait_ge(kc_hi, 1)
                        src = bank(CMP_BANK[0])[0:HD, 0:62].rearrange("p (g n) -> p g n", g=2)
                        for half in (0, HD):
                            ins = nc.vector.scalar_tensor_tensor(
                                out=KC[half:half + HD, 1, :, 0:N_CMP], in0=src, scalar=1.0,
                                in1=KC[0:HD, 0, :, 0:N_CMP].bitcast(F32), op0=ALU.mult, op1=ALU.subtract)
                        ins.then_inc(cmp_set, 1)
                    if s == 0 and j == 5:
                        hidden(1)
                        dve.wait_ge(cmp2, 2)
                        for g in range(2):
                            for r in range(2):
                                ins = nc.vector.tensor_copy(vc[32 * r:32 * r + 32, P * g + HD * r:P * g + HD * r + HD],
                                                            bank(CMP_BANK[1])[32 * r:32 * r + 32, HD * g:HD * g + HD])
                        ins.then_inc(cmp_set, 1)
            early(2 * NT - 1)
            out_lo(PAIRS - 2)
            for m in range(NU - LAG_T, NU):
                if not evac_on_act(m):
                    evac(m)
            for m in range(NU - LAG_V - 1, NU):
                if group_last(m):
                    group_end(m)
            out_lo(PAIRS - 1)
            def late(t):
                dve.wait_ge(y_done, t + 1)
                b = 512 * LATE_BANK[t]
                link(nc.vector.tensor_tensor_reduce(out=rows(t), in0=ps[:, b:b + 1024], in1=rows(t), scale=1.0,
                                                    scalar=0.0, op0=ALU.add, op1=ALU.add, accum_out=ysum[:, t:t + 1]))
                nc.vector.tensor_scalar(nmean[:, t:t + 1], ysum[:, t:t + 1], -1.0 / D, None, ALU.mult)\
                    .then_inc(mean_set, 1)
                dve.wait_ge(mean_set, t + 1)

            def inverse(t):
                dve.wait_ge(sd_set, t + 1)
                nc.vector.reciprocal(rstd[:, t:t + 1], sdv[:, t:t + 1]).then_inc(rstd_set, 1)

            def centred(t):
                link(nc.vector.scalar_tensor_tensor(out=vrow, in0=rows(t), scalar=nmean[:, t:t + 1], in1=lng,
                                                    op0=ALU.add, op1=ALU.mult))

            def finish(t):
                w = D // 2 if t == STORES[-1] else D
                for f in range(0, D, w):
                    nc.vector.scalar_tensor_tensor(out=rows(t)[:, f:f + w], in0=vrow[:, f:f + w],
                                                   scalar=rstd[:, t:t + 1], in1=lnb[:, f:f + w], op0=ALU.mult,
                                                   op1=ALU.add).then_inc(aff_dve, 1)

            def factors(t):
                inverse(t)
                dve.wait_ge(rstd_set, t + 1)
                nc.vector.tensor_tensor(nmr[:, t:t + 1], nmean[:, t:t + 1], rstd[:, t:t + 1], ALU.mult)\
                    .then_inc(nmr_set, 1)

            late(0)
            late(1)
            factors(0)
            late(2)
            factors(1)
            dve.wait_ge(ln_in, 32)
            centred(2)
            late(3)
            inverse(2)
            dve.wait_ge(rstd_set, 3)
            finish(2)
            dve.wait_ge(aff_dve, 1)
            centred(3)
            dve.wait_ge(norm_set, 2)
            y = rows(1)[:, POOL_COLS[1]:D]
            link(nc.vector.tensor_tensor(y, y, lng[:, POOL_COLS[1]:D], ALU.mult))
            nc.vector.tensor_tensor(y, y, lnb[:, POOL_COLS[1]:D], ALU.add).then_inc(aff_dve, 1)
            inverse(3)
            dve.wait_ge(rstd_set, 4)
            finish(3)

        @block.tensor
        def _(pe):
            mm = nc.tensor.matmul
            pe.wait_ge(small_in, 80)
            mm(ps[0:16, 0:512], rel, onehot[:, 0:512], start=True, stop=True)
            mm(ps[0:16, 512:TROW], rel, onehot[:, 512:TROW], start=True, stop=True).then_inc(pre_tr, 1)
            pe.wait_ge(consts_set, 1)
            nc.tensor.transpose(bank(6, 0, 16), ba_row, ident[0:16, 0:16])
            nc.tensor.transpose(bank(6, 16, 32), pe_row, ident[0:32, 0:32]).then_inc(pre_tr, 1)
            def three(dst, ah, al, bh, bl, start, stop, shared=False):
                mm(dst, ah, bh, start=start, stop=False, skip_group_check=shared)
                mm(dst, ah, bl, start=False, stop=False, skip_group_check=shared)
                return mm(dst, al, bh, start=False, stop=stop, skip_group_check=shared)

            def col(w, k, a, b):
                return w[:, k * W1ST + a:k * W1ST + b]

            def ada_total(g):
                pe.wait_ge(ada_acc, g + 1)
                if g >= 1:
                    pe.wait_ge(ss_set, g)
                for q in range(4):
                    s, e = q // 2, q % 2
                    ins = mm(bank(7, 320 + 4 * g + q, 1), acc[:, 256 * s + P * e:256 * s + P * (e + 1)],
                             ones[:, 0:1], start=g == 0, stop=True, skip_group_check=True)
                ins.then_inc(ada_red, 1)

            for k in range(KT):
                if k == 4:
                    ada_total(0)
                if k % 4 == 0:
                    pe.wait_ge(x_in[k // 4], 16)
                if k == 4:
                    pe.wait_ge(trow_ev, 1)
                    pe.wait_ge(pre_ev, 1)
                if k == KT - 1:
                    pe.wait_ge(ss_set, 1)
                for t in range(NT):
                    ins = nc.tensor.transpose(bank(x_bank(k), P * t, P),
                                              x_tok[k // 4][:, t, P * (k % 4):P * (k % 4 + 1)], ident[:, :])
                ins.then_inc(x_tr, 1)
            pe.wait_ge(xt_act, 4)
            for g in range(4):
                for k in (2 * g, 2 * g + 1):
                    pe.wait_ge(p1_hi, k + 1)
                    pe.wait_ge(p1_lo, k + 1)
                    pe.wait_ge(hhi_set, k + 1)
                    pe.wait_ge(hlo_pool if k % 2 else hlo_dve, g + 1)
                    last = k == KT - 1
                    for b in range(4):
                        three(bank(2 + b), col(w_hi, k, P * b, P * (b + 1)), col(w_lo, k, P * b, P * (b + 1)),
                              hiv[:, k, :], lov[:, k, :], k == 0, last)
                        if k % 2 and g < 3 and b == (3, 1, 1)[g]:
                            ada_total(g + 1)
                    if k == 0:
                        pe.wait_ge(xt_act, KT)
                    for t in range(NT):
                        if t == NT - 1:
                            pe.wait_ge(ss_set, min((k + 1) // 2 + 1, 4))
                        ins = three(bank(TOK_BANK[t], 0, 280), hiv[:, k, P * t:P * (t + 1)],
                                    lov[:, k, P * t:P * (t + 1)], col(w_hi, k, 4 * P, W1ST), col(w_lo, k, 4 * P, W1ST),
                                    k == 0, last, True)
                    ins.then_inc(p1_used, 1)

            def tile_range(t, lo, hi):
                c, e = t // 3, t % 3
                by_token = TILES[t][0] in "zv"
                part = TILES[t][2]
                groups = [(tt, k) for tt in range(2 * part, 2 * part + 2) for k in range(KT)] if by_token else \
                    [(0, k) for k in range(KT)]
                n = len(groups)
                for m, (tt, k) in enumerate(groups):
                    if not lo <= m / n < hi:
                        continue
                    if m == 0:
                        if t < 2:
                            pe.wait_ge(tok_ev, t + 1)
                        else:
                            pe.wait_ge(pj_dve, t - 1)
                    if e == 0 and k % 4 == 0:
                        pe.wait_ge(hi_set, 2 * c + k // 4 + 1)
                        pe.wait_ge(lo_set, 2 * c + k // 4 + 1)
                    if not by_token:
                        ins = three(bank(t % 2), chunk(w_hi, c, k, P * e, P * e + P),
                                    chunk(w_lo, c, k, P * e, P * e + P), hiv[:, k, :], lov[:, k, :],
                                    k == 0, k == KT - 1)
                    else:
                        ins = three(bank(t % 2, 256 * (tt % 2), 256), hiv[:, k, P * tt:P * (tt + 1)],
                                    lov[:, k, P * tt:P * (tt + 1)], chunk(w_hi, c, k, P, 3 * P),
                                    chunk(w_lo, c, k, P, 3 * P), k == 0, k == KT - 1)
                    if m == n - 1:
                        ins.then_inc(pj, 1)

            def project(s, j):
                a, b = quantum(s, j)
                for e in range(3):
                    lo, hi = a - e, b - e
                    if hi > 0 and lo < 1:
                        tile_range(3 * s + e, lo, hi)

            def compress1(v, part):
                src = raw_landed(pe, ("w1", v, part))
                if part == 0:
                    pe.wait_ge(bt_set, v + 1)
                    if v == 0:
                        pe.wait_ge(tok_ev, 4)
                k0, k1 = W1PARTS[part]
                for k in range(k0, k1):
                    for jj in range(2):
                        o = (k - k0) * CMP_HID + P * jj
                        ins = mm(bank(HID_BANK[v] + jj, 0, 62), src[:, o:o + P], bt[:, v, k, :], start=k == 0,
                                 stop=k == 15)
                ins.then_inc(w1_used, 1)

            def compress2(v):
                pe.wait_ge(hs_set, v + 1)
                if v == 0:
                    pe.wait_ge(w2_in, 16)
                    pe.wait_ge(kb_lo, 2)
                    for jj in range(2):
                        ins = mm(bank(CMP_BANK[0])[0:HD, 0:62], W2[:, 0, jj, :], HS[:, jj, :], start=jj == 0,
                                 stop=jj == 1)
                else:
                    for g in range(2):
                        for jj in range(2):
                            ins = mm(bank(CMP_BANK[1])[0:HD, HD * g:HD * (g + 1)],
                                     HSV[:, jj, g, :, :].rearrange("p r n -> p (r n)"), W2[:, 1, jj, :],
                                     start=jj == 0, stop=jj == 1)
                ins.then_inc(cmp2, 1)

            def scores(n):
                kind, c, h, br, i = UNITS[n]
                if n < 2:
                    pe.wait_ge(hs_set, 2)
                else:
                    pe.wait_ge(lg_set, n - 1)
                if n == UBASE[c]:
                    pe.wait_ge(pj_dve, TILE["q", c, 0] + 1)
                    if c < 4:
                        pe.wait_ge(cmp_set, 1)
                    pe.wait_ge(kdup[c // 2 if c < 4 else c % 2], 16 if c < 4 else 16 + 32 * (c // 2 - 1))
                b = S_BANK + n % 2
                if kind == "cmp":
                    for i in range(NT):
                        for h in range(2):
                            qt = QS[:, c % 2, h, P * i:P * (i + 1)]
                            ins = mm(bank(b, (2 * i + h) * 64, 64), qt, KC[:, :, c // 2, :], start=True, stop=True)
                else:
                    w = P * (i + 1)
                    qt = QS[:, c % 2, h, P * i:P * (i + 1)]
                    sl, a = (c // 2, br) if c < 4 else (c % 2, h)
                    mm(bank(b, 0, w), qt, K[:, sl, a, 0, 0:w], start=True, stop=False)
                    ins = mm(bank(b, 0, w), qt, K[:, sl, a, 1, 0:w], start=False, stop=True)
                ins.then_inc(qk_done, 1)

            def turn(n):
                kind, c, h, br, i = UNITS[n]
                if kind == "cmp":
                    pe.wait_ge(cn_set, c + 1)
                else:
                    pe.wait_ge(ex_set, n + 1)
                if n < 2:
                    pe.wait_ge(cmp_set, 2)
                else:
                    evacuated(pe, n - 2)
                src = lg[:, 512 * (n % 4):512 * (n % 4) + 512]
                b = T_BANK + n % 2
                if kind == "cmp":
                    for i in range(NT):
                        ins = nc.tensor.transpose(bank(b, P * i, P)[0:HD, :], src[:, HD * i:HD * (i + 1)], flip[:, :])
                else:
                    for m in range(i + 1):
                        ins = nc.tensor.transpose(bank(b, P * m, P), src[:, P * m:P * (m + 1)], flip[:, :])
                ins.then_inc(tr_done, 1)

            def values(n):
                kind, c, h, br, i = UNITS[n]
                evacuated(pe, n)
                gi = GROUP[n]
                if n == 0 or GROUP[n - 1] != gi:
                    pe.wait_ge(cmp_set, 2)
                    pe.wait_ge(tok_ev, 4)
                    if c >= 4:
                        pe.wait_ge(pj_dve, TILE["v", c // 2 - 2, 1] + 1)
                    if gi >= 2:
                        pe.wait_ge(og_set, gi - 1)
                    if spared["gate"]:
                        pe.wait_ge(g1_set, spared["gate"])
                    if spared["out"]:
                        pe.wait_ge(ot_lo, spared["out"])
                b = O_BANK + gi % 2
                src = pt[:, 512 * (n % N_PT):512 * (n % N_PT) + 512]
                if kind == "cmp":
                    for i in range(NT):
                        ins = mm(bank(b, P * i, P), src[0:HD, P * i:P * (i + 1)], vc[:, P * (c // 2):P * (c // 2 + 1)],
                                 start=True, stop=True)
                else:
                    for m in range(i + 1):
                        v = VB[:, m, br, c // 2, :] if c < 4 else VAv[c // 2 - 2][:, c % 2, m, h, :]
                        ins = mm(bank(b, 65 * i, 65), src[:, P * m:P * (m + 1)], v, start=m == 0, stop=m == i)
                ins.then_inc(pv_done, 1)

            def gate_total(half):
                pe.wait_ge(gate_used, KT + 1)
                mm(bank(gate_bank(half)), ones[:, :], gacc[:, 512 * half:512 * half + 512], start=True, stop=True)\
                    .then_inc(grow, 1)

            def turn_out(i):
                k = out_tile(OUT_PAIRS[i])
                pe.wait_ge(gated, i + 1)
                for t in range(NT):
                    ins = nc.tensor.transpose(bank(out_bank(i), P * t, P), OS[:, t, P * k:P * (k + 1)], ident[:, :])
                ins.then_inc(ot_tr, 1)

            def out_product(b, t, half, q, start, stop):
                pe.wait_ge(hi_set, 2 * PAIRS + q + 1)
                pe.wait_ge(lo_set, 2 * PAIRS + q + 1)
                k = WO[q]
                pair = k + 4 if k < 4 else k - 4
                pe.wait_ge(ot_lo, OUT_PAIRS.index(pair) + 1)
                f = slice(512 * half, 512 * half + 512)
                return three(bank(b), OTh[:, t, P * k:P * (k + 1)], OTl[:, t, P * k:P * (k + 1)],
                             wo_at(w_hi, q)[:, f], wo_at(w_lo, q)[:, f], start, stop)

            def early_product(m, q0, q1):
                if q0 == 0:
                    if m < 2:
                        pe.wait_ge(pj_dve, 23 + m)
                    else:
                        pe.wait_ge(ya_ev, m - 1)
                for q in range(q0, q1):
                    ins = out_product(m % 2, m // 2, m % 2, q, q == 0, q == N_EARLY - 1)
                if q1 == N_EARLY:
                    ins.then_inc(ya_done, 1)

            def late_product(t, q):
                if q == N_EARLY:
                    if t == 0:
                        pe.wait_ge(lg_set, NU)
                    elif t == 1:
                        pe.wait_ge(ya_ev, 2 * NT)
                    else:
                        evacuated(pe, NU - 1)
                        evacuated(pe, NU - 2)
                for half in range(2):
                    ins = out_product(LATE_BANK[t] + half, t, half, q, q == N_EARLY, q == KT - 1)
                if q == KT - 1:
                    ins.then_inc(y_done, 1)

            spared = {"gate": 0, "out": 0}
            pe.wait_ge(flip_set, 1)
            n = 0
            for s in range(PAIRS + 1):
                for j in range(iters(s)):
                    if s >= 1:
                        scores(n)
                    if s < PAIRS:
                        project(s, j)
                    if s == 0:
                        for v, part in (((0, 0),), ((0, 1),), ((0, 2),), ((1, 0),), ((1, 1), (1, 2)), ())[j]:
                            compress1(v, part)
                        if j == 3:
                            compress2(0)
                        if j == 5:
                            compress2(1)
                    else:
                        if n >= LAG_T:
                            turn(n - LAG_T)
                        if n >= LAG_V:
                            values(n - LAG_V)
                        if (s, j) in SPARE:
                            kind, i = SPARE[s, j]
                            pe.wait_ge(og_set, GROUP[n - LAG_V])
                            if kind == "gate":
                                gate_total(i)
                            else:
                                turn_out(i)
                            spared[kind] += 1
                        n += 1
                    if s == PAIRS:
                        if j == 0:
                            early_product(0, 0, 3)
                            early_product(1, 0, 3)
                        elif j == 1:
                            for q in range(3, N_EARLY):
                                early_product(0, q, q + 1)
                                early_product(1, q, q + 1)
                        else:
                            early_product(j, 0, N_EARLY)
            for n in range(NU, NU + LAG_V):
                if n - LAG_T < NU:
                    turn(n - LAG_T)
                values(n - LAG_V)
                if n - NU < 4:
                    late_product((n - NU) // 2, N_EARLY + (n - NU) % 2)
            for q in range(N_EARLY, KT - 1):
                late_product(2, q)
            pe.wait_ge(og_set, GROUP[NU - 1] + 1)
            turn_out(PAIRS - 1)
            free = 1 - (out_bank(PAIRS - 1) - O_BANK)
            for q in range(N_EARLY, KT - 1):
                out_product(O_BANK + free, NT - 1, free, q, q == N_EARLY, False)
            for t in range(NT - 1):
                late_product(t, KT - 1)
            pe.wait_ge(ot_lo, PAIRS)
            for q in range(N_EARLY, KT - 1):
                out_product(O_BANK + 1 - free, NT - 1, 1 - free, q, q == N_EARLY, False)
            late_product(NT - 1, KT - 1)


def blocks(ap):
    return ap.rearrange("p (i t) -> p i t", t=P)


def shape_constants():
    k = np.arange(TROW)
    d = SEQ - 1 - k
    dm = np.maximum(d, 1)
    exact = N_B // 2
    large = exact + (np.log(dm.astype(np.float32) / np.float32(exact)) / np.log(MAX_DIST / exact)
                     * (N_B - exact)).astype(np.int32)
    bucket = np.where(d < exact, np.maximum(d, 0), np.minimum(large, N_B - 1))
    t = np.zeros((N_B + 2, TROW + 16), np.float32)
    t[bucket, k] = -1.0
    seen = sum(((d >= 0) & (d <= w) & (d % dil == 0)).astype(np.int64) for w, dil in DILATED)
    t[N_B, :TROW] = np.where(seen > 0, -np.log(np.maximum(seen, 1)), BIG)
    t[N_B + 1, :TROW] = np.where(d >= 0, 0.0, BIG)
    t[N_B, TROW:TROW + H_A] = 1.0
    t[N_B + 1, TROW + H_A:] = 1.0
    return t


def kernel(**inputs):
    import concourse.bacc as bacc
    from concourse.bass_utils import run_bass_kernel_spmd

    nc = bacc.Bacc("TRN2", target_bir_lowering=False, num_devices=1)
    arrays, aps = {}, {}
    for name in ("x", "c", "w_in", "w_out", "cmp_pe", "cmp_w1", "cmp_w2", "w_ada", "b_ada", "ln_g", "ln_b", "rel_bias"):
        a = np.ascontiguousarray(inputs[name])
        if name in ("w_in", "w_out", "cmp_pe", "cmp_w1", "cmp_w2", "w_ada"):
            a = a[0]
        arrays["in_" + name] = a
        aps[name] = nc.dram_tensor("in_" + name, a.shape, F32, kind="ExternalInput").ap()
    arrays["in_consts"] = shape_constants()
    consts = nc.dram_tensor("in_consts", arrays["in_consts"].shape, F32, kind="ExternalInput").ap()
    scratch = nc.dram_tensor("bias_rows", (16, TROW), F32, kind="Internal").ap()
    out = nc.dram_tensor("out", (1, SEQ, D), F32, kind="ExternalOutput").ap()
    build(nc, aps["x"], aps["c"], aps["w_in"], aps["w_out"], aps["cmp_pe"], aps["cmp_w1"], aps["cmp_w2"],
          aps["w_ada"], aps["b_ada"], aps["ln_g"], aps["ln_b"], aps["rel_bias"], consts, scratch, out)
    r = run_bass_kernel_spmd(nc, [arrays], core_ids=[0])
    return r.results[0]["out"]
```
